# Optimizing a Trainium2 kernel written in Bass

```python
import math
import jax
import jax.numpy as jnp
from jax import lax
import numpy as np

D_MODEL = 1024
BATCH = 1
SEQ = 1024
DEPTH = 1

D_MIX = D_MODEL
GLA_WIDTH = D_MIX // 2
GLA_HEADS = 4
GLA_DV = GLA_WIDTH // GLA_HEADS
GLA_DK = GLA_DV // 2
GLA_GATE_RANK = 16
GLA_TAU = 16.0
GLA_CHUNK = 16
DIFF_WIDTH = D_MIX - GLA_WIDTH
DIFF_HEADS = 4
DIFF_DV = DIFF_WIDTH // DIFF_HEADS
DIFF_DK = DIFF_DV // 2
Q_BLOCK = 128
REL_BUCKETS = 32
REL_MAX_DIST = 128
N_GROUPS = 4
EXPERTS_PER_GROUP = 8
N_EXPERTS = N_GROUPS * EXPERTS_PER_GROUP
TOP_K = 2
D_EXPERT = 512
ROW_BLOCK = 128
EPS = 1e-6

GLA_QK = GLA_HEADS * GLA_DK
GLA_V = GLA_HEADS * GLA_DV
DIFF_QK = DIFF_HEADS * 2 * DIFF_DK
DIFF_V = DIFF_HEADS * DIFF_DV
SPLIT_SIZES = (GLA_QK, GLA_QK, GLA_V, GLA_V, GLA_GATE_RANK, DIFF_QK, DIFF_QK, DIFF_V)
IN_COLS = 2 * GLA_QK + 2 * GLA_V + GLA_GATE_RANK + 2 * DIFF_QK + DIFF_V

kernel_name = 'hybrid_gla_diffattn_hiermoe'

def _split_offsets():
    offs, acc = [], 0
    for s in SPLIT_SIZES[:-1]:
        acc += s
        offs.append(acc)
    return offs

def rms_norm(x, g):
    xf = x.astype(jnp.float32)
    y = xf * lax.rsqrt(jnp.mean(xf * xf, axis=-1, keepdims=True) + EPS)
    return (y * g.astype(jnp.float32)).astype(x.dtype)

def rel_bucket(dist):
    n = jnp.maximum(dist, 0)
    max_exact = REL_BUCKETS // 2
    large = max_exact + (jnp.log(jnp.maximum(n, max_exact).astype(jnp.float32) / max_exact)
                         / math.log(REL_MAX_DIST / max_exact) * (REL_BUCKETS - max_exact)).astype(jnp.int32)
    large = jnp.minimum(large, REL_BUCKETS - 1)
    return jnp.where(n < max_exact, n, large)

def gla_mixer(q, k, v, r, gate_lr, wa2, ba, onorm_g):
    bsz, seq, _ = q.shape
    n_chunks = seq // GLA_CHUNK
    f32 = jnp.float32

    def heads(t, d):
        return t.astype(f32).reshape(bsz, n_chunks, GLA_CHUNK, GLA_HEADS, d).transpose(0, 3, 1, 2, 4)

    log_a = jax.nn.log_sigmoid((gate_lr @ wa2 + ba).astype(f32)) / GLA_TAU
    qh = heads(q, GLA_DK) * (GLA_DK ** -0.5)
    kh = heads(k, GLA_DK)
    vh = heads(v, GLA_DV)
    b = jnp.cumsum(heads(log_a, GLA_DK), axis=3)
    causal = jnp.tril(jnp.ones((GLA_CHUNK, GLA_CHUNK), dtype=bool))
    diff = b[:, :, :, :, None, :] - b[:, :, :, None, :, :]
    decay = jnp.exp(jnp.where(causal[:, :, None], diff, -jnp.inf))
    attn = jnp.einsum('bhntk,bhnsk,bhntsk->bhnts', qh, kh, decay)
    o_intra = jnp.einsum('bhnts,bhnsv->bhntv', attn, vh)
    g_last = b[:, :, :, -1, :]
    k_dec = kh * jnp.exp(g_last[:, :, :, None, :] - b)
    d_state = jnp.einsum('bhnsk,bhnsv->nbhkv', k_dec, vh)

    def step(state, inp):
        g_n, ds_n = inp
        return jnp.exp(g_n)[..., None] * state + ds_n, state

    s0 = jnp.zeros((bsz, GLA_HEADS, GLA_DK, GLA_DV), f32)
    _, s_prev = lax.scan(step, s0, (g_last.transpose(2, 0, 1, 3), d_state))
    o_inter = jnp.einsum('bhntk,nbhkv->bhntv', qh * jnp.exp(b), s_prev)
    o = (o_intra + o_inter).transpose(0, 2, 3, 1, 4).reshape(bsz, seq, GLA_HEADS, GLA_DV)
    o = rms_norm(o, onorm_g).reshape(bsz, seq, GLA_V) * jax.nn.silu(r.astype(f32))
    return o.astype(q.dtype)

def diff_attention(q, k, v, qn_g, kn_g, lq1, lk1, lq2, lk2, subln_g, rel_bias, lambda_init):
    bsz, seq, _ = q.shape
    f32 = jnp.float32
    qh = rms_norm(q.reshape(bsz, seq, DIFF_HEADS, 2, DIFF_DK), qn_g) * (DIFF_DK ** -0.5)
    kh = rms_norm(k.reshape(bsz, seq, DIFF_HEADS, 2, DIFF_DK), kn_g)
    qh = qh.transpose(0, 2, 3, 1, 4)
    kh = kh.transpose(0, 2, 3, 1, 4)
    vh = v.reshape(bsz, seq, DIFF_HEADS, DIFF_DV).transpose(0, 2, 1, 3)
    lam = (jnp.exp(jnp.sum(lq1.astype(f32) * lk1.astype(f32)))
           - jnp.exp(jnp.sum(lq2.astype(f32) * lk2.astype(f32))) + lambda_init)
    n_blocks = seq // Q_BLOCK
    q_blocks = qh.reshape(bsz, DIFF_HEADS, 2, n_blocks, Q_BLOCK, DIFF_DK).transpose(3, 0, 1, 2, 4, 5)
    kpos = jnp.arange(seq)

    def block(args):
        qb, blk = args
        qpos = blk * Q_BLOCK + jnp.arange(Q_BLOCK)
        rel = qpos[:, None] - kpos[None, :]
        bias = rel_bias[rel_bucket(rel)].transpose(2, 0, 1).astype(f32)
        logits = jnp.einsum('bhcqd,bhckd->bhcqk', qb, kh).astype(f32) + bias[None, :, None]
        logits = jnp.where((rel >= 0)[None, None, None], logits, -jnp.inf)
        p = jax.nn.softmax(logits, axis=-1)
        w = p[:, :, 0] - lam * p[:, :, 1]
        return jnp.einsum('bhqk,bhkv->bhqv', w.astype(vh.dtype), vh)

    out = lax.map(block, (q_blocks, jnp.arange(n_blocks)))
    out = out.transpose(1, 0, 3, 2, 4).reshape(bsz, seq, DIFF_HEADS, DIFF_DV)
    out = rms_norm(out, subln_g) * (1.0 - lambda_init)
    return out.reshape(bsz, seq, DIFF_V).astype(q.dtype)

def hier_moe(x, wg, bg, we, be, w1, w3, w2):
    bsz, seq, d = x.shape
    n_tok = bsz * seq
    f32 = jnp.float32
    xt = x.reshape(n_tok, d)
    g_prob = jax.nn.softmax((xt @ wg + bg).astype(f32), axis=-1)
    g_w, g_idx = lax.top_k(g_prob, 1)
    e_logits = (xt @ we + be).astype(f32).reshape(n_tok, N_GROUPS, EXPERTS_PER_GROUP)
    e_sel = jnp.take_along_axis(e_logits, g_idx[:, :, None], axis=1)[:, 0]
    e_w, e_idx = lax.top_k(jax.nn.softmax(e_sel, axis=-1), TOP_K)
    e_w = e_w / jnp.sum(e_w, axis=-1, keepdims=True)
    weights = g_w * e_w
    expert = g_idx * EXPERTS_PER_GROUP + e_idx
    m = n_tok * TOP_K
    flat_e = expert.reshape(m)
    flat_t = jnp.arange(m, dtype=jnp.int32) // TOP_K
    flat_w = weights.reshape(m)
    order = jnp.argsort(flat_e)
    sorted_e = flat_e[order]
    counts = jnp.bincount(flat_e, length=N_EXPERTS)
    padded = (counts + ROW_BLOCK - 1) // ROW_BLOCK * ROW_BLOCK
    pad_end = jnp.cumsum(padded)
    pad_start = pad_end - padded
    start = jnp.cumsum(counts) - counts
    dest = pad_start[sorted_e] + jnp.arange(m) - start[sorted_e]
    n_blocks = -(-m // ROW_BLOCK) + N_EXPERTS
    n_rows = n_blocks * ROW_BLOCK
    row_tok = jnp.full((n_rows,), n_tok, dtype=jnp.int32).at[dest].set(flat_t[order])
    row_w = jnp.zeros((n_rows,), f32).at[dest].set(flat_w[order])
    block_expert = jnp.minimum(
        jnp.searchsorted(pad_end, jnp.arange(n_blocks) * ROW_BLOCK, side='right'), N_EXPERTS - 1)
    x_rows = jnp.concatenate([xt, jnp.zeros((1, d), xt.dtype)], axis=0)[row_tok]
    x_rows = x_rows.reshape(n_blocks, ROW_BLOCK, d)

    def expert_block(args):
        xb, e = args
        hdn = jax.nn.silu(xb @ w1[e]) * (xb @ w3[e])
        return hdn @ w2[e]

    y = lax.map(expert_block, (x_rows, block_expert)).reshape(n_rows, d)
    out = jnp.zeros((n_tok + 1, d), f32).at[row_tok].add(y.astype(f32) * row_w[:, None])[:n_tok]
    return out.astype(x.dtype).reshape(bsz, seq, d)

def setup_inputs(seed: int = 0) -> dict:
    key = jax.random.key(seed)
    ks = jax.random.split(key, 24)
    f32 = jnp.float32

    def nrm(k, shape, scale):
        return jax.random.normal(k, shape, f32) * scale

    def gain(k, shape):
        return 1.0 + nrm(k, shape, 0.02)

    L = DEPTH
    return {
        'x': nrm(ks[0], (BATCH, SEQ, D_MODEL), 1.0),
        'rel_bias': nrm(ks[1], (REL_BUCKETS, DIFF_HEADS), 0.2),
        'norm1_g': gain(ks[2], (L, D_MODEL)),
        'w_in': nrm(ks[3], (L, D_MODEL, IN_COLS), D_MODEL ** -0.5),
        'gla_wa2': nrm(ks[4], (L, GLA_GATE_RANK, GLA_QK), GLA_GATE_RANK ** -0.5),
        'gla_ba': nrm(ks[5], (L, GLA_QK), 0.01),
        'gla_onorm_g': gain(ks[6], (L, GLA_DV)),
        'diff_qnorm_g': gain(ks[7], (L, DIFF_DK)),
        'diff_knorm_g': gain(ks[8], (L, DIFF_DK)),
        'diff_lq1': nrm(ks[9], (L, DIFF_DK), 0.1),
        'diff_lk1': nrm(ks[10], (L, DIFF_DK), 0.1),
        'diff_lq2': nrm(ks[11], (L, DIFF_DK), 0.1),
        'diff_lk2': nrm(ks[12], (L, DIFF_DK), 0.1),
        'diff_subln_g': gain(ks[13], (L, DIFF_DV)),
        'w_out': nrm(ks[14], (L, D_MIX, D_MODEL), D_MIX ** -0.5),
        'norm2_g': gain(ks[15], (L, D_MODEL)),
        'moe_wg': nrm(ks[16], (L, D_MODEL, N_GROUPS), D_MODEL ** -0.5),
        'moe_bg': nrm(ks[17], (L, N_GROUPS), 0.01),
        'moe_we': nrm(ks[18], (L, D_MODEL, N_EXPERTS), D_MODEL ** -0.5),
        'moe_be': nrm(ks[19], (L, N_EXPERTS), 0.01),
        'moe_w1': nrm(ks[20], (L, N_EXPERTS, D_MODEL, D_EXPERT), D_MODEL ** -0.5),
        'moe_w3': nrm(ks[21], (L, N_EXPERTS, D_MODEL, D_EXPERT), D_MODEL ** -0.5),
        'moe_w2': nrm(ks[22], (L, N_EXPERTS, D_EXPERT, D_MODEL), D_EXPERT ** -0.5),
    }

def reference(x, rel_bias, norm1_g, w_in, gla_wa2, gla_ba, gla_onorm_g, diff_qnorm_g, diff_knorm_g,
              diff_lq1, diff_lk1, diff_lq2, diff_lk2, diff_subln_g, w_out, norm2_g,
              moe_wg, moe_bg, moe_we, moe_be, moe_w1, moe_w3, moe_w2):
    h = x
    offsets = _split_offsets()
    for l in range(DEPTH):
        xn = rms_norm(h, norm1_g[l])
        proj = xn @ w_in[l]
        gq, gk, gv, gr, glr, dq, dk, dv = jnp.split(proj, offsets, axis=-1)
        o_gla = gla_mixer(gq, gk, gv, gr, glr, gla_wa2[l], gla_ba[l], gla_onorm_g[l])
        lambda_init = 0.8 - 0.6 * math.exp(-0.3 * l)
        o_diff = diff_attention(dq, dk, dv, diff_qnorm_g[l], diff_knorm_g[l], diff_lq1[l], diff_lk1[l],
                                diff_lq2[l], diff_lk2[l], diff_subln_g[l], rel_bias, lambda_init)
        h = h + jnp.concatenate([o_gla, o_diff], axis=-1) @ w_out[l]
        h = h + hier_moe(rms_norm(h, norm2_g[l]), moe_wg[l], moe_bg[l], moe_we[l], moe_be[l],
                         moe_w1[l], moe_w3[l], moe_w2[l])
    return h


_drawn_inputs = setup_inputs


def setup_inputs(seed=0):
    import zlib

    import numpy as np

    out = dict(_drawn_inputs(seed))
    spreads = {}
    factors = {'gla_ba': 8.0,
     'gla_onorm_g': 10.887,
     'diff_knorm_g': 2.703,
     'diff_lq1': 3.679,
     'diff_lk1': 5.705,
     'diff_subln_g': 8.842,
     'moe_bg': 21.143,
     'moe_be': 13.865,
     'diff_lk2': 5.018,
     'norm2_g': 4.009}
    for name, (base, spread) in spreads.items():
        noise = np.random.default_rng([zlib.crc32(name.encode()), seed]).standard_normal(out[name].shape)
        drawn = base * np.exp(spread * noise) if base else spread * noise
        out[name] = jnp.asarray(drawn.astype(out[name].dtype))
    for name, factor in factors.items():
        out[name] = (out[name] * factor).astype(out[name].dtype)
    return out
```

```python
import math
from contextlib import ExitStack

import numpy as np
import concourse.bass as bass
from concourse import mybir

F32 = mybir.dt.float32
F32R = mybir.dt.float32r
BF16 = mybir.dt.bfloat16
U32 = mybir.dt.uint32
I32 = mybir.dt.int32
ALU = mybir.AluOpType
ACT = mybir.ActivationFunctionType
AX = mybir.AxisListType

P = 128
SEQ = 1024
D = 1024
T = SEQ // P
KD = D // P
HG = 4
GDK, GDV = 64, 128
HD = 4
DDK, DDV = 64, 128
GR = 16
TAU = 16.0
EPS = 1e-6
LAMBDA_INIT = 0.8 - 0.6 * math.exp(-0.3 * 0)
NG, EPG = 4, 8
NE = NG * EPG
DE = 512
KE = DE // P
NEG = -1e30
BUCKETS, MAX_DIST = 32, 128
CAP = P
REL = 3 * P
CW = 256
NROUTE = 8

GQ, GK, GV, GRC, GLR, DQ, DK, DV = 0, 256, 512, 1024, 1536, 1552, 2064, 2576


def buckets():
    rel = (REL - P) - np.arange(REL)
    n = np.maximum(rel, 0)
    exact = BUCKETS // 2
    large = exact + (np.log(np.maximum(n, exact).astype(np.float32) / np.float32(exact))
                     / np.float32(math.log(MAX_DIST / exact)) * np.float32(BUCKETS - exact)).astype(np.int32)
    b = np.where(n < exact, n, np.minimum(large, BUCKETS - 1))
    return (b[None, :] == np.arange(BUCKETS)[:, None]).astype(np.float32)


MAP = {"dqT": 20, "dkT": 36, "dv": 52, "gv": 68, "gqT": 84, "gkT": 92, "glr": 100, "xh": 101, "xl": 133,
       "rg": 101, "h": 191.75,
       "slot_rows": 187, "place": 186, "iota_slot": 185.5, "counts": 185.25}
LOCAL = {"constants": 101, "norm1": 165, "project": 165, "gated": 117, "diff": 117, "router": 20}
END = 223.9


def mem(nc, c, stage):
    at = [LOCAL.get(stage, 20) * 1024]

    def sb(name, shape, dt=F32, kib=None):
        size = math.prod(shape[1:]) * mybir.dt.size(dt)
        size = -(-size // 32) * 32
        if kib is None:
            kib = at[0] / 1024
            at[0] += size
        assert kib * 1024 + size <= END * 1024, (name, kib, size)
        return nc.alloc_sbuf_tensor_at(f"{stage}_{name}", shape, dt, offset=int(kib * 1024))

    def ps(name, shape, dt=F32):
        return c.enter_context(nc.psum_tensor(f"{stage}_{name}", shape, dt))

    sems = []

    def sem(name):
        sems.append(nc.alloc_semaphore(f"{stage}_{name}"))
        return sems[-1]

    def clear():
        nc.clear_and_free_semaphores(sems)
        nc.all_engine_barrier()
    c.callback(clear)
    return sb, ps, sem


def build(nc, a):
    with ExitStack() as top:
        def keep(name, shape, dt=F32):
            return top.enter_context(nc.sbuf_tensor(name, shape, dt))

        def dram(name, shape, dt=F32):
            return nc.dram_tensor(name, shape, dt, kind="Internal").ap()

        def place(name, shape, dt=F32):
            return nc.alloc_sbuf_tensor_at(name, shape, dt, offset=int(MAP[name] * 1024))

        s = {
            "rel_dram": dram("rel_dram", [HD, REL]), "xn2_dram": dram("xn2_dram", [SEQ, D]),
            "r_dram": dram("r_dram", [P, T, HG * GDV]), "y_dram": dram("y_dram", [2 * SEQ, D]),
            "ident": keep("ident", [P, P]), "causal": keep("causal", [P, HG, 64]),
            "gain_q": keep("gain_q", [P, 1]), "gain_k": keep("gain_k", [P, 1]), "lam": keep("lam", [P, 1]),
            "minus_half": keep("minus_half", [P, 8]),
            "logits": keep("logits", [P, T, NG + NE]),
            "dqT": place("dqT", [P, HD, SEQ]), "dkT": place("dkT", [P, HD, SEQ]),
            "dv": place("dv", [P, T, HD * DDV]), "gv": place("gv", [P, T, HG * GDV]),
            "gqT": place("gqT", [P, 2, SEQ]), "gkT": place("gkT", [P, 2, SEQ]),
            "glr": place("glr", [P, T, GR]), "xh": place("xh", [P, KD, SEQ], F32R),
            "xl": place("xl", [P, KD, SEQ], F32R), "rg": place("rg", [P, T, HG * GDV]),
            "h": place("h", [P, T, D]),
            "slot_rows": place("slot_rows", [P, T, NE, NROUTE], BF16),
            "place": place("place", [P, NE, T]), "iota_slot": place("iota_slot", [P, CAP]),
            "counts": place("counts", [1, NE + 1], I32),
        }
        s["od"] = s["gv"]
        stages = [stage_constants, stage_norm1, stage_project, stage_gla, stage_diffattn, stage_outproj,
                  stage_route, stage_experts, stage_combine]
        for stage in stages:
            stage(nc, a, s)


def stage_constants(nc, a, s):
    with ExitStack() as c:
        sb, ps, sem = mem(nc, c, "constants")
        onehot = sb("onehot", [BUCKETS, REL])
        relb = sb("relb", [BUCKETS, HD])
        relf = sb("relf", [HD, REL])
        lvec = sb("lvec", [P, 4, DDK])
        lprod = sb("lprod", [P, 2, DDK])
        lsum = sb("lsum", [P, 2])
        lexp = sb("lexp", [P, 2])
        graw = sb("graw", [P, 2])
        pf = ps("pf", [HD, 512])
        ident, causal = s["ident"], s["causal"]
        relb_in = sem("relb_in")
        onehot_in = sem("onehot_in")
        lvec_in = [sem(f"lvec_in{i}") for i in range(4)]
        gain_in = [sem(f"gain_in{i}") for i in range(4)]
        rel_out = sem("rel_out")
        filled = sem("filled")
        relf_mm = sem("relf_mm")
        step = sem("step")
        lam_step = sem("lam_step")
        lam_exp = sem("lam_exp")
        masked = sem("masked")
        block = c.enter_context(nc.Block())

        @block.sync
        def _(sp):
            sp.dma_start(relb[:], a["rel_bias"]).then_inc(relb_in, 16)
            sp.dma_start(onehot[:], a["bucket_onehot"]).then_inc(onehot_in, 16)
            for i, n in enumerate(("diff_lq1", "diff_lk1", "diff_lq2", "diff_lk2")):
                sp.dma_start(lvec[:, i, :], a[n].to_broadcast([P, DDK])).then_inc(lvec_in[i], 16)
            for i, n in enumerate(("diff_qnorm_g", "diff_knorm_g")):
                for half in range(2):
                    sp.dma_start(graw[half * 64:half * 64 + 64, i:i + 1],
                                 a[n].rearrange("a k -> k a")).then_inc(gain_in[2 * i + half], 16)
            sp.wait_ge(masked, 1)
            sp.dma_start(s["rel_dram"], relf[:]).then_inc(rel_out, 16)
            sp.wait_ge(rel_out, 16)

        @block.gpsimd
        def _(pool):
            nc.gpsimd.memset(ident[:], 0.0).then_inc(filled, 1)
            nc.gpsimd.memset(causal[:], 1.0).then_inc(filled, 1)
            nc.gpsimd.memset(s["minus_half"][:], -0.5)
            pool.wait_ge(filled, 2)
            nc.gpsimd.affine_select(out=ident[:], in_=ident[:], compare_op=ALU.not_equal, fill=1.0, base=0,
                                    pattern=[[-1, P]], channel_multiplier=1).then_inc(filled, 1)
            for half in range(2):
                v = causal[64 * half:64 * half + 64]
                pool.wait_ge(filled, 3 + half)
                nc.gpsimd.affine_select(out=v, in_=v, compare_op=ALU.is_ge, fill=0.0, base=0,
                                        pattern=[[0, HG], [1, 64]],
                                        channel_multiplier=-1).then_inc(filled, 1)

        @block.tensor
        def _(pe):
            pe.wait_ge(relb_in, 16)
            pe.wait_ge(onehot_in, 16)
            nc.tensor.matmul(pf[:, 0:REL], relb[:], onehot[:], start=True, stop=True).then_inc(relf_mm, 1)

        @block.vector
        def _(dve):
            dve.wait_ge(relf_mm, 1)
            nc.vector.tensor_copy(relf[:], pf[:, 0:REL]).then_inc(step, 1)
            dve.wait_ge(step, 1)
            nc.vector.tensor_scalar(relf[:, 1:REL], relf[:, 1:REL], relf[:, 0:1], None,
                                    ALU.subtract).then_inc(step, 1)
            dve.wait_ge(step, 2)
            nc.vector.memset(relf[:, 0:1], 0.0)
            nc.vector.memset(relf[:, REL - P + 1:REL], NEG).then_inc(masked, 1)
            for i in range(4):
                dve.wait_ge(lvec_in[i], 16)
            for i in range(2):
                nc.vector.tensor_tensor(lprod[:, i, :], lvec[:, 2 * i, :], lvec[:, 2 * i + 1, :],
                                        ALU.mult).then_inc(lam_step, 1)
            dve.wait_ge(lam_step, 2)
            nc.vector.tensor_reduce(lsum[:], lprod[:], AX.X, ALU.add).then_inc(lam_step, 1)
            dve.wait_ge(lam_exp, 1)
            nc.vector.tensor_tensor(lexp[:, 0:1], lexp[:, 0:1], lexp[:, 1:2], ALU.subtract).then_inc(lam_step, 1)
            dve.wait_ge(lam_step, 4)
            nc.vector.tensor_scalar(s["lam"][:], lexp[:, 0:1], LAMBDA_INIT, None, ALU.add)
            for i in range(4):
                dve.wait_ge(gain_in[i], 16)
            nc.vector.tensor_scalar(s["gain_q"][:], graw[:, 0:1], DDK ** -0.5 * DDK ** 0.5, None, ALU.mult)
            nc.vector.tensor_scalar(s["gain_k"][:], graw[:, 1:2], DDK ** 0.5, None, ALU.mult)

        @block.scalar
        def _(act):
            act.wait_ge(lam_step, 3)
            nc.scalar.activation(lexp[:], lsum[:], ACT.Exp).then_inc(lam_exp, 1)


def stage_norm1(nc, a, s):
    with ExitStack() as c:
        sb, ps, sem = mem(nc, c, "norm1")
        g1 = sb("g1", [P, D])
        x = sb("x", [P, 2, D])
        sq = sb("sq", [P, D])
        xs = sb("xs", [P, 2, D])
        ss = sb("ss", [P, T])
        rs = sb("rs", [P, T])
        pt = [ps(f"pt{i}", [P, 4, P]) for i in range(4)]
        xh, xl, ident = s["xh"], s["xl"], s["ident"]
        g1_in = sem("g1_in")
        x_in = [sem("x_in0"), sem("x_in1")]
        squared = sem("squared")
        gain_ready = sem("gain_ready")
        shifted = sem("shifted")
        rstd_ready = sem("rstd_ready")
        scaled = sem("scaled")
        transposed = sem("transposed")
        high_ready = sem("high_ready")
        low_ready = sem("low_ready")
        block = c.enter_context(nc.Block())
        x_rows = a["x"].rearrange("b (t p) d -> (b t) p d", p=P)

        @block.sync
        def _(sp):
            sp.dma_start(x[:, 0, :], x_rows[0]).then_inc(x_in[0], 16)
            sp.dma_start(g1[:], a["norm1_g"].to_broadcast([P, D])).then_inc(g1_in, 16)
            sp.dma_start(x[:, 1, :], x_rows[1]).then_inc(x_in[1], 16)
            for t in range(2, T):
                sp.wait_ge(scaled, t - 1)
                sp.dma_start(x[:, t % 2, :], x_rows[t]).then_inc(x_in[t % 2], 16)

        @block.scalar
        def _(act):
            def high(t):
                for j in range(2):
                    act.wait_ge(transposed, 2 * t + j + 1)
                    nc.scalar.copy(xh[:, 4 * j:4 * j + 4, t * P:(t + 1) * P],
                                   pt[(2 * t + j) % 4][:]).then_inc(high_ready, 1)
            for t in range(T):
                act.wait_ge(x_in[t % 2], 16 * (t // 2 + 1))
                if t >= 1:
                    act.wait_ge(squared, t)
                nc.scalar.activation(sq[:], x[:, t % 2, :], ACT.Square,
                                     accum_out=ss[:, t:t + 1]).then_inc(squared, 1)
                if t >= 1:
                    high(t - 1)
            high(T - 1)

        @block.vector
        def _(dve):
            def low(t):
                for j in range(2):
                    n = 2 * t + j
                    dve.wait_ge(high_ready, n + 1)
                    hi = xh[:, 4 * j:4 * j + 4, t * P:(t + 1) * P]
                    nc.vector.tensor_tensor(xl[:, 4 * j:4 * j + 4, t * P:(t + 1) * P], pt[n % 4][:],
                                            hi.bitcast(F32), ALU.subtract).then_inc(low_ready, 1)
            dve.wait_ge(g1_in, 16)
            nc.vector.tensor_scalar(g1[:], g1[:], D ** 0.5, None, ALU.mult).then_inc(gain_ready, 1)
            dve.wait_ge(gain_ready, 1)
            for t in range(T):
                dve.wait_ge(rstd_ready, t + 1)
                if t >= 2:
                    dve.wait_ge(transposed, 2 * (t - 1))
                nc.vector.scalar_tensor_tensor(out=xs[:, t % 2, :], in0=x[:, t % 2, :], scalar=rs[:, t:t + 1],
                                               in1=g1[:], op0=ALU.mult, op1=ALU.mult).then_inc(scaled, 1)
                if t >= 1:
                    low(t - 1)
            low(T - 1)

        @block.gpsimd
        def _(pool):
            for t in range(T):
                pool.wait_ge(squared, t + 1)
                nc.gpsimd.tensor_scalar(rs[:, t:t + 1], ss[:, t:t + 1], EPS * D, None,
                                        ALU.add).then_inc(shifted, 1)
                pool.wait_ge(shifted, t + 1)
                nc.gpsimd.tensor_tensor(rs[:, t:t + 1], rs[:, t:t + 1], s["minus_half"][:, 0:1],
                                        ALU.pow).then_inc(rstd_ready, 1)

        @block.tensor
        def _(pe):
            for t in range(T):
                pe.wait_ge(scaled, t + 1)
                for j in range(2):
                    n = 2 * t + j
                    if n >= 4:
                        pe.wait_ge(low_ready, n - 3)
                    for k in range(4):
                        last = nc.tensor.transpose(pt[n % 4][:, k, :],
                                                   xs[:, t % 2, (4 * j + k) * P:(4 * j + k + 1) * P], ident[:])
                    last.then_inc(transposed, 1)


CHUNKS = [(DQ, CW), (DQ + CW, CW), (DK, CW), (DK + CW, CW), (GV, CW), (GV + CW, CW), (DV, CW),
          (DV + CW, CW), (GRC, CW), (GRC + CW, CW + GR), (GQ, CW), (GK, CW)]
NORMED = 4
SILU = 8
CHANNEL = 10


def stage_project(nc, a, s):
    with ExitStack() as c:
        sb, ps, sem = mem(nc, c, "project")
        W = CW + GR
        raw = [sb(f"w_raw{i}", [P, KD, W]) for i in range(2)]
        wh = [sb(f"w_high{i}", [P, KD, W], F32R) for i in range(2)]
        wl = [sb(f"w_low{i}", [P, KD, W], F32R) for i in range(2)]
        sq = sb("sq", [P, 2, 4, DDK])
        ss = sb("ss", [P, 2, 4])
        rs = sb("rs", [P, 2, 4])
        qn = sb("qn", [P, 2, 4 * DDK])
        rst = sb("rst", [P, 2, CW])
        pm = [ps(f"pm{i}", [P, 512]) for i in range(4)]
        pt = [ps(f"pt{i}", [P, 2, P]) for i in range(2)]
        xh, xl, ident = s["xh"], s["xl"], s["ident"]
        raw_in = [sem("raw_in0"), sem("raw_in1")]
        high_ready = sem("high_ready")
        low_ready = sem("low_ready")
        tile_ready = sem("tile_ready")
        bank_free_dve = sem("bank_free_dve")
        bank_free_act = sem("bank_free_act")
        squared = sem("squared")
        summed = sem("summed")
        shifted = sem("shifted")
        rstd_ready = sem("rstd_ready")
        normed = sem("normed")
        transposed = sem("transposed")
        stored = sem("stored")
        gated = sem("gated")
        r_out = [sem("r_out0"), sem("r_out1")]
        block = c.enter_context(nc.Block())
        BANKS = 4

        @block.sync
        def _(sp):
            for i, (col, w) in enumerate(CHUNKS):
                if i >= 2:
                    sp.wait_ge(low_ready, i - 1)
                sp.dma_start(raw[i % 2][:, :, 0:w], a["w_in"][0, :, col:col + w].rearrange(
                    "(k p) c -> p k c", p=P)).then_inc(raw_in[i % 2], 16)

        @block.tensor
        def _(pe):
            def products(t, slot, out, w):
                for k in range(KD):
                    hi, lo = xh[:, k, t * P:(t + 1) * P], xl[:, k, t * P:(t + 1) * P]
                    w_hi, w_lo = wh[slot][:, k, 0:w], wl[slot][:, k, 0:w]
                    nc.tensor.matmul(out, hi, w_hi, start=(k == 0), stop=False)
                    nc.tensor.matmul(out, hi, w_lo, start=False, stop=False)
                    last = nc.tensor.matmul(out, lo, w_hi, start=False, stop=(k == KD - 1))
                last.then_inc(tile_ready, 1)

            def transposes(n, t):
                pe.wait_ge(normed, n + 1)
                pe.wait_ge(stored, n + 1)
                for j in range(2):
                    last = nc.tensor.transpose(pt[t % 2][:, j, :], qn[:, t % 2, j * P:(j + 1) * P], ident[:])
                last.then_inc(transposed, 1)

            with pe.Fori(0, NORMED // 2) as i:
                for slot in range(2):
                    pe.wait_ge(low_ready, 2 * i + slot + 1)
                    for t in range(T):
                        n = (2 * i + slot) * T + t
                        pe.wait_ge(bank_free_dve, n + 1)
                        products(t, slot, pm[t % BANKS][:, 0:CW], CW)
                        if t >= 2:
                            transposes(n - 2, t - 2)
                    for t in range(T - 2, T):
                        transposes((2 * i + slot) * T + t, t)
            with pe.Fori(NORMED // 2, SILU // 2) as i:
                for slot in range(2):
                    pe.wait_ge(low_ready, 2 * i + slot + 1)
                    for t in range(T):
                        pe.wait_ge(bank_free_dve, (2 * i + slot) * T + t + 1)
                        products(t, slot, pm[t % BANKS][:, 0:CW], CW)
            for ch in range(SILU, CHANNEL):
                w = CHUNKS[ch][1]
                pe.wait_ge(low_ready, ch + 1)
                for t in range(T):
                    m = (ch - SILU) * T + t - BANKS
                    if m < 0:
                        pe.wait_ge(bank_free_dve, SILU * T + t + 1)
                    else:
                        pe.wait_ge(bank_free_act, m + 1)
                    products(t, ch % 2, pm[t % BANKS][:, 0:w], w)
            for ch in range(CHANNEL, len(CHUNKS)):
                pe.wait_ge(low_ready, ch + 1)
                w_hi, w_lo = wh[ch % 2], wl[ch % 2]
                for g in range(4):
                    j, half = g // 2, g % 2
                    if ch == CHANNEL:
                        pe.wait_ge(bank_free_act, (CHANNEL - SILU) * T - BANKS + g + 1)
                    else:
                        pe.wait_ge(bank_free_dve, SILU * T + BANKS + g + 1)
                    for k in range(KD):
                        m_hi, m_lo = w_hi[:, k, j * P:(j + 1) * P], w_lo[:, k, j * P:(j + 1) * P]
                        n_hi, n_lo = xh[:, k, half * 512:half * 512 + 512], xl[:, k, half * 512:half * 512 + 512]
                        nc.tensor.matmul(pm[g][:], m_hi, n_hi, start=(k == 0), stop=False)
                        nc.tensor.matmul(pm[g][:], m_hi, n_lo, start=False, stop=False)
                        last = nc.tensor.matmul(pm[g][:], m_lo, n_hi, start=False, stop=(k == KD - 1))
                    last.then_inc(tile_ready, 1)

        @block.scalar
        def _(act):
            def high(ch):
                w = CHUNKS[ch][1]
                act.wait_ge(raw_in[ch % 2], 16 * (ch // 2 + 1))
                if ch >= 2:
                    act.wait_ge(tile_ready, T * (ch - 1))
                nc.scalar.copy(wh[ch % 2][:, :, 0:w], raw[ch % 2][:, :, 0:w]).then_inc(high_ready, 1)

            def store_transposed(n):
                ch, t = n // T, n % T
                dst, gain = (s["dqT"], s["gain_q"]) if ch < 2 else (s["dkT"], s["gain_k"])
                pair = 2 * (ch % 2)
                act.wait_ge(transposed, n + 1)
                nc.scalar.activation(dst[:, pair:pair + 2, t * P:(t + 1) * P], pt[n % 2][:], ACT.Copy,
                                     scale=gain[:, 0:1]).then_inc(stored, 1)

            act.sem_inc(stored, 2)
            high(0)
            for ch in range(len(CHUNKS)):
                if ch + 1 < len(CHUNKS):
                    high(ch + 1)
                for t in range(T):
                    n = ch * T + t
                    if ch < NORMED:
                        act.wait_ge(tile_ready, n + 1)
                        if n >= 2:
                            act.wait_ge(summed, n - 1)
                        nc.scalar.activation(sq[:, n % 2], pm[t % BANKS][:, 0:CW].rearrange(
                            "p (g d) -> p g d", g=4), ACT.Square).then_inc(squared, 1)
                        if t >= 3:
                            store_transposed(n - 3)
                        if t == T - 1:
                            for m in range(n - 2, n + 1):
                                store_transposed(m)
                    elif SILU <= ch < CHANNEL:
                        m = (ch - SILU) * T + t
                        act.wait_ge(tile_ready, n + 1)
                        if m >= 2:
                            act.wait_ge(r_out[m % 2], 16 * (m // 2))
                        if ch == SILU + 1:
                            nc.scalar.copy(s["glr"][:, t, :], pm[t % BANKS][:, CW:CW + GR])
                        nc.scalar.activation(rst[:, m % 2, :], pm[t % BANKS][:, 0:CW], ACT.Silu) \
                            .then_inc(bank_free_act, 1)
                        act.wait_ge(bank_free_act, m + 1)
                        act.dma_start(s["r_dram"][:, t, (ch - SILU) * CW:(ch - SILU + 1) * CW],
                                      rst[:, m % 2, :]).then_inc(r_out[m % 2], 16)
            for i in range(2):
                act.wait_ge(r_out[i], 16 * T)

        @block.gpsimd
        def _(pool):
            for n in range(NORMED * T):
                pool.wait_ge(summed, n + 1)
                if n >= 2:
                    pool.wait_ge(normed, n - 1)
                nc.gpsimd.tensor_scalar(rs[:, n % 2, :], ss[:, n % 2, :], EPS * DDK, None,
                                        ALU.add).then_inc(shifted, 1)
                pool.wait_ge(shifted, n + 1)
                nc.gpsimd.tensor_tensor(rs[:, n % 2, :], rs[:, n % 2, :], s["minus_half"][:, 0:4],
                                        ALU.pow).then_inc(rstd_ready, 1)

        @block.vector
        def _(dve):
            def low(ch):
                w = CHUNKS[ch][1]
                dve.wait_ge(high_ready, ch + 1)
                nc.vector.tensor_tensor(wl[ch % 2][:, :, 0:w], raw[ch % 2][:, :, 0:w],
                                        wh[ch % 2][:, :, 0:w].bitcast(F32), ALU.subtract).then_inc(low_ready, 1)

            dve.sem_inc(bank_free_dve, BANKS)
            low(0)
            for ch in range(len(CHUNKS)):
                if ch + 1 < len(CHUNKS):
                    low(ch + 1)
                for t in range(T):
                    n = ch * T + t
                    if ch < NORMED:
                        i = n % 2
                        dve.wait_ge(squared, n + 1)
                        if n >= 2:
                            dve.wait_ge(rstd_ready, n - 1)
                        nc.vector.tensor_reduce(ss[:, i, :], sq[:, i], AX.X, ALU.add).then_inc(summed, 1)
                        dve.wait_ge(rstd_ready, n + 1)
                        if n >= 2:
                            dve.wait_ge(transposed, n - 1)
                        nc.vector.tensor_tensor(qn[:, i].rearrange("p (g d) -> p g d", g=4),
                                                pm[t % BANKS][:, 0:CW].rearrange("p (g d) -> p g d", g=4),
                                                rs[:, i, :].unsqueeze(2).to_broadcast([P, 4, DDK]),
                                                ALU.mult).then_inc(normed, 1)
                        dve.wait_ge(normed, n + 1)
                        dve.sem_inc(bank_free_dve, 1)
                    elif ch < SILU:
                        dst = s["gv"] if ch < 6 else s["dv"]
                        dve.wait_ge(tile_ready, n + 1)
                        nc.vector.tensor_copy(dst[:, t, (ch % 2) * CW:(ch % 2 + 1) * CW],
                                              pm[t % BANKS][:, 0:CW]).then_inc(bank_free_dve, 1)
                    elif ch >= CHANNEL and t < 4:
                        dst = s["gqT"] if ch == CHANNEL else s["gkT"]
                        dve.wait_ge(tile_ready, CHANNEL * T + (ch - CHANNEL) * 4 + t + 1)
                        nc.vector.tensor_copy(dst[:, t // 2, (t % 2) * 512:(t % 2) * 512 + 512],
                                              pm[t][:]).then_inc(bank_free_dve, 1)


def stage_gla(nc, a, s):
    with ExitStack() as c:
        sb, ps, sem = mem(nc, c, "gated")
        glrT = sb("glrT", [GR, SEQ])
        wa2 = sb("wa2", [GR, 2 * P])
        ba = sb("ba", [P, 2])
        absz = sb("absz", [P, 2, SEQ])
        minz = sb("minz", [P, 2, SEQ])
        keepsum = sb("keepsum", [P, SEQ])
        b = sb("b", [P, 2, SEQ])
        arg = sb("arg", [P, 3, 2 * SEQ])
        e_b = sb("e_b", [P, 2, SEQ])
        e_mid = sb("e_mid", [P, 2, 2, SEQ])
        rgn = s["rg"]
        gain = sb("gain", [P, GDV])
        st = sb("st", [P, 2, 5, 2, P])
        QD, KD_, QO, QI, KL = range(5)
        kdT = sb("kdT", [P, 2, 2, P])
        sc = sb("sc", [P, 2, 2, 2, P])
        state = sb("state", [P, 2, GDV])
        sq = sb("sq", [P, HG, GDV])
        ss = sb("ss", [P, 2, HG])
        rs = sb("rs", [P, 2, HG])
        on = sb("on", [P, HG, GDV])
        banks = [ps(f"bank{i}", [P, 512]) for i in range(8)]
        wa2_in, gain_in, r_in = sem("wa2_in"), sem("gain_in"), sem("r_in")
        ba_in = [sem("ba_in0"), sem("ba_in1")]
        filled = sem("filled")
        glrT_mm, glrT_ready, z_ready = sem("glrT_mm"), sem("glrT_ready"), sem("z_ready")
        abs_ready, min_ready, log_step = sem("abs_ready"), sem("min_ready"), sem("log_step")
        sum_step, b_ready, arg_ready = sem("sum_step"), sem("b_ready"), sem("arg_ready")
        exp_ready = sem("exp_ready")
        gain_ready, rgn_ready = sem("gain_ready"), sem("rgn_ready")
        staged, scores_ready, kdT_ready = sem("staged"), sem("scores_ready"), sem("kdT_ready")
        masked, o_ready, ds_ready = sem("masked"), sem("o_ready"), sem("ds_ready")
        state_ready, squared, summed = sem("state_ready"), sem("squared"), sem("summed")
        shifted, rstd_ready, normed, gated = sem("shifted"), sem("rstd_ready"), sem("normed"), sem("gated")
        masked_clear = sem("masked_clear")
        block = c.enter_context(nc.Block())
        ident, causal, gqT, gkT, gv = s["ident"], s["causal"], s["gqT"], s["gkT"], s["gv"]
        HALVES = 2 * SEQ // 64

        def out_bank(u, odd):
            return banks[(3, 4, 5, 7)[2 * u + odd]]

        def tok(x, n):
            return x[:, :, n * P:(n + 1) * P]

        @block.sync
        def _(sp):
            sp.dma_start(wa2[:], a["gla_wa2"][0]).then_inc(wa2_in, 16)
            for j in range(2):
                sp.dma_start(ba[:, j:j + 1], a["gla_ba"][:, j * P:(j + 1) * P].rearrange(
                    "a p -> p a")).then_inc(ba_in[j], 16)
            sp.dma_start(gain[:], a["gla_onorm_g"].to_broadcast([P, GDV])).then_inc(gain_in, 16)
            sp.dma_start(rgn[:], s["r_dram"]).then_inc(r_in, 16)

        @block.gpsimd
        def _(pool):
            nc.gpsimd.memset(keepsum[:], 1.0).then_inc(filled, 1)
            pool.wait_ge(filled, 1)
            nc.gpsimd.memset(keepsum[:].rearrange("p (n x) -> p n x", x=P)[:, :, 0:1], 0.0).then_inc(filled, 1)
            pool.wait_ge(gain_ready, 1)
            pool.wait_ge(r_in, 16)
            for n in range(T):
                v = rgn[:, n, :].rearrange("p (h d) -> p h d", h=HG)
                nc.gpsimd.tensor_tensor(v, v, gain[:].unsqueeze(1).to_broadcast([P, HG, GDV]),
                                        ALU.mult).then_inc(rgn_ready, 1)
            for n in range(T):
                pool.wait_ge(summed, n + 1)
                if n >= 2:
                    pool.wait_ge(normed, n - 1)
                nc.gpsimd.tensor_scalar(rs[:, n % 2, :], ss[:, n % 2, :], EPS * GDV, None,
                                        ALU.add).then_inc(shifted, 1)
                pool.wait_ge(shifted, n + 1)
                nc.gpsimd.tensor_tensor(rs[:, n % 2, :], rs[:, n % 2, :], s["minus_half"][:, 0:HG],
                                        ALU.pow).then_inc(rstd_ready, 1)

        @block.tensor
        def _(pe):
            for t in range(T):
                last = nc.tensor.transpose(banks[4 + t // 4][0:GR, (t % 4) * P:(t % 4 + 1) * P],
                                           s["glr"][:, t, :], ident[:])
            last.then_inc(glrT_mm, 1)
            pe.wait_ge(wa2_in, 16)
            pe.wait_ge(glrT_ready, 1)
            for g in range(4):
                nc.tensor.matmul(banks[g][:], wa2[:, (g // 2) * P:(g // 2 + 1) * P],
                                 glrT[:, (g % 2) * 512:(g % 2 + 1) * 512], start=True,
                                 stop=True).then_inc(z_ready, 1)

            def scores(n):
                u = n % 2
                pe.wait_ge(staged, n + 1)
                if n >= 1:
                    pe.wait_ge(kdT_ready, n)
                    pe.wait_ge(masked, n)
                for p in range(2):
                    nc.tensor.transpose(banks[0][:, p * P:(p + 1) * P], st[:, u, KL, p, :], ident[:])
                for i, (key, query) in enumerate(((KD_, QD), (QO, QO))):
                    for p in range(2):
                        for odd in range(2):
                            r = 64 * odd
                            last = nc.tensor.matmul(banks[1 + odd][:, (2 * i + p) * P:(2 * i + p + 1) * P],
                                                    st[r:r + 64, u, key, p, :], st[r:r + 64, u, query, p, :],
                                                    start=True, stop=True)
                last.then_inc(scores_ready, 1)

            def outputs(n):
                u = n % 2
                pe.wait_ge(masked, n + 1)
                pe.wait_ge(state_ready, n + 1)
                if n >= 2:
                    pe.wait_ge(normed, n - 1)
                for h in range(HG):
                    r, p = 64 * (h % 2), h // 2
                    o = out_bank(u, h % 2)[:, p * P:(p + 1) * P]
                    nc.tensor.matmul(o, sc[:, u, h % 2, p, :], gv[:, n, h * P:(h + 1) * P], start=True,
                                     stop=False)
                    last = nc.tensor.matmul(o, st[r:r + 64, u, QI, p, :], state[r:r + 64, p, :],
                                            start=False, stop=True)
                last.then_inc(o_ready, 1)
                pe.wait_ge(kdT_ready, n + 1)
                for p in range(2):
                    last = nc.tensor.matmul(banks[6][:, p * 256:(p + 1) * 256], kdT[:, u, p, :],
                                            gv[:, n, p * 256:(p + 1) * 256], start=True, stop=True)
                last.then_inc(ds_ready, 1)

            scores(0)
            for n in range(T):
                if n + 1 < T:
                    scores(n + 1)
                outputs(n)

        @block.scalar
        def _(act):
            act.wait_ge(ba_in[0], 16)
            act.wait_ge(ba_in[1], 16)
            for g in range(4):
                act.wait_ge(z_ready, g + 1)
                nc.scalar.activation(absz[:, g // 2, (g % 2) * 512:(g % 2 + 1) * 512], banks[g][:], ACT.Abs,
                                     bias=ba[:, g // 2:g // 2 + 1]).then_inc(abs_ready, 1)
            for p in range(2):
                act.wait_ge(abs_ready, 2 * p + 2)
                nc.scalar.activation(absz[:, p, :], absz[:, p, :], ACT.Exp, scale=-1.0).then_inc(log_step, 1)
                act.wait_ge(log_step, 2 * p + 1)
                nc.scalar.activation(absz[:, p, :], absz[:, p, :], ACT.Ln, bias=1.0).then_inc(log_step, 1)
            act.wait_ge(b_ready, 2)
            nc.scalar.activation(e_b[:], b[:], ACT.Exp, scale=1.0 / TAU).then_inc(exp_ready, 1)
            act.wait_ge(arg_ready, 1)
            flat = arg[:, 0, :].rearrange("p (j x) -> p j x", j=2)
            nc.scalar.activation(e_mid[:, 0], flat, ACT.Exp, scale=1.0 / TAU).then_inc(exp_ready, 1)
            nc.scalar.activation(e_mid[:, 1], flat, ACT.Exp, scale=-1.0 / TAU).then_inc(exp_ready, 1)
            act.wait_ge(arg_ready, 2)
            halves = arg[:, 1, :].rearrange("p (w g x) -> p w g x", g=2, x=64)
            nc.scalar.activation(halves[:, :, 0, :], halves[:, :, 0, :], ACT.Exp,
                                 scale=-1.0 / TAU).then_inc(exp_ready, 1)
            nc.scalar.activation(halves[:, :, 1, :], halves[:, :, 1, :], ACT.Exp,
                                 scale=1.0 / TAU).then_inc(exp_ready, 1)
            act.wait_ge(arg_ready, 3)
            nc.scalar.activation(arg[:, 2, :], arg[:, 2, :], ACT.Exp, scale=-1.0 / TAU).then_inc(exp_ready, 1)
            for n in range(T):
                act.wait_ge(scores_ready, n + 1)
                if n >= 2:
                    act.wait_ge(ds_ready, n - 1)
                nc.scalar.copy(kdT[:, n % 2], banks[0][:, 0:2 * P].rearrange("p (j x) -> p j x", j=2)) \
                    .then_inc(kdT_ready, 1)
                act.wait_ge(o_ready, n + 1)
                if n >= 1:
                    act.wait_ge(summed, n)
                for odd in range(2):
                    last = nc.scalar.activation(sq[:, 2 * odd:2 * odd + 2, :], out_bank(n % 2, odd)[:, 0:2 * P]
                                                .rearrange("p (h d) -> p h d", h=2), ACT.Square)
                last.then_inc(squared, 1)

        @block.vector
        def _(dve):
            dve.wait_ge(glrT_mm, 1)
            for i in range(2):
                last = nc.vector.tensor_copy(glrT[:, i * 512:(i + 1) * 512], banks[4 + i][0:GR, :])
            last.then_inc(glrT_ready, 1)
            dve.wait_ge(gain_in, 16)
            nc.vector.tensor_scalar(gain[:], gain[:], GDV ** 0.5, None, ALU.mult).then_inc(gain_ready, 1)
            nc.vector.memset(sc[:], 0.0).then_inc(masked_clear, 1)
            nc.vector.memset(state[:], 0.0).then_inc(state_ready, 1)
            dve.wait_ge(ba_in[0], 16)
            dve.wait_ge(ba_in[1], 16)
            for g in range(4):
                dve.wait_ge(abs_ready, g + 1)
                nc.vector.tensor_scalar(minz[:, g // 2, (g % 2) * 512:(g % 2 + 1) * 512], banks[g][:],
                                        ba[:, g // 2:g // 2 + 1], 0.0, ALU.add, ALU.min).then_inc(min_ready, 1)
            dve.wait_ge(filled, 2)
            for p in range(2):
                dve.wait_ge(log_step, 2 * p + 2)
                dve.wait_ge(min_ready, 2 * p + 2)
                nc.vector.tensor_tensor(minz[:, p, :], minz[:, p, :], absz[:, p, :],
                                        ALU.subtract).then_inc(sum_step, 1)
                dve.wait_ge(sum_step, p + 1)
                nc.vector.tensor_tensor_scan(b[:, p, :], keepsum[:], minz[:, p, :], 0.0, ALU.mult,
                                             ALU.add).then_inc(b_ready, 1)
            dve.wait_ge(b_ready, 2)
            bf = b[:].rearrange("p j x -> p (j x)")

            def minus(i, width, at):
                v = bf.rearrange("p (w x) -> p w x", x=width)
                return nc.vector.tensor_tensor(arg[:, i, :].rearrange("p (w x) -> p w x", x=width), v,
                                               v[:, :, at:at + 1].to_broadcast([P, 2 * SEQ // width, width]),
                                               ALU.subtract)
            minus(0, 64, 31).then_inc(sum_step, 1)
            dve.wait_ge(sum_step, 3)
            nc.vector.tensor_scalar(arg[:, 0, :], arg[:, 0, :], 40.0 * TAU, -40.0 * TAU, ALU.min,
                                    ALU.max).then_inc(arg_ready, 1)
            minus(1, P, 63).then_inc(arg_ready, 1)
            minus(2, P, 127).then_inc(arg_ready, 1)

            def stage(n):
                u = n % 2
                if n >= 2:
                    dve.wait_ge(o_ready, n - 1)
                e_off = arg[:, 1, :].rearrange("p (j x) -> p j x", j=2)[:, :, n * P:(n + 1) * P]
                e_last = arg[:, 2, :].rearrange("p (j x) -> p j x", j=2)[:, :, n * P:(n + 1) * P]
                q, k = tok(gqT, n), tok(gkT, n)

                def scaled_q(dst, src, e):
                    return nc.vector.scalar_tensor_tensor(out=dst, in0=src, scalar=GDK ** -0.5, in1=e,
                                                          op0=ALU.mult, op1=ALU.mult)
                scaled_q(st[:, u, QD], q, tok(e_mid[:, 0], n))
                nc.vector.tensor_tensor(st[:, u, KD_], k, tok(e_mid[:, 1], n), ALU.mult)
                nc.vector.tensor_tensor(st[:, u, QO, :, 0:64], k[:, :, 0:64], e_off[:, :, 0:64], ALU.mult)
                scaled_q(st[:, u, QO, :, 64:P], q[:, :, 64:P], e_off[:, :, 64:P])
                nc.vector.tensor_tensor(st[:, u, KL], k, e_last, ALU.mult)
                scaled_q(st[:, u, QI], q, tok(e_b, n)).then_inc(staged, 1)

            def mask(n):
                u = n % 2
                dve.wait_ge(scores_ready, n + 1)
                for odd in range(2):
                    v = banks[1 + odd][:].rearrange("p (i h x) -> p i h x", i=2, h=2)
                    nc.vector.tensor_copy(sc[0:64, u, odd, :, 64:P], v[0:64, 1, :, 64:P])
                    for g in (0, 64):
                        last = nc.vector.tensor_tensor(sc[g:g + 64, u, odd, :, g:g + 64],
                                                       v[g:g + 64, 0, :, g:g + 64], causal[g:g + 64, 0:2],
                                                       ALU.mult)
                last.then_inc(masked, 1)

            def carry(n):
                dve.wait_ge(o_ready, n + 1)
                dve.wait_ge(ds_ready, n + 1)
                for r in (0, 64):
                    for p in range(2):
                        last = nc.vector.scalar_tensor_tensor(
                            out=state[r:r + 64, p, :], in0=state[r:r + 64, p, :],
                            scalar=e_b[r:r + 64, p, n * P + P - 1:n * P + P],
                            in1=banks[6][r:r + 64, p * 256 + 2 * r:p * 256 + 2 * r + P],
                            op0=ALU.mult, op1=ALU.add)
                last.then_inc(state_ready, 1)

            def norm(n):
                u = n % 2
                dve.wait_ge(squared, n + 1)
                if n >= 2:
                    dve.wait_ge(rstd_ready, n - 1)
                nc.vector.tensor_reduce(ss[:, u, :], sq[:], AX.X, ALU.add).then_inc(summed, 1)
                dve.wait_ge(rstd_ready, n + 1)
                if n >= 1:
                    dve.wait_ge(gated, n)
                for odd in range(2):
                    last = nc.vector.tensor_tensor(
                        on[:, 2 * odd:2 * odd + 2, :],
                        out_bank(u, odd)[:, 0:2 * P].rearrange("p (h d) -> p h d", h=2),
                        rs[:, u, 2 * odd:2 * odd + 2].unsqueeze(2).to_broadcast([P, 2, GDV]), ALU.mult)
                last.then_inc(normed, 1)
                dve.wait_ge(normed, n + 1)
                dve.wait_ge(rgn_ready, n + 1)
                v = rgn[:, n, :].rearrange("p (h o d) -> p o h d", h=2, o=2)
                nc.vector.tensor_tensor(v, on[:].rearrange("p (o h) d -> p o h d", o=2), v,
                                        ALU.mult).then_inc(gated, 1)

            dve.wait_ge(exp_ready, 6)
            dve.wait_ge(masked_clear, 1)
            stage(0)
            for n in range(T):
                if n + 1 < T:
                    stage(n + 1)
                mask(n)
                carry(n)
                if n >= 1:
                    norm(n - 1)
            norm(T - 1)


def stage_diffattn(nc, a, s):
    with ExitStack() as c:
        sb, ps, sem = mem(nc, c, "diff")
        bias = sb("bias", [P, HD, 2 * P])
        mirror = sb("mirror", [P, HD, 2 * P])
        anti = sb("anti", [P, P])
        gain = sb("gain", [P, DDV])
        neg_lam = sb("neg_lam", [P, 1])
        nmax = sb("nmax", [P, 2, 2])
        sums = sb("sums", [P, 3, 2])
        coef = sb("coef", [P, 2, 2])
        prob = sb("prob", [P, 2, 2, SEQ])
        wt = sb("wt", [P, 2, SEQ])
        wT = sb("wT", [P, 2, T, P])
        sq = sb("sq", [P, DDV])
        ss = sb("ss", [P, 2])
        rs = sb("rs", [P, 2])
        inv = sb("inv", [P, 4])
        score = [ps(f"score{i}", [P, SEQ]) for i in range(2)]
        pt = [ps(f"pt{i}", [P, 4, P]) for i in range(2)]
        po = [ps(f"po{i}", [P, 512]) for i in range(2)]
        dqT, dkT, dv, od, ident = s["dqT"], s["dkT"], s["dv"], s["od"], s["ident"]
        bias_in, gain_in = sem("bias_in"), sem("gain_in")
        prepared, zeroed, anti_ready, turned = sem("prepared"), sem("zeroed"), sem("anti_ready"), sem("turned")
        scored = [sem("scored0"), sem("scored1")]
        biased = [sem("biased0"), sem("biased1")]
        max_ready = [sem("max_ready0"), sem("max_ready1")]
        exp_done = [sem("exp_done0"), sem("exp_done1")]
        coef_step, weighted = sem("coef_step"), sem("weighted")
        transposed, wT_ready = sem("transposed"), sem("wT_ready")
        o_ready, squared = sem("o_ready"), sem("squared")
        shifted, rooted, rstd_ready, normed = sem("shifted"), sem("rooted"), sem("rstd_ready"), sem("normed")
        block = c.enter_context(nc.Block())
        N = HD * T
        groups = [-(-(n % T + 1) // 4) for n in range(N)]
        first = [sum(groups[:n]) for n in range(N + 1)]

        @block.sync
        def _(sp):
            sp.dma_start(gain[:], a["diff_subln_g"].to_broadcast([P, DDV])).then_inc(gain_in, 16)
            for h in range(HD):
                sp.dma_start(mirror[:, h, :], bass.AP(s["rel_dram"].tensor, h * REL + 1,
                                                      [[1, P], [1, 2 * P]])).then_inc(bias_in, 16)

        @block.tensor
        def _(pe):
            def scores(n):
                h, t = n // T, n % T
                for comp in range(2):
                    r = 64 * comp
                    if n >= 1:
                        pe.wait_ge(exp_done[comp], n)
                    for k0 in range(0, (t + 1) * P, 512):
                        k1 = min(k0 + 512, (t + 1) * P)
                        last = nc.tensor.matmul(score[comp][:, k0:k1], dqT[r:r + 64, h, t * P:(t + 1) * P],
                                                dkT[r:r + 64, h, k0:k1], start=True, stop=True)
                    last.then_inc(scored[comp], 1)

            def transposes(n):
                pe.wait_ge(weighted, n + 1)
                for g in range(groups[n]):
                    i = first[n] + g
                    if i >= 2:
                        pe.wait_ge(wT_ready, i - 1)
                    for j in range(4 * g, min(4 * g + 4, n % T + 1)):
                        last = nc.tensor.transpose(pt[i % 2][:, j % 4, :], wt[:, n % 2, j * P:(j + 1) * P],
                                                   ident[:])
                    last.then_inc(transposed, 1)

            def values(n):
                h, t = n // T, n % T
                pe.wait_ge(wT_ready, first[n + 1])
                if n == 0:
                    pe.wait_ge(prepared, 4)
                if n >= 2:
                    pe.wait_ge(normed, n - 1)
                for j in range(t + 1):
                    last = nc.tensor.matmul(po[n % 2][:, 0:DDV], wT[:, n % 2, j, :],
                                            dv[:, j, h * DDV:(h + 1) * DDV], start=(j == 0), stop=(j == t))
                last.then_inc(o_ready, 1)

            pe.wait_ge(bias_in, 16 * HD)
            pe.wait_ge(anti_ready, 1)
            for h in range(HD):
                last = nc.tensor.matmul(po[h // 2][:, (h % 2) * 256:(h % 2) * 256 + 256], anti[:],
                                        mirror[:, h, :], start=True, stop=True)
            last.then_inc(turned, 1)

            for n in range(N + 2):
                if n < N:
                    scores(n)
                if 1 <= n <= N:
                    transposes(n - 1)
                if n >= 2:
                    values(n - 2)

        @block.scalar
        def _(act):
            def exps(n):
                nk = (n % T + 1) * P
                for comp in range(2):
                    act.wait_ge(max_ready[comp], n + 1)
                    if n >= 2:
                        act.wait_ge(weighted, n - 1)
                    nc.scalar.activation(prob[:, n % 2, comp, 0:nk], score[comp][:, 0:nk], ACT.Exp,
                                         bias=nmax[:, n % 2, comp:comp + 1],
                                         accum_out=sums[:, n % 3, comp:comp + 1]).then_inc(exp_done[comp], 1)

            def copies(n):
                for g in range(groups[n]):
                    w = min(4, n % T + 1 - 4 * g)
                    act.wait_ge(transposed, first[n] + g + 1)
                    if n >= 2 and g == 0:
                        act.wait_ge(o_ready, n - 1)
                    nc.scalar.copy(wT[:, n % 2, 4 * g:4 * g + w, :],
                                   pt[(first[n] + g) % 2][:, 0:w, :]).then_inc(wT_ready, 1)

            def square(n):
                act.wait_ge(o_ready, n + 1)
                if n >= 1:
                    act.wait_ge(squared, n)
                if n >= 2:
                    act.wait_ge(shifted, n - 1)
                nc.scalar.activation(sq[:], po[n % 2][:, 0:DDV], ACT.Square, scale=inv[:, n % 4:n % 4 + 1],
                                     accum_out=ss[:, n % 2:n % 2 + 1]).then_inc(squared, 1)

            for n in range(N + 2):
                if n < N:
                    exps(n)
                if 1 <= n <= N:
                    copies(n - 1)
                if n >= 2:
                    square(n - 2)

        @block.gpsimd
        def _(pool):
            nc.gpsimd.memset(anti[:], 0.0).then_inc(zeroed, 1)
            pool.wait_ge(zeroed, 1)
            nc.gpsimd.affine_select(out=anti[:], in_=anti[:], compare_op=ALU.not_equal, fill=1.0,
                                    base=-(P - 1), pattern=[[1, P]], channel_multiplier=1).then_inc(anti_ready, 1)
            for n in range(N):
                i = n % 2
                pool.wait_ge(squared, n + 1)
                if n >= 2:
                    pool.wait_ge(normed, n - 1)
                nc.gpsimd.tensor_scalar(rs[:, i:i + 1], ss[:, i:i + 1], EPS * DDV, None,
                                        ALU.add).then_inc(shifted, 1)
                pool.wait_ge(shifted, n + 1)
                nc.gpsimd.tensor_tensor(rs[:, i:i + 1], rs[:, i:i + 1], s["minus_half"][:, 0:1],
                                        ALU.pow).then_inc(rooted, 1)
                pool.wait_ge(rooted, n + 1)
                nc.gpsimd.tensor_tensor(rs[:, i:i + 1], rs[:, i:i + 1], inv[:, n % 4:n % 4 + 1],
                                        ALU.mult).then_inc(rstd_ready, 1)

        @block.vector
        def _(dve):
            dve.wait_ge(gain_in, 16)
            nc.vector.tensor_scalar(gain[:], gain[:], (1.0 - LAMBDA_INIT) * DDV ** 0.5, None,
                                    ALU.mult).then_inc(prepared, 1)
            nc.vector.tensor_scalar(neg_lam[:], s["lam"][:], -1.0, None, ALU.mult).then_inc(prepared, 1)
            dve.wait_ge(turned, 1)
            for i in range(2):
                nc.vector.tensor_copy(bias[:, 2 * i:2 * i + 2, :], po[i][:].rearrange(
                    "p (h x) -> p h x", h=2)).then_inc(prepared, 1)
            dve.wait_ge(prepared, 4)

            def maxima(n):
                h, nk = n // T, (n % T + 1) * P
                w = min(nk, 2 * P)
                for comp in range(2):
                    dve.wait_ge(scored[comp], n + 1)
                    near = score[comp][:, nk - w:nk]
                    nc.vector.tensor_tensor(near, near, bias[:, h, 2 * P - w:2 * P],
                                            ALU.add).then_inc(biased[comp], 1)
                for comp in range(2):
                    dve.wait_ge(biased[comp], n + 1)
                    nc.vector.tensor_reduce(nmax[:, n % 2, comp:comp + 1], score[comp][:, 0:nk], AX.X, ALU.max,
                                            negate=True).then_inc(max_ready[comp], 1)

            def weights(n):
                nk, i = (n % T + 1) * P, n % 2
                dve.wait_ge(exp_done[0], n + 1)
                dve.wait_ge(exp_done[1], n + 1)
                if n >= 4:
                    dve.wait_ge(rstd_ready, n - 3)
                nc.vector.reciprocal(inv[:, n % 4:n % 4 + 1], sums[:, n % 3, 0:1])
                nc.vector.reciprocal(coef[:, i, 0:1], sums[:, n % 3, 1:2]).then_inc(coef_step, 1)
                dve.wait_ge(coef_step, 2 * n + 1)
                nc.vector.tensor_scalar(coef[:, i, 1:2], coef[:, i, 0:1], sums[:, n % 3, 0:1], neg_lam[:],
                                        ALU.mult, ALU.mult).then_inc(coef_step, 1)
                dve.wait_ge(coef_step, 2 * n + 2)
                if n >= 2:
                    dve.wait_ge(transposed, first[n - 1])
                nc.vector.scalar_tensor_tensor(out=wt[:, i, 0:nk], in0=prob[:, i, 1, 0:nk],
                                               scalar=coef[:, i, 1:2], in1=prob[:, i, 0, 0:nk],
                                               op0=ALU.mult, op1=ALU.add).then_inc(weighted, 1)

            def norm(n):
                h, t = n // T, n % T
                dve.wait_ge(rstd_ready, n + 1)
                nc.vector.scalar_tensor_tensor(out=od[:, t, h * DDV:(h + 1) * DDV], in0=po[n % 2][:, 0:DDV],
                                               scalar=rs[:, n % 2:n % 2 + 1], in1=gain[:], op0=ALU.mult,
                                               op1=ALU.mult).then_inc(normed, 1)

            for n in range(N + 3):
                if n < N:
                    maxima(n)
                if 1 <= n <= N:
                    weights(n - 1)
                if n >= 3:
                    norm(n - 3)


def stage_outproj(nc, a, s):
    with ExitStack() as c:
        sb, ps, sem = mem(nc, c, "outproj")
        x = sb("x", [P, 2, D])
        g2 = sb("g2", [P, D])
        xn = sb("xn", [P, 2, D])
        oh = sb("o_high", [P, 2, KD, P], F32R)
        ol = sb("o_low", [P, 2, KD, P], F32R)
        sq = sb("sq", [P, D])
        raw = [sb("w_raw0", [P, KD, CW]), sb("w_raw1", [P, KD, CW], kib=181)]
        xnT = sb("xnT", [P, KD, 512], kib=84)
        wh = sb("w_high", [P, KD, D], F32R, kib=117)
        wl = sb("w_low", [P, KD, D], F32R, kib=149)
        wr = sb("w_router", [P, KD, NG + NE], kib=189)
        br = sb("b_router", [P, NG + NE], kib=190.5)
        ss = sb("ss", [P, T], kib=190.75)
        rs = sb("rs", [P, T], kib=190.8125)
        lT = sb("lT", [NG + NE, 512], kib=100)
        h, ident = s["h"], s["ident"]
        pt = [ps(f"pt{i}", [P, 4, P]) for i in range(2)]
        po = [ps(f"po{i}", [P, 512]) for i in range(4)]
        pr = ps("pr", [P, 512])
        pl = ps("pl", [P, T, NG + NE])
        x_in = [sem("x_in0"), sem("x_in1")]
        g2_in = sem("g2_in")
        router_in = [sem(f"router_in{i}") for i in range(4)]
        raw_in = [sem("raw_in0"), sem("raw_in1")]
        w_high, w_low = sem("w_high_ready"), sem("w_low_ready")
        transposed, o_high, o_low = sem("transposed"), sem("o_high_ready"), sem("o_low_ready")
        xn_stored = sem("xn_stored")
        product, added = sem("product"), sem("added")
        squared, shifted, rstd_ready = sem("squared"), sem("shifted"), sem("rstd_ready")
        gain_ready, normed = sem("gain_ready"), sem("normed")
        xn_out = [sem("xn_out0"), sem("xn_out1")]
        logits_mm, lT_ready, logits_t = sem("logits_mm"), sem("lT_ready"), sem("logits_t")
        block = c.enter_context(nc.Block())
        x_rows = a["x"].rearrange("b (t p) d -> (b t) p d", p=P)
        xn_rows = s["xn2_dram"].rearrange("(t p) d -> t p d", p=P)
        order = [("o", 0)]
        for t in range(T):
            order += ([("o", t + 1)] if t + 1 < T else []) + ([("x", t - 1)] if t >= 1 else [])
        order += [("x", T - 1)]
        place = {what: i for i, what in enumerate(order)}

        @block.sync
        def _(sp):
            for i in range(4):
                if i >= 2:
                    sp.wait_ge(w_low, i - 1)
                sp.dma_start(raw[i % 2][:], a["w_out"][0, :, i * CW:(i + 1) * CW].rearrange(
                    "(k p) c -> p k c", p=P)).then_inc(raw_in[i % 2], 16)
            for t in range(2):
                sp.dma_start(x[:, t, :], x_rows[t]).then_inc(x_in[t], 16)
            sp.dma_start(g2[:], a["norm2_g"].to_broadcast([P, D])).then_inc(g2_in, 16)
            for i, (dst, src) in enumerate((
                    (wr[:, :, 0:NG], a["moe_wg"][0].rearrange("(p k) e -> p k e", p=P)),
                    (wr[:, :, NG:], a["moe_we"][0].rearrange("(p k) e -> p k e", p=P)),
                    (br[:, 0:NG], a["moe_bg"].to_broadcast([P, NG])),
                    (br[:, NG:], a["moe_be"].to_broadcast([P, NE])))):
                sp.dma_start(dst, src).then_inc(router_in[i], 16)
            for t in range(T):
                sp.wait_ge(normed, t + 1)
                sp.dma_start(xn_rows[t], xn[:, t % 2, :]).then_inc(xn_out[t % 2], 16)
                if t + 2 < T:
                    sp.wait_ge(added, 2 * t + 2)
                    sp.dma_start(x[:, t % 2, :], x_rows[t + 2]).then_inc(x_in[t % 2], 16)
            for i in range(2):
                sp.wait_ge(xn_out[i], 16 * (T // 2))

        @block.tensor
        def _(pe):
            def transposes(kind, t):
                if (kind, t) not in place:
                    return
                i = place[kind, t]
                pe.wait_ge(normed, t + 1) if kind == "x" else None
                for g in range(2):
                    if i >= 1:
                        before = order[:i]
                        pe.wait_ge(o_low, 2 * sum(k == "o" for k, _ in before) - (1 - g)
                                   ) if before[-1][0] == "o" else pe.wait_ge(
                            xn_stored, 2 * sum(k == "x" for k, _ in before) - (1 - g))
                    for j in range(4):
                        if kind == "o":
                            src = (s["rg"] if g == 0 else s["od"])[:, t, j * P:(j + 1) * P]
                        else:
                            src = xn[:, t % 2, :].rearrange("p (c k) -> p k c", k=KD)[:, 4 * g + j, :]
                        last = nc.tensor.transpose(pt[g][:, j, :], src, ident[:])
                    last.then_inc(transposed, 1)

            def products(t):
                for half in range(2):
                    n = 2 * t + half
                    if t == 0:
                        pe.wait_ge(w_low, 2 * half + 2)
                    if n >= 4:
                        pe.wait_ge(added, n - 3)
                    if half == 0:
                        pe.wait_ge(o_low, 2 * t + 2)
                    for k in range(KD):
                        hi, lo = oh[:, t % 2, k, :], ol[:, t % 2, k, :]
                        w_hi, w_lo = wh[:, k, half * 512:half * 512 + 512], wl[:, k, half * 512:half * 512 + 512]
                        nc.tensor.matmul(po[n % 4][:], hi, w_hi, start=(k == 0), stop=False)
                        nc.tensor.matmul(po[n % 4][:], hi, w_lo, start=False, stop=False)
                        last = nc.tensor.matmul(po[n % 4][:], lo, w_hi, start=False, stop=(k == KD - 1))
                    last.then_inc(product, 1)

            def router(half):
                pe.wait_ge(xn_stored, 8 * (half + 1))
                if half == 0:
                    pe.wait_ge(router_in[0], 16)
                    pe.wait_ge(router_in[1], 16)
                else:
                    pe.wait_ge(lT_ready, 1)
                for k in range(KD):
                    last = nc.tensor.matmul(pr[0:NG + NE, :], wr[:, k, :], xnT[:, k, :], start=(k == 0),
                                            stop=(k == KD - 1))
                last.then_inc(logits_mm, 1)
                pe.wait_ge(lT_ready, half + 1)
                for j in range(4):
                    last = nc.tensor.transpose(pl[:, 4 * half + j, :], lT[:, j * P:(j + 1) * P],
                                               ident[0:NG + NE, 0:NG + NE])
                last.then_inc(logits_t, 1)

            transposes("o", 0)
            for t in range(T):
                transposes("o", t + 1)
                products(t)
                transposes("x", t - 1)
                if t == 4:
                    router(0)
            transposes("x", T - 1)
            router(1)

        @block.scalar
        def _(act):
            def w_split(i):
                act.wait_ge(raw_in[i % 2], 16 * (i // 2 + 1))
                nc.scalar.copy(wh[:, :, i * CW:(i + 1) * CW], raw[i % 2][:]).then_inc(w_high, 1)

            def take(kind, t):
                i = place[kind, t]
                for g in range(2):
                    act.wait_ge(transposed, 2 * i + g + 1)
                    if kind == "o":
                        if t >= 2 and g == 0:
                            act.wait_ge(product, 2 * (t - 1))
                        nc.scalar.copy(oh[:, t % 2, 4 * g:4 * g + 4, :], pt[g][:]).then_inc(o_high, 1)
                    else:
                        if t >= 4 and g == 0:
                            act.wait_ge(logits_mm, 1)
                        nc.scalar.copy(xnT[:, 4 * g:4 * g + 4, (t % 4) * P:(t % 4 + 1) * P],
                                       pt[g][:]).then_inc(xn_stored, 1)

            def square(t):
                act.wait_ge(added, 2 * t + 2)
                if t >= 1:
                    act.wait_ge(squared, t)
                nc.scalar.activation(sq[:], h[:, t, :], ACT.Square,
                                     accum_out=ss[:, t:t + 1]).then_inc(squared, 1)

            take("o", 0)
            for i in range(4):
                w_split(i)
            for t in range(T):
                if t + 1 < T:
                    take("o", t + 1)
                if t >= 1:
                    take("x", t - 1)
                square(t)
            take("x", T - 1)

        @block.gpsimd
        def _(pool):
            for t in range(T):
                pool.wait_ge(squared, t + 1)
                nc.gpsimd.tensor_scalar(rs[:, t:t + 1], ss[:, t:t + 1], EPS * D, None,
                                        ALU.add).then_inc(shifted, 1)
                pool.wait_ge(shifted, t + 1)
                nc.gpsimd.tensor_tensor(rs[:, t:t + 1], rs[:, t:t + 1], s["minus_half"][:, 0:1],
                                        ALU.pow).then_inc(rstd_ready, 1)

        @block.vector
        def _(dve):
            def low(t):
                for g in range(2):
                    dve.wait_ge(o_high, 2 * t + g + 1)
                    nc.vector.tensor_tensor(ol[:, t % 2, 4 * g:4 * g + 4, :], pt[g][:],
                                            oh[:, t % 2, 4 * g:4 * g + 4, :].bitcast(F32),
                                            ALU.subtract).then_inc(o_low, 1)

            def add(t):
                dve.wait_ge(x_in[t % 2], 16 * (t // 2 + 1))
                for half in range(2):
                    n = 2 * t + half
                    dve.wait_ge(product, n + 1)
                    nc.vector.tensor_tensor(h[:, t, half * 512:half * 512 + 512], po[n % 4][:],
                                            x[:, t % 2, half * 512:half * 512 + 512], ALU.add).then_inc(added, 1)

            def norm(t):
                dve.wait_ge(rstd_ready, t + 1)
                if t >= 2:
                    dve.wait_ge(xn_out[t % 2], 16 * (t // 2))
                    dve.wait_ge(transposed, 2 * place["x", t - 2] + 2)
                nc.vector.scalar_tensor_tensor(out=xn[:, t % 2, :], in0=h[:, t, :], scalar=rs[:, t:t + 1],
                                               in1=g2[:], op0=ALU.mult, op1=ALU.mult).then_inc(normed, 1)

            def logits(half):
                dve.wait_ge(logits_mm, half + 1)
                if half == 1:
                    dve.wait_ge(logits_t, 1)
                nc.vector.tensor_copy(lT[:], pr[0:NG + NE, :]).then_inc(lT_ready, 1)
                dve.wait_ge(logits_t, half + 1)
                nc.vector.tensor_tensor(s["logits"][:, 4 * half:4 * half + 4, :],
                                        pl[:, 4 * half:4 * half + 4, :],
                                        br[:].unsqueeze(1).to_broadcast([P, 4, NG + NE]), ALU.add)

            low(0)
            for i in range(4):
                dve.wait_ge(w_high, i + 1)
                nc.vector.tensor_tensor(wl[:, :, i * CW:(i + 1) * CW], raw[i % 2][:],
                                        wh[:, :, i * CW:(i + 1) * CW].bitcast(F32), ALU.subtract).then_inc(w_low, 1)
            dve.wait_ge(g2_in, 16)
            nc.vector.tensor_scalar(g2[:], g2[:], D ** 0.5, None, ALU.mult).then_inc(gain_ready, 1)
            dve.wait_ge(gain_ready, 1)
            dve.wait_ge(router_in[2], 16)
            dve.wait_ge(router_in[3], 16)
            for t in range(T):
                if t + 1 < T:
                    low(t + 1)
                add(t)
                norm(t)
                if t == 4:
                    logits(0)
            logits(1)


def stage_route(nc, a, s):
    with ExitStack() as c:
        sb, ps, sem = mem(nc, c, "route")
        gmax = sb("gmax", [P, T, 1])
        gexp = sb("gexp", [P, T, NG])
        gw = sb("gw", [P, T, 1])
        first = sb("first", [P, T, NG])
        taken = sb("taken", [P, T, 1])
        le = sb("le", [P, T, NG, EPG])
        top = sb("top", [P, T, 8])
        top_at = sb("top_at", [P, T, 8], U32)
        at = sb("at", [P, T, 2])
        e2 = sb("e2", [P, T, 1])
        w = sb("w", [P, T, 2])
        one = sb("one", [P, 2, T, NE])
        member = sb("member", [P, T, NE], BF16)
        weight = sb("weight", [P, T, NE])
        weight2 = sb("weight2", [P, T, NE])
        part = sb("part", [P, T, NE], BF16)
        iota_e = sb("iota_e", [P, NE])
        iota_t = sb("iota_t", [P, T])
        iota_p = sb("iota_p", [P, 1])
        before = sb("before", [P, P], BF16)
        ones = sb("ones", [P, P], BF16)
        plus1 = sb("plus1", [P, T, NE])
        pp = ps("pp", [P, T, NE])
        pc = ps("pc", [P, NE])
        logits, rows, place, counts = s["logits"], s["slot_rows"], s["place"], s["counts"]
        made, before_ready = sem("made"), sem("before_ready")
        step, gshift, gexp_ready = sem("step"), sem("gshift"), sem("gexp_ready")
        dshift, e2_ready = sem("dshift"), sem("e2_ready")
        member_ready, counted = sem("member_ready"), sem("counted")
        block = c.enter_context(nc.Block())

        @block.gpsimd
        def _(pool):
            nc.gpsimd.memset(ones[:], 1.0).then_inc(made, 1)
            nc.gpsimd.memset(before[:], 1.0).then_inc(made, 1)
            pool.wait_ge(made, 2)
            nc.gpsimd.affine_select(out=before[:], in_=before[:], compare_op=ALU.is_gt, fill=0.0, base=0,
                                    pattern=[[1, P]], channel_multiplier=-1).then_inc(before_ready, 1)
            for dst, pattern, mult in ((iota_e, [[1, NE]], 0), (iota_t, [[1, T]], 0), (iota_p, [[0, 1]], 1),
                                       (s["iota_slot"], [[1, CAP]], 0)):
                nc.gpsimd.iota(dst[:], pattern=pattern, base=0, channel_multiplier=mult,
                               allow_small_or_imprecise_dtypes=True).then_inc(made, 1)

        @block.tensor
        def _(pe):
            pe.wait_ge(before_ready, 1)
            pe.wait_ge(member_ready, 1)
            for t in range(T):
                nc.tensor.matmul(pp[:, t, :], before[:], member[:, t, :], start=True, stop=(t == 0))
                for earlier in range(t):
                    nc.tensor.matmul(pp[:, t, :], ones[:], member[:, earlier, :], start=False,
                                     stop=(earlier == t - 1))
            for t in range(T):
                last = nc.tensor.matmul(pc[:], ones[:], member[:, t, :], start=(t == 0), stop=(t == T - 1))
            last.then_inc(counted, 1)

        @block.scalar
        def _(act):
            act.wait_ge(gshift, 1)
            nc.scalar.activation(gexp[:], gexp[:], ACT.Exp).then_inc(gexp_ready, 1)
            act.wait_ge(dshift, 1)
            nc.scalar.activation(e2[:], e2[:], ACT.Exp).then_inc(e2_ready, 1)

        @block.vector
        def _(dve):
            n = [0]

            def then(ins):
                n[0] += 1
                ins.then_inc(step, 1)
                dve.wait_ge(step, n[0])

            V = nc.vector
            lg = logits[:, :, 0:NG]
            then(V.tensor_reduce(gmax[:], lg, AX.X, ALU.max))
            V.tensor_tensor(gexp[:], lg, gmax[:].to_broadcast([P, T, NG]), ALU.subtract).then_inc(gshift, 1)
            then(V.tensor_tensor(first[:], lg, gmax[:].to_broadcast([P, T, NG]), ALU.is_equal))
            then(V.tensor_copy(taken[:], first[:, :, 0:1]))
            for j in range(1, NG):
                then(V.tensor_tensor(first[:, :, j:j + 1], first[:, :, j:j + 1], taken[:], ALU.is_gt))
                then(V.tensor_tensor(taken[:], taken[:], first[:, :, j:j + 1], ALU.max))
            then(V.tensor_scalar(first[:], first[:], -1.0, -NEG, ALU.add, ALU.mult))
            then(V.tensor_tensor(le[:], logits[:, :, NG:].rearrange("p t (g e) -> p t g e", g=NG),
                                 first[:].unsqueeze(3).to_broadcast([P, T, NG, EPG]), ALU.add))
            for t in range(T):
                last = V.max(top[:, t, :], le[:, t].rearrange("p g e -> p (g e)"))
            then(last)
            for t in range(T):
                last = V.max_index(top_at[:, t, :], top[:, t, :], le[:, t].rearrange("p g e -> p (g e)"))
            V.tensor_tensor(e2[:], top[:, :, 1:2], top[:, :, 0:1], ALU.subtract).then_inc(dshift, 1)
            then(last)
            then(V.tensor_copy(at[:], top_at[:, :, 0:2]))
            dve.wait_ge(made, 6)
            for k in range(2):
                last = V.tensor_tensor(one[:, k], iota_e[:].unsqueeze(1).to_broadcast([P, T, NE]),
                                       at[:, :, k:k + 1].to_broadcast([P, T, NE]), ALU.is_equal)
            then(last)
            V.tensor_tensor(member[:], one[:, 0], one[:, 1], ALU.add).then_inc(member_ready, 1)
            dve.wait_ge(gexp_ready, 1)
            then(V.tensor_reduce(gw[:], gexp[:], AX.X, ALU.add))
            then(V.reciprocal(gw[:], gw[:]))
            dve.wait_ge(e2_ready, 1)
            then(V.tensor_scalar(w[:, :, 1:2], e2[:], 1.0, None, ALU.add))
            then(V.reciprocal(w[:, :, 0:1], w[:, :, 1:2]))
            then(V.tensor_tensor(w[:, :, 0:1], w[:, :, 0:1], gw[:], ALU.mult))
            then(V.tensor_tensor(w[:, :, 1:2], w[:, :, 0:1], e2[:], ALU.mult))
            then(V.tensor_tensor(weight[:], one[:, 0], w[:, :, 0:1].to_broadcast([P, T, NE]), ALU.mult))
            then(V.tensor_tensor(weight2[:], one[:, 1], w[:, :, 1:2].to_broadcast([P, T, NE]), ALU.mult))
            then(V.tensor_tensor(weight[:], weight[:], weight2[:], ALU.add))
            for k in range(3):
                then(V.tensor_copy(part[:], weight[:]))
                then(V.tensor_copy(rows[:, :, :, 4 + k], part[:]))
                if k < 2:
                    then(V.tensor_tensor(weight[:], weight[:], part[:], ALU.subtract))
            V.tensor_copy(rows[:, :, :, 0], iota_t[:].unsqueeze(2).to_broadcast([P, T, NE]))
            V.tensor_copy(rows[:, :, :, 1], iota_p[:].unsqueeze(2).to_broadcast([P, T, NE]))
            V.tensor_copy(rows[:, :, :, 2], one[:, 1])
            V.memset(rows[:, :, :, 3], 1.0)
            V.memset(rows[:, :, :, 7], 0.0)
            dve.wait_ge(counted, 1)
            dve.wait_ge(member_ready, 1)
            then(V.scalar_tensor_tensor(out=plus1[:].rearrange("p t e -> p (t e)"),
                                        in0=pp[:].rearrange("p t e -> p (t e)"), scalar=1.0,
                                        in1=member[:].rearrange("p t e -> p (t e)"), op0=ALU.add, op1=ALU.mult))
            V.tensor_scalar(place[:].rearrange("p e t -> p t e"), plus1[:], -1.0, None, ALU.add)
            V.tensor_copy(counts[:, 0:NE], pc[0:1, :])
            V.tensor_reduce(counts[:, NE:NE + 1], pc[0:1, :], AX.X, ALU.max)


def stage_experts(nc, a, s):
    with ExitStack() as c:
        sb, ps, sem = mem(nc, c, "experts")
        w13 = [[sb(f"w{m}_{u}", [P, KD, DE]) for m in (1, 3)] for u in range(2)]
        w2 = [sb(f"w2_{u}", [P, KE, D]) for u in range(2)]
        onehot = [sb(f"onehot{u}", [P, T, CAP], BF16) for u in range(2)]
        row = [sb(f"row{u}", [P, NROUTE]) for u in range(2)]
        tmp = [sb(f"tmp{u}", [P, 4]) for u in range(2)]
        token = [sb(f"token{u}", [P, 1], U32) for u in range(2)]
        dest = [sb(f"dest{u}", [P, 1], U32) for u in range(4)]
        wrow = [sb(f"wrow{u}", [P, 1]) for u in range(4)]
        xg = [sb(f"xg{u}", [P, D]) for u in range(2)]
        xT = [sb(f"xT{u}", [P, KD, CAP]) for u in range(2)]
        sl = sb("sl", [P, DE])
        hd = sb("hd", [P, DE])
        hT = sb("hT", [P, KE, CAP])
        y = [sb(f"y{u}", [P, D]) for u in range(2)]
        shifted_place = sb("shifted_place", [P, T])
        list_start = sb("list_start", [P, SEQ // CAP - 1])
        pid = ps("pid", [P, NROUTE])
        px = [ps(f"px{g}", [P, 4, CAP]) for g in range(2)]
        ph = [ps(f"ph{m}", [P, DE]) for m in range(2)]
        pt = ps("pt", [P, KE, CAP])
        py = [ps(f"py{g}", [P, 512]) for g in range(2)]
        ident, rows, place, counts, iota = s["ident"], s["slot_rows"], s["place"], s["counts"], s["iota_slot"]
        BIG = 4 * SEQ

        class Sems:
            def __init__(self, k):
                self.w1_in = [sem(f"w1_in{k}{u}") for u in range(2)]
                self.w3_in = [sem(f"w3_in{k}{u}") for u in range(2)]
                self.w2_in = [sem(f"w2_in{k}{u}") for u in range(2)]
                self.starts = sem(f"starts{k}")
                self.shift = sem(f"shifted{k}")
                self.onehot = sem(f"onehot_ready{k}")
                self.ids_mm = sem(f"ids_mm{k}")
                self.row_step = sem(f"row_step{k}")
                self.ids = sem(f"ids_ready{k}")
                self.passed = sem(f"pool_passed{k}")
                self.xg_in = [sem(f"xg_in{k}{u}") for u in range(2)]
                self.x_mm = sem(f"x_transposed{k}")
                self.xT_act = sem(f"xT_act{k}")
                self.xT_dve = sem(f"xT_dve{k}")
                self.h1 = sem(f"h1_ready{k}")
                self.h3 = sem(f"h3_ready{k}")
                self.silu = sem(f"silu_ready{k}")
                self.hd = sem(f"hidden_ready{k}")
                self.h_mm = sem(f"hidden_transposed{k}")
                self.hT = sem(f"hT_ready{k}")
                self.y_mm = sem(f"y_product{k}")
                self.y_act = sem(f"y_act{k}")
                self.y_dve = sem(f"y_dve{k}")
                self.y_out = [sem(f"y_out{k}{u}") for u in range(2)]

        def view_w(name, e):
            w = a[name][0]
            return w[bass.ds(e, 1)].rearrange("a (p k) f -> (a p) k f", k=KE if name == "moe_w2" else KD)

        def pick(q, e, n, u, src=None):
            places = place[:, bass.ds(e, 1), :].rearrange("p a t -> p (a t)") if src is None else src
            nc.vector.tensor_tensor(onehot[u][:], iota[:].unsqueeze(1).to_broadcast([P, T, CAP]),
                                    places.unsqueeze(2).to_broadcast([P, T, CAP]),
                                    ALU.is_equal).then_inc(q.onehot, 1)

        def ids_mm(pe, q, e, n, u):
            pe.wait_ge(q.onehot, n + 1)
            for t in range(T):
                last = nc.tensor.matmul(pid[:], onehot[u][:, t, :],
                                        rows[:, t, bass.ds(e, 1), :].rearrange("p a r -> p (a r)"),
                                        start=(t == 0), stop=(t == T - 1))
            last.then_inc(q.ids_mm, 1)

        def ids(dve, q, n, u, v):
            V = nc.vector
            dve.wait_ge(q.ids_mm, n + 1)
            V.tensor_copy(row[u][:], pid[:]).then_inc(q.row_step, 1)
            dve.wait_ge(q.row_step, 5 * n + 1)
            V.scalar_tensor_tensor(out=token[u][:], in0=row[u][:, 0:1], scalar=float(P), in1=row[u][:, 1:2],
                                   op0=ALU.mult, op1=ALU.add)
            V.scalar_tensor_tensor(out=tmp[u][:, 0:1], in0=row[u][:, 0:1], scalar=float(P),
                                   in1=row[u][:, 1:2], op0=ALU.mult, op1=ALU.add).then_inc(q.row_step, 1)
            V.tensor_tensor(tmp[u][:, 2:3], row[u][:, 4:5], row[u][:, 5:6], ALU.add).then_inc(q.row_step, 1)
            V.tensor_scalar(tmp[u][:, 3:4], row[u][:, 3:4], -float(BIG), float(BIG), ALU.mult,
                            ALU.add).then_inc(q.row_step, 1)
            dve.wait_ge(q.row_step, 5 * n + 4)
            V.scalar_tensor_tensor(out=tmp[u][:, 1:2], in0=row[u][:, 2:3], scalar=float(SEQ),
                                   in1=tmp[u][:, 0:1], op0=ALU.mult, op1=ALU.add).then_inc(q.row_step, 1)
            V.tensor_tensor(wrow[v][:], tmp[u][:, 2:3], row[u][:, 6:7], ALU.add)
            dve.wait_ge(q.row_step, 5 * n + 5)
            V.tensor_tensor(dest[v][:], tmp[u][:, 1:2], tmp[u][:, 3:4], ALU.add).then_inc(q.ids, 1)

        bound = {}

        def set_bounds(pool):
            bound["x"] = pool.to_reg(SEQ - 1)
            bound["y"] = pool.to_reg(2 * SEQ - 1)

        def gather(pool, q, n, u):
            pool.wait_ge(q.ids, n + 1)
            pool.sem_inc(q.passed, 1)
            nc.gpsimd.indirect_dma_start(xg[u][:], None, s["xn2_dram"],
                                         bass.IndirectOffsetOnAxis(token[u][:, 0:1], 0),
                                         bounds_check=bound["x"], oob_is_err=False).then_inc(q.xg_in[u], 16)

        def x_transposes(pe, q, n, u, arrived):
            pe.wait_ge(q.xg_in[u], arrived)
            for g in range(2):
                for j in range(4):
                    last = nc.tensor.transpose(px[g][:, j, :], xg[u][:].rearrange(
                        "p (c k) -> p k c", k=KD)[:, 4 * g + j, :], ident[:])
                last.then_inc(q.x_mm, 1)

        def gate(pe, q, m, u, arrived, done):
            pe.wait_ge((q.w1_in, q.w3_in)[m][u], arrived)
            for k in range(KD):
                last = nc.tensor.matmul(ph[m][:], xT[u][:, k, :], w13[u][m][:, k, :], start=(k == 0),
                                        stop=(k == KD - 1))
            last.then_inc(done, 1)

        def h_transposes(pe, q, n):
            pe.wait_ge(q.hd, n + 1)
            for j in range(KE):
                last = nc.tensor.transpose(pt[:, j, :], hd[:].rearrange("p (c k) -> p k c", k=KE)[:, j, :],
                                           ident[:])
            last.then_inc(q.h_mm, 1)

        def down(pe, q, n, u, arrived):
            pe.wait_ge(q.w2_in[u], arrived)
            pe.wait_ge(q.hT, n + 1)
            for g in range(2):
                for k in range(KE):
                    last = nc.tensor.matmul(py[g][:], hT[:, k, :], w2[u][:, k, g * 512:g * 512 + 512],
                                            start=(k == 0), stop=(k == KE - 1))
            last.then_inc(q.y_mm, 1)

        def scatter(pool, q, n, u, v):
            pool.wait_ge(q.y_act, n + 1)
            pool.wait_ge(q.y_dve, n + 1)
            pool.sem_inc(q.passed, 1)
            nc.gpsimd.indirect_dma_start(s["y_dram"], bass.IndirectOffsetOnAxis(dest[v][:, 0:1], 0), y[u][:],
                                         None, bounds_check=bound["y"],
                                         oob_is_err=False).then_inc(q.y_out[u], 16)

        def silu(act, q, n):
            act.wait_ge(q.h1, n + 1)
            nc.scalar.activation(sl[:], ph[0][:], ACT.Silu).then_inc(q.silu, 1)

        def hidden(dve, q, n):
            dve.wait_ge(q.silu, n + 1)
            dve.wait_ge(q.h3, n + 1)
            nc.vector.tensor_tensor(hd[:], ph[1][:], sl[:], ALU.mult).then_inc(q.hd, 1)

        def some(n, k):
            return n >= k if isinstance(n, int) else True

        def evacuate_x(eng, q, n, u, g, done):
            eng.wait_ge(q.x_mm, 2 * n + g + 1)
            dst = xT[u][:, 4 * g:4 * g + 4, :]
            (nc.scalar.copy if g == 0 else nc.vector.tensor_copy)(dst, px[g][:]).then_inc(done, 1)

        def evacuate_h(dve, q, n):
            dve.wait_ge(q.h_mm, n + 1)
            nc.vector.tensor_copy(hT[:], pt[:]).then_inc(q.hT, 1)

        q = Sems("")

        def sp_expert(sp, e, r, j):
            u = j % 2
            if some(e, 2):
                sp.wait_ge(q.h1, e - 1)
            sp.dma_start(w13[u][0][:], view_w("moe_w1", e)).then_inc(q.w1_in[u], 16)
            if some(e, 2):
                sp.wait_ge(q.h3, e - 1)
            sp.dma_start(w13[u][1][:], view_w("moe_w3", e)).then_inc(q.w3_in[u], 16)
            if some(e, 2):
                sp.wait_ge(q.y_mm, e - 1)
            sp.dma_start(w2[u][:], view_w("moe_w2", e)).then_inc(q.w2_in[u], 16)

        def pe_ids(pe, e, u):
            if some(e, 1):
                pe.wait_ge(q.row_step, 5 * (e - 1) + 1)
            ids_mm(pe, q, e, e, u)

        def pe_x(pe, e, r, u):
            if some(e, 1):
                pe.wait_ge(q.xT_act, e)
                pe.wait_ge(q.xT_dve, e)
            x_transposes(pe, q, e, u, 16 * (r + 1))

        def pe_expert(pe, e, r, j, last):
            u = j % 2
            pe.wait_ge(q.xT_act, e + 1)
            pe.wait_ge(q.xT_dve, e + 1)
            gate(pe, q, 0, u, 16 * (r + 1), q.h1)
            if not (last and j >= 2):
                pe_ids(pe, e + 2, u)
            gate(pe, q, 1, u, 16 * (r + 1), q.h3)
            if not (last and j == 3):
                pe_x(pe, e + 1, r + (j % 2), 1 - u)
            h_transposes(pe, q, e)
            if some(e, 1):
                pe.wait_ge(q.y_act, e)
                pe.wait_ge(q.y_dve, e)
            down(pe, q, e, u, 16 * (r + 1))

        def act_expert(act, e, r, j, last):
            u = j % 2
            silu(act, q, e)
            if not (last and j == 3):
                evacuate_x(act, q, e + 1, 1 - u, 0, q.xT_act)
            act.wait_ge(q.y_mm, e + 1)
            if some(e, 2):
                act.wait_ge(q.y_out[u], 16 * r)
            nc.scalar.activation(y[u][:, 0:512], py[0][:], ACT.Copy, scale=wrow[j][:, 0:1]).then_inc(q.y_act, 1)

        def dve_ids(dve, e, r, j):
            if some(e, 2):
                dve.wait_ge(q.xg_in[j % 2], 16 * r)
            if some(e, 4):
                dve.wait_ge(q.y_out[j % 2], 16 * (r - 1))
            ids(dve, q, e, j % 2, j)

        def dve_expert(dve, e, r, j, last):
            u = j % 2
            if not (last and j >= 2):
                pick(q, e + 2, e + 2, u)
            hidden(dve, q, e)
            if not (last and j >= 2):
                dve_ids(dve, e + 2, r + 1, (j + 2) % 4)
            if not (last and j == 3):
                evacuate_x(dve, q, e + 1, 1 - u, 1, q.xT_dve)
            evacuate_h(dve, q, e)
            dve.wait_ge(q.y_mm, e + 1)
            if some(e, 2):
                dve.wait_ge(q.y_out[u], 16 * r)
            nc.vector.tensor_scalar(y[u][:, 512:D], py[1][:], wrow[j][:, 0:1], None,
                                    ALU.mult).then_inc(q.y_dve, 1)

        def pool_gather(pool, e, u):
            if some(e, 2):
                pool.wait_ge(q.x_mm, 2 * (e - 1))
            gather(pool, q, e, u)

        def pool_expert(pool, e, r, j, last):
            u = j % 2
            if not (last and j >= 2):
                pool_gather(pool, e + 2, u)
            scatter(pool, q, e, u, j)

        def over_experts(eng, expert, **peeled):
            for j in range(4):
                expert(eng, j, j // 2, j, *([False] if peeled else []))
            with eng.Fori(1, NE // 4 - 1) as i:
                for j in range(4):
                    expert(eng, 4 * i + j, 2 * i + j // 2, j, *([False] if peeled else []))
            for j in range(4):
                e = NE - 4 + j
                expert(eng, e, e // 2, j, *([True] if peeled else []))

        with ExitStack() as b:
            block = b.enter_context(nc.Block())

            @block.sync
            def _(sp):
                over_experts(sp, sp_expert)

            @block.tensor
            def _(pe):
                for e in range(2):
                    pe_ids(pe, e, e)
                pe_x(pe, 0, 0, 0)
                over_experts(pe, pe_expert, last=True)

            @block.scalar
            def _(act):
                evacuate_x(act, q, 0, 0, 0, q.xT_act)
                over_experts(act, act_expert, last=True)

            @block.gpsimd
            def _(pool):
                set_bounds(pool)
                for e in range(2):
                    pool_gather(pool, e, e)
                over_experts(pool, pool_expert, last=True)
                for u in range(2):
                    pool.wait_ge(q.y_out[u], 16 * (NE // 2))

            @block.vector
            def _(dve):
                for e in range(2):
                    pick(q, e, e, e)
                    dve_ids(dve, e, 0, e)
                evacuate_x(dve, q, 0, 0, 1, q.xT_dve)
                over_experts(dve, dve_expert, last=True)

        MORE = SEQ // CAP - 1
        o = Sems("o")
        turn = sem("turn")

        def items(eng, item, skip):
            most = eng.value_load(counts[0:1, NE:NE + 1], min_val=0, max_val=SEQ)
            with eng.If(most > CAP):
                with eng.Fori(0, NE) as e:
                    count = eng.value_load(counts[0:1, bass.ds(e, 1)], min_val=0, max_val=SEQ)
                    with eng.Fori(0, MORE) as k:
                        n = MORE * e + k
                        with eng.If(count > CAP * (k + 1)):
                            item(eng, e, k, n)
                        with eng.Else():
                            skip(eng)
                        eng.nop()
                    eng.nop()
                eng.nop()
            eng.nop()

        def own(eng, *counted):
            for which, amount in counted:
                eng.sem_inc(which, amount)

        with ExitStack() as b:
            block = b.enter_context(nc.Block())

            @block.sync
            def _(sp):
                def item(sp, e, k, n):
                    sp.wait_ge(turn, n + 1)
                    sp.dma_start(w13[0][0][:], view_w("moe_w1", e)).then_inc(o.w1_in[0], 16)
                    sp.dma_start(w13[0][1][:], view_w("moe_w3", e)).then_inc(o.w3_in[0], 16)
                    sp.dma_start(w2[0][:], view_w("moe_w2", e)).then_inc(o.w2_in[0], 16)
                items(sp, item, lambda eng: own(eng, (o.w1_in[0], 16), (o.w3_in[0], 16), (o.w2_in[0], 16)))

            @block.tensor
            def _(pe):
                def item(pe, e, k, n):
                    ids_mm(pe, o, e, n, 0)
                    x_transposes(pe, o, n, 0, 16 * (n + 1))
                    pe.wait_ge(o.xT_act, n + 1)
                    pe.wait_ge(o.xT_dve, n + 1)
                    gate(pe, o, 0, 0, 16 * (n + 1), o.h1)
                    gate(pe, o, 1, 0, 16 * (n + 1), o.h3)
                    h_transposes(pe, o, n)
                    down(pe, o, n, 0, 16 * (n + 1))
                items(pe, item, lambda eng: own(eng, (o.ids_mm, 1), (o.x_mm, 2), (o.h1, 1), (o.h3, 1),
                                                (o.h_mm, 1), (o.y_mm, 1)))

            @block.scalar
            def _(act):
                def item(act, e, k, n):
                    evacuate_x(act, o, n, 0, 0, o.xT_act)
                    silu(act, o, n)
                    act.wait_ge(o.y_mm, n + 1)
                    nc.scalar.activation(y[0][:, 0:512], py[0][:], ACT.Copy,
                                         scale=wrow[0][:, 0:1]).then_inc(o.y_act, 1)
                items(act, item, lambda eng: own(eng, (o.xT_act, 1), (o.silu, 1), (o.y_act, 1)))

            @block.gpsimd
            def _(pool):
                def item(pool, e, k, n):
                    gather(pool, o, n, 0)
                    scatter(pool, o, n, 0, 0)
                    pool.wait_ge(o.y_out[0], 16 * (n + 1))
                    pool.sem_inc(turn, 1)
                set_bounds(pool)
                pool.sem_inc(turn, 1)
                items(pool, item, lambda eng: own(eng, (o.xg_in[0], 16), (o.y_out[0], 16), (turn, 1)))

            @block.vector
            def _(dve):
                for k in range(MORE):
                    last = nc.vector.memset(list_start[:, k:k + 1], float(CAP * (k + 1)))
                last.then_inc(o.starts, 1)
                dve.wait_ge(o.starts, 1)

                def item(dve, e, k, n):
                    dve.wait_ge(turn, n + 1)
                    nc.vector.tensor_tensor(shifted_place[:], place[:, bass.ds(e, 1), :].rearrange(
                        "p a t -> p (a t)"), list_start[:, bass.ds(k, 1)].to_broadcast([P, T]),
                        ALU.subtract).then_inc(o.shift, 1)
                    dve.wait_ge(o.shift, n + 1)
                    pick(o, e, n, 0, shifted_place[:])
                    ids(dve, o, n, 0, 0)
                    evacuate_x(dve, o, n, 0, 1, o.xT_dve)
                    hidden(dve, o, n)
                    evacuate_h(dve, o, n)
                    dve.wait_ge(o.y_mm, n + 1)
                    nc.vector.tensor_scalar(y[0][:, 512:D], py[1][:], wrow[0][:, 0:1], None,
                                            ALU.mult).then_inc(o.y_dve, 1)
                items(dve, item, lambda eng: own(eng, (o.shift, 1), (o.onehot, 1), (o.row_step, 5), (o.ids, 1),
                                                 (o.xT_dve, 1), (o.hd, 1), (o.hT, 1), (o.y_dve, 1)))


def stage_combine(nc, a, s):
    with ExitStack() as c:
        sb, ps, sem = mem(nc, c, "combine")
        ya = [sb(f"ya{u}", [P, 2, D]) for u in range(2)]
        res = [sb(f"res{u}", [P, D]) for u in range(2)]
        y_in = [sem("y_in0"), sem("y_in1")]
        added, summed = sem("added"), sem("summed")
        out_done = [sem("out_done0"), sem("out_done1")]
        block = c.enter_context(nc.Block())
        y_rows = s["y_dram"].rearrange("(k t p) d -> t p k d", k=2, p=P)
        out_rows = a["out"].rearrange("b (t p) d -> (b t) p d", p=P)

        @block.sync
        def _(sp):
            for t in range(T):
                if t >= 2:
                    sp.wait_ge(summed, t - 1)
                sp.dma_start(ya[t % 2][:], y_rows[t]).then_inc(y_in[t % 2], 16)

        @block.scalar
        def _(act):
            for t in range(T):
                act.wait_ge(summed, t + 1)
                act.dma_start(out_rows[t], res[t % 2][:]).then_inc(out_done[t % 2], 16)
            for u in range(2):
                act.wait_ge(out_done[u], 16 * (T // 2))

        @block.vector
        def _(dve):
            for t in range(T):
                u = t % 2
                dve.wait_ge(y_in[u], 16 * (t // 2 + 1))
                nc.vector.tensor_tensor(ya[u][:, 0, :], ya[u][:, 0, :], ya[u][:, 1, :],
                                        ALU.add).then_inc(added, 1)
                dve.wait_ge(added, t + 1)
                if t >= 2:
                    dve.wait_ge(out_done[u], 16 * (t // 2))
                nc.vector.tensor_tensor(res[u][:], ya[u][:, 0, :], s["h"][:, t, :], ALU.add).then_inc(summed, 1)


INPUTS = ["x", "rel_bias", "norm1_g", "w_in", "gla_wa2", "gla_ba", "gla_onorm_g", "diff_qnorm_g",
          "diff_knorm_g", "diff_lq1", "diff_lk1", "diff_lq2", "diff_lk2", "diff_subln_g", "w_out", "norm2_g",
          "moe_wg", "moe_bg", "moe_we", "moe_be", "moe_w1", "moe_w3", "moe_w2"]


def kernel(**inputs):
    import concourse.bacc as bacc
    from concourse.bass_utils import run_bass_kernel_spmd

    nc = bacc.Bacc("TRN2", target_bir_lowering=False, num_devices=1)
    arrays = {f"in_{n}": np.ascontiguousarray(inputs[n]) for n in INPUTS}
    arrays["in_bucket_onehot"] = buckets()
    a = {n[3:]: nc.dram_tensor(n, v.shape, mybir.dt.from_np(v.dtype), kind="ExternalInput").ap()
         for n, v in arrays.items()}
    a["out"] = nc.dram_tensor("out", (1, SEQ, D), F32, kind="ExternalOutput").ap()
    build(nc, a)
    r = run_bass_kernel_spmd(nc, [arrays], core_ids=[0])
    return r.results[0]["out"]
```

```python
import math
from contextlib import ExitStack

import numpy as np
import concourse.bass as bass
from concourse import mybir

F32 = mybir.dt.float32
F32R = mybir.dt.float32r
BF16 = mybir.dt.bfloat16
U32 = mybir.dt.uint32
I32 = mybir.dt.int32
ALU = mybir.AluOpType
ACT = mybir.ActivationFunctionType
AX = mybir.AxisListType

P = 128
SEQ = 1024
D = 1024
T = SEQ // P
KD = D // P
HG = 4
GDK, GDV = 64, 128
HD = 4
DDK, DDV = 64, 128
GR = 16
TAU = 16.0
EPS = 1e-6
LAMBDA_INIT = 0.8 - 0.6 * math.exp(-0.3 * 0)
NG, EPG = 4, 8
NE = NG * EPG
DE = 512
KE = DE // P
NEG = -1e30
BUCKETS, MAX_DIST = 32, 128
CAP = P
REL = 3 * P
CW = 256
CHUNKS_E, WC = 6, 2048
NROUTE = 6

GQ, GK, GV, GRC, GLR, DQ, DK, DV = 0, 256, 512, 1024, 1536, 1552, 2064, 2576


def buckets():
    rel = (REL - P) - np.arange(REL)
    n = np.maximum(rel, 0)
    exact = BUCKETS // 2
    large = exact + (np.log(np.maximum(n, exact).astype(np.float32) / np.float32(exact))
                     / np.float32(math.log(MAX_DIST / exact)) * np.float32(BUCKETS - exact)).astype(np.int32)
    b = np.where(n < exact, n, np.minimum(large, BUCKETS - 1))
    return (b[None, :] == np.arange(BUCKETS)[:, None]).astype(np.float32)


MAP = {"dqT": 20, "dkT": 36, "dv": 52, "gv": 68, "gqT": 84, "gkT": 92, "glr": 100, "xh": 101, "xl": 133,
       "rg": 101,
       "slot_rows": 187, "place": 186, "iota_slot": 185.5, "counts": 185.25}
LOCAL = {"constants": 101, "norm1": 165, "project": 165, "gated": 117, "diff": 117, "router": 20}
END = 223.9


def mem(nc, c, stage):
    at = [LOCAL.get(stage, 20) * 1024]

    def sb(name, shape, dt=F32, kib=None):
        size = math.prod(shape[1:]) * mybir.dt.size(dt)
        size = -(-size // 32) * 32
        if kib is None:
            kib = at[0] / 1024
            at[0] += size
        assert kib * 1024 + size <= END * 1024, (name, kib, size)
        return nc.alloc_sbuf_tensor_at(f"{stage}_{name}", shape, dt, offset=int(kib * 1024))

    def ps(name, shape, dt=F32):
        return c.enter_context(nc.psum_tensor(f"{stage}_{name}", shape, dt))

    sems = []

    def sem(name):
        sems.append(nc.alloc_semaphore(f"{stage}_{name}"))
        return sems[-1]

    def clear():
        nc.clear_and_free_semaphores(sems)
        nc.all_engine_barrier()
    c.callback(clear)
    return sb, ps, sem


def build(nc, a):
    with ExitStack() as top:
        def keep(name, shape, dt=F32):
            return top.enter_context(nc.sbuf_tensor(name, shape, dt))

        def dram(name, shape, dt=F32):
            return nc.dram_tensor(name, shape, dt, kind="Internal").ap()

        def place(name, shape, dt=F32):
            return nc.alloc_sbuf_tensor_at(name, shape, dt, offset=int(MAP[name] * 1024))

        s = {
            "rel_dram": dram("rel_dram", [HD, REL]), "xn2_dram": dram("xn2_dram", [SEQ, D]),
            "r_dram": dram("r_dram", [P, T, HG * GDV]), "sum_dram": dram("sum_dram", [SEQ + CAP, D]),
            "ident": keep("ident", [P, P]), "causal": keep("causal", [P, HG, 64]),
            "gain_q": keep("gain_q", [P, 1]), "gain_k": keep("gain_k", [P, 1]), "lam": keep("lam", [P, 1]),
            "minus_half": keep("minus_half", [P, 8]),
            "logits": keep("logits", [P, T, NG + NE]),
            "dqT": place("dqT", [P, HD, SEQ]), "dkT": place("dkT", [P, HD, SEQ]),
            "dv": place("dv", [P, T, HD * DDV]), "gv": place("gv", [P, T, HG * GDV]),
            "gqT": place("gqT", [P, 2, SEQ]), "gkT": place("gkT", [P, 2, SEQ]),
            "glr": place("glr", [P, T, GR]), "xh": place("xh", [P, KD, SEQ], F32R),
            "xl": place("xl", [P, KD, SEQ], F32R), "rg": place("rg", [P, T, HG * GDV]),
            "slot_rows": place("slot_rows", [P, T, NE, NROUTE], BF16),
            "place": place("place", [P, NE, T]), "iota_slot": place("iota_slot", [P, CAP]),
            "counts": place("counts", [1, NE + 1], I32),
        }
        s["od"] = s["gv"]
        stages = [stage_constants, stage_norm1, stage_project, stage_gla, stage_diffattn, stage_outproj,
                  stage_route, stage_experts, stage_store]
        for stage in stages:
            stage(nc, a, s)


def stage_constants(nc, a, s):
    with ExitStack() as c:
        sb, ps, sem = mem(nc, c, "constants")
        onehot = sb("onehot", [BUCKETS, REL])
        relb = sb("relb", [BUCKETS, HD])
        relf = sb("relf", [HD, REL])
        lvec = sb("lvec", [P, 4, DDK])
        lprod = sb("lprod", [P, 2, DDK])
        lsum = sb("lsum", [P, 2])
        lexp = sb("lexp", [P, 2])
        graw = sb("graw", [P, 2])
        pf = ps("pf", [HD, 512])
        ident, causal = s["ident"], s["causal"]
        relb_in = sem("relb_in")
        onehot_in = sem("onehot_in")
        lvec_in = [sem(f"lvec_in{i}") for i in range(4)]
        gain_in = [sem(f"gain_in{i}") for i in range(4)]
        rel_out = sem("rel_out")
        filled = sem("filled")
        relf_mm = sem("relf_mm")
        step = sem("step")
        lam_step = sem("lam_step")
        lam_exp = sem("lam_exp")
        masked = sem("masked")
        block = c.enter_context(nc.Block())

        @block.sync
        def _(sp):
            sp.dma_start(relb[:], a["rel_bias"]).then_inc(relb_in, 16)
            sp.dma_start(onehot[:], a["bucket_onehot"]).then_inc(onehot_in, 16)
            for i, n in enumerate(("diff_lq1", "diff_lk1", "diff_lq2", "diff_lk2")):
                sp.dma_start(lvec[:, i, :], a[n].to_broadcast([P, DDK])).then_inc(lvec_in[i], 16)
            for i, n in enumerate(("diff_qnorm_g", "diff_knorm_g")):
                for half in range(2):
                    sp.dma_start(graw[half * 64:half * 64 + 64, i:i + 1],
                                 a[n].rearrange("a k -> k a")).then_inc(gain_in[2 * i + half], 16)
            sp.wait_ge(masked, 1)
            sp.dma_start(s["rel_dram"], relf[:]).then_inc(rel_out, 16)
            sp.wait_ge(rel_out, 16)

        @block.gpsimd
        def _(pool):
            nc.gpsimd.memset(ident[:], 0.0).then_inc(filled, 1)
            nc.gpsimd.memset(causal[:], 1.0).then_inc(filled, 1)
            nc.gpsimd.memset(s["minus_half"][:], -0.5)
            pool.wait_ge(filled, 2)
            nc.gpsimd.affine_select(out=ident[:], in_=ident[:], compare_op=ALU.not_equal, fill=1.0, base=0,
                                    pattern=[[-1, P]], channel_multiplier=1).then_inc(filled, 1)
            for half in range(2):
                v = causal[64 * half:64 * half + 64]
                pool.wait_ge(filled, 3 + half)
                nc.gpsimd.affine_select(out=v, in_=v, compare_op=ALU.is_ge, fill=0.0, base=0,
                                        pattern=[[0, HG], [1, 64]],
                                        channel_multiplier=-1).then_inc(filled, 1)

        @block.tensor
        def _(pe):
            pe.wait_ge(relb_in, 16)
            pe.wait_ge(onehot_in, 16)
            nc.tensor.matmul(pf[:, 0:REL], relb[:], onehot[:], start=True, stop=True).then_inc(relf_mm, 1)

        @block.vector
        def _(dve):
            dve.wait_ge(relf_mm, 1)
            nc.vector.tensor_copy(relf[:], pf[:, 0:REL]).then_inc(step, 1)
            dve.wait_ge(step, 1)
            nc.vector.tensor_scalar(relf[:, 1:REL], relf[:, 1:REL], relf[:, 0:1], None,
                                    ALU.subtract).then_inc(step, 1)
            dve.wait_ge(step, 2)
            nc.vector.memset(relf[:, 0:1], 0.0)
            nc.vector.memset(relf[:, REL - P + 1:REL], NEG).then_inc(masked, 1)
            for i in range(4):
                dve.wait_ge(lvec_in[i], 16)
            for i in range(2):
                nc.vector.tensor_tensor(lprod[:, i, :], lvec[:, 2 * i, :], lvec[:, 2 * i + 1, :],
                                        ALU.mult).then_inc(lam_step, 1)
            dve.wait_ge(lam_step, 2)
            nc.vector.tensor_reduce(lsum[:], lprod[:], AX.X, ALU.add).then_inc(lam_step, 1)
            dve.wait_ge(lam_exp, 1)
            nc.vector.tensor_tensor(lexp[:, 0:1], lexp[:, 0:1], lexp[:, 1:2], ALU.subtract).then_inc(lam_step, 1)
            dve.wait_ge(lam_step, 4)
            nc.vector.tensor_scalar(s["lam"][:], lexp[:, 0:1], LAMBDA_INIT, None, ALU.add)
            for i in range(4):
                dve.wait_ge(gain_in[i], 16)
            nc.vector.tensor_scalar(s["gain_q"][:], graw[:, 0:1], DDK ** -0.5 * DDK ** 0.5, None, ALU.mult)
            nc.vector.tensor_scalar(s["gain_k"][:], graw[:, 1:2], DDK ** 0.5, None, ALU.mult)

        @block.scalar
        def _(act):
            act.wait_ge(lam_step, 3)
            nc.scalar.activation(lexp[:], lsum[:], ACT.Exp).then_inc(lam_exp, 1)


def stage_norm1(nc, a, s):
    with ExitStack() as c:
        sb, ps, sem = mem(nc, c, "norm1")
        g1 = sb("g1", [P, D])
        x = sb("x", [P, 2, D])
        sq = sb("sq", [P, D])
        xs = sb("xs", [P, 2, D])
        ss = sb("ss", [P, T])
        rs = sb("rs", [P, T])
        pt = [ps(f"pt{i}", [P, 4, P]) for i in range(4)]
        xh, xl, ident = s["xh"], s["xl"], s["ident"]
        g1_in = sem("g1_in")
        x_in = [sem("x_in0"), sem("x_in1")]
        squared = sem("squared")
        gain_ready = sem("gain_ready")
        shifted = sem("shifted")
        rstd_ready = sem("rstd_ready")
        scaled = sem("scaled")
        transposed = sem("transposed")
        high_ready = sem("high_ready")
        low_ready = sem("low_ready")
        block = c.enter_context(nc.Block())
        x_rows = a["x"].rearrange("b (t p) d -> (b t) p d", p=P)

        @block.sync
        def _(sp):
            sp.dma_start(x[:, 0, :], x_rows[0]).then_inc(x_in[0], 16)
            sp.dma_start(g1[:], a["norm1_g"].to_broadcast([P, D])).then_inc(g1_in, 16)
            sp.dma_start(x[:, 1, :], x_rows[1]).then_inc(x_in[1], 16)
            for t in range(2, T):
                sp.wait_ge(scaled, t - 1)
                sp.dma_start(x[:, t % 2, :], x_rows[t]).then_inc(x_in[t % 2], 16)

        @block.scalar
        def _(act):
            def high(t):
                for j in range(2):
                    act.wait_ge(transposed, 2 * t + j + 1)
                    nc.scalar.copy(xh[:, 4 * j:4 * j + 4, t * P:(t + 1) * P],
                                   pt[(2 * t + j) % 4][:]).then_inc(high_ready, 1)
            for t in range(T):
                act.wait_ge(x_in[t % 2], 16 * (t // 2 + 1))
                if t >= 1:
                    act.wait_ge(squared, t)
                nc.scalar.activation(sq[:], x[:, t % 2, :], ACT.Square,
                                     accum_out=ss[:, t:t + 1]).then_inc(squared, 1)
                if t >= 1:
                    high(t - 1)
            high(T - 1)

        @block.vector
        def _(dve):
            def low(t):
                for j in range(2):
                    n = 2 * t + j
                    dve.wait_ge(high_ready, n + 1)
                    hi = xh[:, 4 * j:4 * j + 4, t * P:(t + 1) * P]
                    nc.vector.tensor_tensor(xl[:, 4 * j:4 * j + 4, t * P:(t + 1) * P], pt[n % 4][:],
                                            hi.bitcast(F32), ALU.subtract).then_inc(low_ready, 1)
            dve.wait_ge(g1_in, 16)
            nc.vector.tensor_scalar(g1[:], g1[:], D ** 0.5, None, ALU.mult).then_inc(gain_ready, 1)
            dve.wait_ge(gain_ready, 1)
            for t in range(T):
                dve.wait_ge(rstd_ready, t + 1)
                if t >= 2:
                    dve.wait_ge(transposed, 2 * (t - 1))
                nc.vector.scalar_tensor_tensor(out=xs[:, t % 2, :], in0=x[:, t % 2, :], scalar=rs[:, t:t + 1],
                                               in1=g1[:], op0=ALU.mult, op1=ALU.mult).then_inc(scaled, 1)
                if t >= 1:
                    low(t - 1)
            low(T - 1)

        @block.gpsimd
        def _(pool):
            for t in range(T):
                pool.wait_ge(squared, t + 1)
                nc.gpsimd.tensor_scalar(rs[:, t:t + 1], ss[:, t:t + 1], EPS * D, None,
                                        ALU.add).then_inc(shifted, 1)
                pool.wait_ge(shifted, t + 1)
                nc.gpsimd.tensor_tensor(rs[:, t:t + 1], rs[:, t:t + 1], s["minus_half"][:, 0:1],
                                        ALU.pow).then_inc(rstd_ready, 1)

        @block.tensor
        def _(pe):
            for t in range(T):
                pe.wait_ge(scaled, t + 1)
                for j in range(2):
                    n = 2 * t + j
                    if n >= 4:
                        pe.wait_ge(low_ready, n - 3)
                    for k in range(4):
                        last = nc.tensor.transpose(pt[n % 4][:, k, :],
                                                   xs[:, t % 2, (4 * j + k) * P:(4 * j + k + 1) * P], ident[:])
                    last.then_inc(transposed, 1)


CHUNKS = [(DQ, CW), (DQ + CW, CW), (DK, CW), (DK + CW, CW), (GV, CW), (GV + CW, CW), (DV, CW),
          (DV + CW, CW), (GRC, CW), (GRC + CW, CW + GR), (GQ, CW), (GK, CW)]
NORMED = 4
SILU = 8
CHANNEL = 10


def stage_project(nc, a, s):
    with ExitStack() as c:
        sb, ps, sem = mem(nc, c, "project")
        W = CW + GR
        raw = [sb(f"w_raw{i}", [P, KD, W]) for i in range(2)]
        wh = [sb(f"w_high{i}", [P, KD, W], F32R) for i in range(2)]
        wl = [sb(f"w_low{i}", [P, KD, W], F32R) for i in range(2)]
        sq = sb("sq", [P, 2, 4, DDK])
        ss = sb("ss", [P, 2, 4])
        rs = sb("rs", [P, 2, 4])
        qn = sb("qn", [P, 2, 4 * DDK])
        rst = sb("rst", [P, 2, CW])
        pm = [ps(f"pm{i}", [P, 512]) for i in range(4)]
        pt = [ps(f"pt{i}", [P, 2, P]) for i in range(2)]
        xh, xl, ident = s["xh"], s["xl"], s["ident"]
        raw_in = [sem("raw_in0"), sem("raw_in1")]
        high_ready = sem("high_ready")
        low_ready = sem("low_ready")
        tile_ready = sem("tile_ready")
        bank_free_dve = sem("bank_free_dve")
        bank_free_act = sem("bank_free_act")
        squared = sem("squared")
        summed = sem("summed")
        shifted = sem("shifted")
        rstd_ready = sem("rstd_ready")
        normed = sem("normed")
        transposed = sem("transposed")
        stored = sem("stored")
        gated = sem("gated")
        r_out = [sem("r_out0"), sem("r_out1")]
        block = c.enter_context(nc.Block())
        BANKS = 4

        @block.sync
        def _(sp):
            for i, (col, w) in enumerate(CHUNKS):
                if i >= 2:
                    sp.wait_ge(low_ready, i - 1)
                sp.dma_start(raw[i % 2][:, :, 0:w], a["w_in"][0, :, col:col + w].rearrange(
                    "(k p) c -> p k c", p=P)).then_inc(raw_in[i % 2], 16)

        @block.tensor
        def _(pe):
            def products(t, slot, out, w):
                for k in range(KD):
                    hi, lo = xh[:, k, t * P:(t + 1) * P], xl[:, k, t * P:(t + 1) * P]
                    w_hi, w_lo = wh[slot][:, k, 0:w], wl[slot][:, k, 0:w]
                    nc.tensor.matmul(out, hi, w_hi, start=(k == 0), stop=False)
                    nc.tensor.matmul(out, hi, w_lo, start=False, stop=False)
                    last = nc.tensor.matmul(out, lo, w_hi, start=False, stop=(k == KD - 1))
                last.then_inc(tile_ready, 1)

            def transposes(n, t):
                pe.wait_ge(normed, n + 1)
                pe.wait_ge(stored, n + 1)
                for j in range(2):
                    last = nc.tensor.transpose(pt[t % 2][:, j, :], qn[:, t % 2, j * P:(j + 1) * P], ident[:])
                last.then_inc(transposed, 1)

            with pe.Fori(0, NORMED // 2) as i:
                for slot in range(2):
                    pe.wait_ge(low_ready, 2 * i + slot + 1)
                    for t in range(T):
                        n = (2 * i + slot) * T + t
                        pe.wait_ge(bank_free_dve, n + 1)
                        products(t, slot, pm[t % BANKS][:, 0:CW], CW)
                        if t >= 2:
                            transposes(n - 2, t - 2)
                    for t in range(T - 2, T):
                        transposes((2 * i + slot) * T + t, t)
            with pe.Fori(NORMED // 2, SILU // 2) as i:
                for slot in range(2):
                    pe.wait_ge(low_ready, 2 * i + slot + 1)
                    for t in range(T):
                        pe.wait_ge(bank_free_dve, (2 * i + slot) * T + t + 1)
                        products(t, slot, pm[t % BANKS][:, 0:CW], CW)
            for ch in range(SILU, CHANNEL):
                w = CHUNKS[ch][1]
                pe.wait_ge(low_ready, ch + 1)
                for t in range(T):
                    m = (ch - SILU) * T + t - BANKS
                    if m < 0:
                        pe.wait_ge(bank_free_dve, SILU * T + t + 1)
                    else:
                        pe.wait_ge(bank_free_act, m + 1)
                    products(t, ch % 2, pm[t % BANKS][:, 0:w], w)
            for ch in range(CHANNEL, len(CHUNKS)):
                pe.wait_ge(low_ready, ch + 1)
                w_hi, w_lo = wh[ch % 2], wl[ch % 2]
                for g in range(4):
                    j, half = g // 2, g % 2
                    if ch == CHANNEL:
                        pe.wait_ge(bank_free_act, (CHANNEL - SILU) * T - BANKS + g + 1)
                    else:
                        pe.wait_ge(bank_free_dve, SILU * T + BANKS + g + 1)
                    for k in range(KD):
                        m_hi, m_lo = w_hi[:, k, j * P:(j + 1) * P], w_lo[:, k, j * P:(j + 1) * P]
                        n_hi, n_lo = xh[:, k, half * 512:half * 512 + 512], xl[:, k, half * 512:half * 512 + 512]
                        nc.tensor.matmul(pm[g][:], m_hi, n_hi, start=(k == 0), stop=False)
                        nc.tensor.matmul(pm[g][:], m_hi, n_lo, start=False, stop=False)
                        last = nc.tensor.matmul(pm[g][:], m_lo, n_hi, start=False, stop=(k == KD - 1))
                    last.then_inc(tile_ready, 1)

        @block.scalar
        def _(act):
            def high(ch):
                w = CHUNKS[ch][1]
                act.wait_ge(raw_in[ch % 2], 16 * (ch // 2 + 1))
                if ch >= 2:
                    act.wait_ge(tile_ready, T * (ch - 1))
                nc.scalar.copy(wh[ch % 2][:, :, 0:w], raw[ch % 2][:, :, 0:w]).then_inc(high_ready, 1)

            def store_transposed(n):
                ch, t = n // T, n % T
                dst, gain = (s["dqT"], s["gain_q"]) if ch < 2 else (s["dkT"], s["gain_k"])
                pair = 2 * (ch % 2)
                act.wait_ge(transposed, n + 1)
                nc.scalar.activation(dst[:, pair:pair + 2, t * P:(t + 1) * P], pt[n % 2][:], ACT.Copy,
                                     scale=gain[:, 0:1]).then_inc(stored, 1)

            act.sem_inc(stored, 2)
            high(0)
            for ch in range(len(CHUNKS)):
                if ch + 1 < len(CHUNKS):
                    high(ch + 1)
                for t in range(T):
                    n = ch * T + t
                    if ch < NORMED:
                        act.wait_ge(tile_ready, n + 1)
                        if n >= 2:
                            act.wait_ge(summed, n - 1)
                        nc.scalar.activation(sq[:, n % 2], pm[t % BANKS][:, 0:CW].rearrange(
                            "p (g d) -> p g d", g=4), ACT.Square).then_inc(squared, 1)
                        if t >= 3:
                            store_transposed(n - 3)
                        if t == T - 1:
                            for m in range(n - 2, n + 1):
                                store_transposed(m)
                    elif SILU <= ch < CHANNEL:
                        m = (ch - SILU) * T + t
                        act.wait_ge(tile_ready, n + 1)
                        if m >= 2:
                            act.wait_ge(r_out[m % 2], 16 * (m // 2))
                        if ch == SILU + 1:
                            nc.scalar.copy(s["glr"][:, t, :], pm[t % BANKS][:, CW:CW + GR])
                        nc.scalar.activation(rst[:, m % 2, :], pm[t % BANKS][:, 0:CW], ACT.Silu) \
                            .then_inc(bank_free_act, 1)
                        act.wait_ge(bank_free_act, m + 1)
                        act.dma_start(s["r_dram"][:, t, (ch - SILU) * CW:(ch - SILU + 1) * CW],
                                      rst[:, m % 2, :]).then_inc(r_out[m % 2], 16)
            for i in range(2):
                act.wait_ge(r_out[i], 16 * T)

        @block.gpsimd
        def _(pool):
            for n in range(NORMED * T):
                pool.wait_ge(summed, n + 1)
                if n >= 2:
                    pool.wait_ge(normed, n - 1)
                nc.gpsimd.tensor_scalar(rs[:, n % 2, :], ss[:, n % 2, :], EPS * DDK, None,
                                        ALU.add).then_inc(shifted, 1)
                pool.wait_ge(shifted, n + 1)
                nc.gpsimd.tensor_tensor(rs[:, n % 2, :], rs[:, n % 2, :], s["minus_half"][:, 0:4],
                                        ALU.pow).then_inc(rstd_ready, 1)

        @block.vector
        def _(dve):
            def low(ch):
                w = CHUNKS[ch][1]
                dve.wait_ge(high_ready, ch + 1)
                nc.vector.tensor_tensor(wl[ch % 2][:, :, 0:w], raw[ch % 2][:, :, 0:w],
                                        wh[ch % 2][:, :, 0:w].bitcast(F32), ALU.subtract).then_inc(low_ready, 1)

            dve.sem_inc(bank_free_dve, BANKS)
            low(0)
            for ch in range(len(CHUNKS)):
                if ch + 1 < len(CHUNKS):
                    low(ch + 1)
                for t in range(T):
                    n = ch * T + t
                    if ch < NORMED:
                        i = n % 2
                        dve.wait_ge(squared, n + 1)
                        if n >= 2:
                            dve.wait_ge(rstd_ready, n - 1)
                        nc.vector.tensor_reduce(ss[:, i, :], sq[:, i], AX.X, ALU.add).then_inc(summed, 1)
                        dve.wait_ge(rstd_ready, n + 1)
                        if n >= 2:
                            dve.wait_ge(transposed, n - 1)
                        nc.vector.tensor_tensor(qn[:, i].rearrange("p (g d) -> p g d", g=4),
                                                pm[t % BANKS][:, 0:CW].rearrange("p (g d) -> p g d", g=4),
                                                rs[:, i, :].unsqueeze(2).to_broadcast([P, 4, DDK]),
                                                ALU.mult).then_inc(normed, 1)
                        dve.wait_ge(normed, n + 1)
                        dve.sem_inc(bank_free_dve, 1)
                    elif ch < SILU:
                        dst = s["gv"] if ch < 6 else s["dv"]
                        dve.wait_ge(tile_ready, n + 1)
                        nc.vector.tensor_copy(dst[:, t, (ch % 2) * CW:(ch % 2 + 1) * CW],
                                              pm[t % BANKS][:, 0:CW]).then_inc(bank_free_dve, 1)
                    elif ch >= CHANNEL and t < 4:
                        dst = s["gqT"] if ch == CHANNEL else s["gkT"]
                        dve.wait_ge(tile_ready, CHANNEL * T + (ch - CHANNEL) * 4 + t + 1)
                        nc.vector.tensor_copy(dst[:, t // 2, (t % 2) * 512:(t % 2) * 512 + 512],
                                              pm[t][:]).then_inc(bank_free_dve, 1)


def stage_gla(nc, a, s):
    with ExitStack() as c:
        sb, ps, sem = mem(nc, c, "gated")
        glrT = sb("glrT", [GR, SEQ])
        wa2 = sb("wa2", [GR, 2 * P])
        ba = sb("ba", [P, 2])
        absz = sb("absz", [P, 2, SEQ])
        minz = sb("minz", [P, 2, SEQ])
        keepsum = sb("keepsum", [P, SEQ])
        b = sb("b", [P, 2, SEQ])
        arg = sb("arg", [P, 3, 2 * SEQ])
        e_b = sb("e_b", [P, 2, SEQ])
        e_mid = sb("e_mid", [P, 2, 2, SEQ])
        rgn = s["rg"]
        gain = sb("gain", [P, GDV])
        st = sb("st", [P, 2, 5, 2, P])
        QD, KD_, QO, QI, KL = range(5)
        kdT = sb("kdT", [P, 2, 2, P])
        sc = sb("sc", [P, 2, 2, 2, P])
        state = sb("state", [P, 2, GDV])
        sq = sb("sq", [P, HG, GDV])
        ss = sb("ss", [P, 2, HG])
        rs = sb("rs", [P, 2, HG])
        on = sb("on", [P, HG, GDV])
        banks = [ps(f"bank{i}", [P, 512]) for i in range(8)]
        wa2_in, gain_in, r_in = sem("wa2_in"), sem("gain_in"), sem("r_in")
        ba_in = [sem("ba_in0"), sem("ba_in1")]
        filled = sem("filled")
        glrT_mm, glrT_ready, z_ready = sem("glrT_mm"), sem("glrT_ready"), sem("z_ready")
        abs_ready, min_ready, log_step = sem("abs_ready"), sem("min_ready"), sem("log_step")
        sum_step, b_ready, arg_ready = sem("sum_step"), sem("b_ready"), sem("arg_ready")
        exp_ready = sem("exp_ready")
        gain_ready, rgn_ready = sem("gain_ready"), sem("rgn_ready")
        staged, scores_ready, kdT_ready = sem("staged"), sem("scores_ready"), sem("kdT_ready")
        masked, o_ready, ds_ready = sem("masked"), sem("o_ready"), sem("ds_ready")
        state_ready, squared, summed = sem("state_ready"), sem("squared"), sem("summed")
        shifted, rstd_ready, normed, gated = sem("shifted"), sem("rstd_ready"), sem("normed"), sem("gated")
        masked_clear = sem("masked_clear")
        block = c.enter_context(nc.Block())
        ident, causal, gqT, gkT, gv = s["ident"], s["causal"], s["gqT"], s["gkT"], s["gv"]
        HALVES = 2 * SEQ // 64

        def out_bank(u, odd):
            return banks[(3, 4, 5, 7)[2 * u + odd]]

        def tok(x, n):
            return x[:, :, n * P:(n + 1) * P]

        @block.sync
        def _(sp):
            sp.dma_start(wa2[:], a["gla_wa2"][0]).then_inc(wa2_in, 16)
            for j in range(2):
                sp.dma_start(ba[:, j:j + 1], a["gla_ba"][:, j * P:(j + 1) * P].rearrange(
                    "a p -> p a")).then_inc(ba_in[j], 16)
            sp.dma_start(gain[:], a["gla_onorm_g"].to_broadcast([P, GDV])).then_inc(gain_in, 16)
            sp.dma_start(rgn[:], s["r_dram"]).then_inc(r_in, 16)

        @block.gpsimd
        def _(pool):
            nc.gpsimd.memset(keepsum[:], 1.0).then_inc(filled, 1)
            pool.wait_ge(filled, 1)
            nc.gpsimd.memset(keepsum[:].rearrange("p (n x) -> p n x", x=P)[:, :, 0:1], 0.0).then_inc(filled, 1)
            pool.wait_ge(gain_ready, 1)
            pool.wait_ge(r_in, 16)
            for n in range(T):
                v = rgn[:, n, :].rearrange("p (h d) -> p h d", h=HG)
                nc.gpsimd.tensor_tensor(v, v, gain[:].unsqueeze(1).to_broadcast([P, HG, GDV]),
                                        ALU.mult).then_inc(rgn_ready, 1)
            for n in range(T):
                pool.wait_ge(summed, n + 1)
                if n >= 2:
                    pool.wait_ge(normed, n - 1)
                nc.gpsimd.tensor_scalar(rs[:, n % 2, :], ss[:, n % 2, :], EPS * GDV, None,
                                        ALU.add).then_inc(shifted, 1)
                pool.wait_ge(shifted, n + 1)
                nc.gpsimd.tensor_tensor(rs[:, n % 2, :], rs[:, n % 2, :], s["minus_half"][:, 0:HG],
                                        ALU.pow).then_inc(rstd_ready, 1)

        @block.tensor
        def _(pe):
            for t in range(T):
                last = nc.tensor.transpose(banks[4 + t // 4][0:GR, (t % 4) * P:(t % 4 + 1) * P],
                                           s["glr"][:, t, :], ident[:])
            last.then_inc(glrT_mm, 1)
            pe.wait_ge(wa2_in, 16)
            pe.wait_ge(glrT_ready, 1)
            for g in range(4):
                nc.tensor.matmul(banks[g][:], wa2[:, (g // 2) * P:(g // 2 + 1) * P],
                                 glrT[:, (g % 2) * 512:(g % 2 + 1) * 512], start=True,
                                 stop=True).then_inc(z_ready, 1)

            def scores(n):
                u = n % 2
                pe.wait_ge(staged, n + 1)
                if n >= 1:
                    pe.wait_ge(kdT_ready, n)
                    pe.wait_ge(masked, n)
                for p in range(2):
                    nc.tensor.transpose(banks[0][:, p * P:(p + 1) * P], st[:, u, KL, p, :], ident[:])
                for i, (key, query) in enumerate(((KD_, QD), (QO, QO))):
                    for p in range(2):
                        for odd in range(2):
                            r = 64 * odd
                            last = nc.tensor.matmul(banks[1 + odd][:, (2 * i + p) * P:(2 * i + p + 1) * P],
                                                    st[r:r + 64, u, key, p, :], st[r:r + 64, u, query, p, :],
                                                    start=True, stop=True)
                last.then_inc(scores_ready, 1)

            def outputs(n):
                u = n % 2
                pe.wait_ge(masked, n + 1)
                pe.wait_ge(state_ready, n + 1)
                if n >= 2:
                    pe.wait_ge(normed, n - 1)
                for h in range(HG):
                    r, p = 64 * (h % 2), h // 2
                    o = out_bank(u, h % 2)[:, p * P:(p + 1) * P]
                    nc.tensor.matmul(o, sc[:, u, h % 2, p, :], gv[:, n, h * P:(h + 1) * P], start=True,
                                     stop=False)
                    last = nc.tensor.matmul(o, st[r:r + 64, u, QI, p, :], state[r:r + 64, p, :],
                                            start=False, stop=True)
                last.then_inc(o_ready, 1)
                pe.wait_ge(kdT_ready, n + 1)
                for p in range(2):
                    last = nc.tensor.matmul(banks[6][:, p * 256:(p + 1) * 256], kdT[:, u, p, :],
                                            gv[:, n, p * 256:(p + 1) * 256], start=True, stop=True)
                last.then_inc(ds_ready, 1)

            scores(0)
            for n in range(T):
                if n + 1 < T:
                    scores(n + 1)
                outputs(n)

        @block.scalar
        def _(act):
            act.wait_ge(ba_in[0], 16)
            act.wait_ge(ba_in[1], 16)
            for g in range(4):
                act.wait_ge(z_ready, g + 1)
                nc.scalar.activation(absz[:, g // 2, (g % 2) * 512:(g % 2 + 1) * 512], banks[g][:], ACT.Abs,
                                     bias=ba[:, g // 2:g // 2 + 1]).then_inc(abs_ready, 1)
            for p in range(2):
                act.wait_ge(abs_ready, 2 * p + 2)
                nc.scalar.activation(absz[:, p, :], absz[:, p, :], ACT.Exp, scale=-1.0).then_inc(log_step, 1)
                act.wait_ge(log_step, 2 * p + 1)
                nc.scalar.activation(absz[:, p, :], absz[:, p, :], ACT.Ln, bias=1.0).then_inc(log_step, 1)
            act.wait_ge(b_ready, 2)
            nc.scalar.activation(e_b[:], b[:], ACT.Exp, scale=1.0 / TAU).then_inc(exp_ready, 1)
            act.wait_ge(arg_ready, 1)
            flat = arg[:, 0, :].rearrange("p (j x) -> p j x", j=2)
            nc.scalar.activation(e_mid[:, 0], flat, ACT.Exp, scale=1.0 / TAU).then_inc(exp_ready, 1)
            nc.scalar.activation(e_mid[:, 1], flat, ACT.Exp, scale=-1.0 / TAU).then_inc(exp_ready, 1)
            act.wait_ge(arg_ready, 2)
            halves = arg[:, 1, :].rearrange("p (w g x) -> p w g x", g=2, x=64)
            nc.scalar.activation(halves[:, :, 0, :], halves[:, :, 0, :], ACT.Exp,
                                 scale=-1.0 / TAU).then_inc(exp_ready, 1)
            nc.scalar.activation(halves[:, :, 1, :], halves[:, :, 1, :], ACT.Exp,
                                 scale=1.0 / TAU).then_inc(exp_ready, 1)
            act.wait_ge(arg_ready, 3)
            nc.scalar.activation(arg[:, 2, :], arg[:, 2, :], ACT.Exp, scale=-1.0 / TAU).then_inc(exp_ready, 1)
            for n in range(T):
                act.wait_ge(scores_ready, n + 1)
                if n >= 2:
                    act.wait_ge(ds_ready, n - 1)
                nc.scalar.copy(kdT[:, n % 2], banks[0][:, 0:2 * P].rearrange("p (j x) -> p j x", j=2)) \
                    .then_inc(kdT_ready, 1)
                act.wait_ge(o_ready, n + 1)
                if n >= 1:
                    act.wait_ge(summed, n)
                for odd in range(2):
                    last = nc.scalar.activation(sq[:, 2 * odd:2 * odd + 2, :], out_bank(n % 2, odd)[:, 0:2 * P]
                                                .rearrange("p (h d) -> p h d", h=2), ACT.Square)
                last.then_inc(squared, 1)

        @block.vector
        def _(dve):
            dve.wait_ge(glrT_mm, 1)
            for i in range(2):
                last = nc.vector.tensor_copy(glrT[:, i * 512:(i + 1) * 512], banks[4 + i][0:GR, :])
            last.then_inc(glrT_ready, 1)
            dve.wait_ge(gain_in, 16)
            nc.vector.tensor_scalar(gain[:], gain[:], GDV ** 0.5, None, ALU.mult).then_inc(gain_ready, 1)
            nc.vector.memset(sc[:], 0.0).then_inc(masked_clear, 1)
            nc.vector.memset(state[:], 0.0).then_inc(state_ready, 1)
            dve.wait_ge(ba_in[0], 16)
            dve.wait_ge(ba_in[1], 16)
            for g in range(4):
                dve.wait_ge(abs_ready, g + 1)
                nc.vector.tensor_scalar(minz[:, g // 2, (g % 2) * 512:(g % 2 + 1) * 512], banks[g][:],
                                        ba[:, g // 2:g // 2 + 1], 0.0, ALU.add, ALU.min).then_inc(min_ready, 1)
            dve.wait_ge(filled, 2)
            for p in range(2):
                dve.wait_ge(log_step, 2 * p + 2)
                dve.wait_ge(min_ready, 2 * p + 2)
                nc.vector.tensor_tensor(minz[:, p, :], minz[:, p, :], absz[:, p, :],
                                        ALU.subtract).then_inc(sum_step, 1)
                dve.wait_ge(sum_step, p + 1)
                nc.vector.tensor_tensor_scan(b[:, p, :], keepsum[:], minz[:, p, :], 0.0, ALU.mult,
                                             ALU.add).then_inc(b_ready, 1)
            dve.wait_ge(b_ready, 2)
            bf = b[:].rearrange("p j x -> p (j x)")

            def minus(i, width, at):
                v = bf.rearrange("p (w x) -> p w x", x=width)
                return nc.vector.tensor_tensor(arg[:, i, :].rearrange("p (w x) -> p w x", x=width), v,
                                               v[:, :, at:at + 1].to_broadcast([P, 2 * SEQ // width, width]),
                                               ALU.subtract)
            minus(0, 64, 31).then_inc(sum_step, 1)
            dve.wait_ge(sum_step, 3)
            nc.vector.tensor_scalar(arg[:, 0, :], arg[:, 0, :], 40.0 * TAU, -40.0 * TAU, ALU.min,
                                    ALU.max).then_inc(arg_ready, 1)
            minus(1, P, 63).then_inc(arg_ready, 1)
            minus(2, P, 127).then_inc(arg_ready, 1)

            def stage(n):
                u = n % 2
                if n >= 2:
                    dve.wait_ge(o_ready, n - 1)
                e_off = arg[:, 1, :].rearrange("p (j x) -> p j x", j=2)[:, :, n * P:(n + 1) * P]
                e_last = arg[:, 2, :].rearrange("p (j x) -> p j x", j=2)[:, :, n * P:(n + 1) * P]
                q, k = tok(gqT, n), tok(gkT, n)

                def scaled_q(dst, src, e):
                    return nc.vector.scalar_tensor_tensor(out=dst, in0=src, scalar=GDK ** -0.5, in1=e,
                                                          op0=ALU.mult, op1=ALU.mult)
                scaled_q(st[:, u, QD], q, tok(e_mid[:, 0], n))
                nc.vector.tensor_tensor(st[:, u, KD_], k, tok(e_mid[:, 1], n), ALU.mult)
                nc.vector.tensor_tensor(st[:, u, QO, :, 0:64], k[:, :, 0:64], e_off[:, :, 0:64], ALU.mult)
                scaled_q(st[:, u, QO, :, 64:P], q[:, :, 64:P], e_off[:, :, 64:P])
                nc.vector.tensor_tensor(st[:, u, KL], k, e_last, ALU.mult)
                scaled_q(st[:, u, QI], q, tok(e_b, n)).then_inc(staged, 1)

            def mask(n):
                u = n % 2
                dve.wait_ge(scores_ready, n + 1)
                for odd in range(2):
                    v = banks[1 + odd][:].rearrange("p (i h x) -> p i h x", i=2, h=2)
                    nc.vector.tensor_copy(sc[0:64, u, odd, :, 64:P], v[0:64, 1, :, 64:P])
                    for g in (0, 64):
                        last = nc.vector.tensor_tensor(sc[g:g + 64, u, odd, :, g:g + 64],
                                                       v[g:g + 64, 0, :, g:g + 64], causal[g:g + 64, 0:2],
                                                       ALU.mult)
                last.then_inc(masked, 1)

            def carry(n):
                dve.wait_ge(o_ready, n + 1)
                dve.wait_ge(ds_ready, n + 1)
                for r in (0, 64):
                    for p in range(2):
                        last = nc.vector.scalar_tensor_tensor(
                            out=state[r:r + 64, p, :], in0=state[r:r + 64, p, :],
                            scalar=e_b[r:r + 64, p, n * P + P - 1:n * P + P],
                            in1=banks[6][r:r + 64, p * 256 + 2 * r:p * 256 + 2 * r + P],
                            op0=ALU.mult, op1=ALU.add)
                last.then_inc(state_ready, 1)

            def norm(n):
                u = n % 2
                dve.wait_ge(squared, n + 1)
                if n >= 2:
                    dve.wait_ge(rstd_ready, n - 1)
                nc.vector.tensor_reduce(ss[:, u, :], sq[:], AX.X, ALU.add).then_inc(summed, 1)
                dve.wait_ge(rstd_ready, n + 1)
                if n >= 1:
                    dve.wait_ge(gated, n)
                for odd in range(2):
                    last = nc.vector.tensor_tensor(
                        on[:, 2 * odd:2 * odd + 2, :],
                        out_bank(u, odd)[:, 0:2 * P].rearrange("p (h d) -> p h d", h=2),
                        rs[:, u, 2 * odd:2 * odd + 2].unsqueeze(2).to_broadcast([P, 2, GDV]), ALU.mult)
                last.then_inc(normed, 1)
                dve.wait_ge(normed, n + 1)
                dve.wait_ge(rgn_ready, n + 1)
                v = rgn[:, n, :].rearrange("p (h o d) -> p o h d", h=2, o=2)
                nc.vector.tensor_tensor(v, on[:].rearrange("p (o h) d -> p o h d", o=2), v,
                                        ALU.mult).then_inc(gated, 1)

            dve.wait_ge(exp_ready, 6)
            dve.wait_ge(masked_clear, 1)
            stage(0)
            for n in range(T):
                if n + 1 < T:
                    stage(n + 1)
                mask(n)
                carry(n)
                if n >= 1:
                    norm(n - 1)
            norm(T - 1)


def stage_diffattn(nc, a, s):
    with ExitStack() as c:
        sb, ps, sem = mem(nc, c, "diff")
        bias = sb("bias", [P, HD, 2 * P])
        mirror = sb("mirror", [P, HD, 2 * P])
        anti = sb("anti", [P, P])
        gain = sb("gain", [P, DDV])
        neg_lam = sb("neg_lam", [P, 1])
        nmax = sb("nmax", [P, 2, 2])
        sums = sb("sums", [P, 3, 2])
        coef = sb("coef", [P, 2, 2])
        prob = sb("prob", [P, 2, 2, SEQ])
        wt = sb("wt", [P, 2, SEQ])
        wT = sb("wT", [P, 2, T, P])
        sq = sb("sq", [P, DDV])
        ss = sb("ss", [P, 2])
        rs = sb("rs", [P, 2])
        inv = sb("inv", [P, 4])
        score = [ps(f"score{i}", [P, SEQ]) for i in range(2)]
        pt = [ps(f"pt{i}", [P, 4, P]) for i in range(2)]
        po = [ps(f"po{i}", [P, 512]) for i in range(2)]
        dqT, dkT, dv, od, ident = s["dqT"], s["dkT"], s["dv"], s["od"], s["ident"]
        bias_in, gain_in = sem("bias_in"), sem("gain_in")
        prepared, zeroed, anti_ready, turned = sem("prepared"), sem("zeroed"), sem("anti_ready"), sem("turned")
        scored = [sem("scored0"), sem("scored1")]
        biased = [sem("biased0"), sem("biased1")]
        max_ready = [sem("max_ready0"), sem("max_ready1")]
        exp_done = [sem("exp_done0"), sem("exp_done1")]
        coef_step, weighted = sem("coef_step"), sem("weighted")
        transposed, wT_ready = sem("transposed"), sem("wT_ready")
        o_ready, squared = sem("o_ready"), sem("squared")
        shifted, rooted, rstd_ready, normed = sem("shifted"), sem("rooted"), sem("rstd_ready"), sem("normed")
        block = c.enter_context(nc.Block())
        N = HD * T
        groups = [-(-(n % T + 1) // 4) for n in range(N)]
        first = [sum(groups[:n]) for n in range(N + 1)]

        @block.sync
        def _(sp):
            sp.dma_start(gain[:], a["diff_subln_g"].to_broadcast([P, DDV])).then_inc(gain_in, 16)
            for h in range(HD):
                sp.dma_start(mirror[:, h, :], bass.AP(s["rel_dram"].tensor, h * REL + 1,
                                                      [[1, P], [1, 2 * P]])).then_inc(bias_in, 16)

        @block.tensor
        def _(pe):
            def scores(n):
                h, t = n // T, n % T
                for comp in range(2):
                    r = 64 * comp
                    if n >= 1:
                        pe.wait_ge(exp_done[comp], n)
                    for k0 in range(0, (t + 1) * P, 512):
                        k1 = min(k0 + 512, (t + 1) * P)
                        last = nc.tensor.matmul(score[comp][:, k0:k1], dqT[r:r + 64, h, t * P:(t + 1) * P],
                                                dkT[r:r + 64, h, k0:k1], start=True, stop=True)
                    last.then_inc(scored[comp], 1)

            def transposes(n):
                pe.wait_ge(weighted, n + 1)
                for g in range(groups[n]):
                    i = first[n] + g
                    if i >= 2:
                        pe.wait_ge(wT_ready, i - 1)
                    for j in range(4 * g, min(4 * g + 4, n % T + 1)):
                        last = nc.tensor.transpose(pt[i % 2][:, j % 4, :], wt[:, n % 2, j * P:(j + 1) * P],
                                                   ident[:])
                    last.then_inc(transposed, 1)

            def values(n):
                h, t = n // T, n % T
                pe.wait_ge(wT_ready, first[n + 1])
                if n == 0:
                    pe.wait_ge(prepared, 4)
                if n >= 2:
                    pe.wait_ge(normed, n - 1)
                for j in range(t + 1):
                    last = nc.tensor.matmul(po[n % 2][:, 0:DDV], wT[:, n % 2, j, :],
                                            dv[:, j, h * DDV:(h + 1) * DDV], start=(j == 0), stop=(j == t))
                last.then_inc(o_ready, 1)

            pe.wait_ge(bias_in, 16 * HD)
            pe.wait_ge(anti_ready, 1)
            for h in range(HD):
                last = nc.tensor.matmul(po[h // 2][:, (h % 2) * 256:(h % 2) * 256 + 256], anti[:],
                                        mirror[:, h, :], start=True, stop=True)
            last.then_inc(turned, 1)

            for n in range(N + 3):
                if n < N:
                    scores(n)
                if 2 <= n <= N + 1:
                    transposes(n - 2)
                if n >= 3:
                    values(n - 3)

        @block.scalar
        def _(act):
            def exps(n):
                nk = (n % T + 1) * P
                for comp in range(2):
                    act.wait_ge(max_ready[comp], n + 1)
                    if n >= 2:
                        act.wait_ge(weighted, n - 1)
                    nc.scalar.activation(prob[:, n % 2, comp, 0:nk], score[comp][:, 0:nk], ACT.Exp,
                                         bias=nmax[:, n % 2, comp:comp + 1],
                                         accum_out=sums[:, n % 3, comp:comp + 1]).then_inc(exp_done[comp], 1)

            def copies(n):
                for g in range(groups[n]):
                    w = min(4, n % T + 1 - 4 * g)
                    act.wait_ge(transposed, first[n] + g + 1)
                    if n >= 2 and g == 0:
                        act.wait_ge(o_ready, n - 1)
                    nc.scalar.copy(wT[:, n % 2, 4 * g:4 * g + w, :],
                                   pt[(first[n] + g) % 2][:, 0:w, :]).then_inc(wT_ready, 1)

            def square(n):
                act.wait_ge(o_ready, n + 1)
                if n >= 1:
                    act.wait_ge(squared, n)
                if n >= 2:
                    act.wait_ge(shifted, n - 1)
                nc.scalar.activation(sq[:], po[n % 2][:, 0:DDV], ACT.Square, scale=inv[:, n % 4:n % 4 + 1],
                                     accum_out=ss[:, n % 2:n % 2 + 1]).then_inc(squared, 1)

            for n in range(N + 3):
                if n < N:
                    exps(n)
                if 2 <= n <= N + 1:
                    copies(n - 2)
                if n >= 3:
                    square(n - 3)

        @block.gpsimd
        def _(pool):
            nc.gpsimd.memset(anti[:], 0.0).then_inc(zeroed, 1)
            pool.wait_ge(zeroed, 1)
            nc.gpsimd.affine_select(out=anti[:], in_=anti[:], compare_op=ALU.not_equal, fill=1.0,
                                    base=-(P - 1), pattern=[[1, P]], channel_multiplier=1).then_inc(anti_ready, 1)
            for n in range(N):
                i = n % 2
                pool.wait_ge(squared, n + 1)
                if n >= 2:
                    pool.wait_ge(normed, n - 1)
                nc.gpsimd.tensor_scalar(rs[:, i:i + 1], ss[:, i:i + 1], EPS * DDV, None,
                                        ALU.add).then_inc(shifted, 1)
                pool.wait_ge(shifted, n + 1)
                nc.gpsimd.tensor_tensor(rs[:, i:i + 1], rs[:, i:i + 1], s["minus_half"][:, 0:1],
                                        ALU.pow).then_inc(rooted, 1)
                pool.wait_ge(rooted, n + 1)
                nc.gpsimd.tensor_tensor(rs[:, i:i + 1], rs[:, i:i + 1], inv[:, n % 4:n % 4 + 1],
                                        ALU.mult).then_inc(rstd_ready, 1)

        @block.vector
        def _(dve):
            dve.wait_ge(gain_in, 16)
            nc.vector.tensor_scalar(gain[:], gain[:], (1.0 - LAMBDA_INIT) * DDV ** 0.5, None,
                                    ALU.mult).then_inc(prepared, 1)
            nc.vector.tensor_scalar(neg_lam[:], s["lam"][:], -1.0, None, ALU.mult).then_inc(prepared, 1)
            dve.wait_ge(turned, 1)
            for i in range(2):
                nc.vector.tensor_copy(bias[:, 2 * i:2 * i + 2, :], po[i][:].rearrange(
                    "p (h x) -> p h x", h=2)).then_inc(prepared, 1)
            dve.wait_ge(prepared, 4)

            def maxima(n):
                h, nk = n // T, (n % T + 1) * P
                w = min(nk, 2 * P)
                for comp in range(2):
                    dve.wait_ge(scored[comp], n + 1)
                    near = score[comp][:, nk - w:nk]
                    nc.vector.tensor_tensor(near, near, bias[:, h, 2 * P - w:2 * P],
                                            ALU.add).then_inc(biased[comp], 1)
                for comp in range(2):
                    dve.wait_ge(biased[comp], n + 1)
                    nc.vector.tensor_reduce(nmax[:, n % 2, comp:comp + 1], score[comp][:, 0:nk], AX.X, ALU.max,
                                            negate=True).then_inc(max_ready[comp], 1)

            def weights(n):
                nk, i = (n % T + 1) * P, n % 2
                dve.wait_ge(exp_done[0], n + 1)
                dve.wait_ge(exp_done[1], n + 1)
                if n >= 4:
                    dve.wait_ge(rstd_ready, n - 3)
                nc.vector.reciprocal(inv[:, n % 4:n % 4 + 1], sums[:, n % 3, 0:1])
                nc.vector.reciprocal(coef[:, i, 0:1], sums[:, n % 3, 1:2]).then_inc(coef_step, 1)
                dve.wait_ge(coef_step, 2 * n + 1)
                nc.vector.tensor_scalar(coef[:, i, 1:2], coef[:, i, 0:1], sums[:, n % 3, 0:1], neg_lam[:],
                                        ALU.mult, ALU.mult).then_inc(coef_step, 1)
                dve.wait_ge(coef_step, 2 * n + 2)
                if n >= 2:
                    dve.wait_ge(transposed, first[n - 1])
                nc.vector.scalar_tensor_tensor(out=wt[:, i, 0:nk], in0=prob[:, i, 1, 0:nk],
                                               scalar=coef[:, i, 1:2], in1=prob[:, i, 0, 0:nk],
                                               op0=ALU.mult, op1=ALU.add).then_inc(weighted, 1)

            def norm(n):
                h, t = n // T, n % T
                dve.wait_ge(rstd_ready, n + 1)
                nc.vector.scalar_tensor_tensor(out=od[:, t, h * DDV:(h + 1) * DDV], in0=po[n % 2][:, 0:DDV],
                                               scalar=rs[:, n % 2:n % 2 + 1], in1=gain[:], op0=ALU.mult,
                                               op1=ALU.mult).then_inc(normed, 1)

            for n in range(N + 4):
                if n < N:
                    maxima(n)
                if 1 <= n <= N:
                    weights(n - 1)
                if n >= 4:
                    norm(n - 4)


def stage_outproj(nc, a, s):
    with ExitStack() as c:
        sb, ps, sem = mem(nc, c, "outproj")
        x = sb("x", [P, 2, D])
        g2 = sb("g2", [P, D])
        xn = sb("xn", [P, 2, D])
        h = sb("h", [P, 2, D], kib=192)
        oh = sb("o_high", [P, 2, KD, P], F32R)
        ol = sb("o_low", [P, 2, KD, P], F32R)
        sq = sb("sq", [P, D])
        raw = [sb("w_raw0", [P, KD, CW]), sb("w_raw1", [P, KD, CW], kib=181)]
        xnT = sb("xnT", [P, KD, 512], kib=84)
        wh = sb("w_high", [P, KD, D], F32R, kib=117)
        wl = sb("w_low", [P, KD, D], F32R, kib=149)
        wr = sb("w_router", [P, KD, NG + NE], kib=189)
        br = sb("b_router", [P, NG + NE], kib=190.5)
        ss = sb("ss", [P, T], kib=190.75)
        rs = sb("rs", [P, T], kib=190.8125)
        lT = sb("lT", [NG + NE, 512], kib=100)
        ident = s["ident"]
        pt = [ps(f"pt{i}", [P, 4, P]) for i in range(2)]
        po = [ps(f"po{i}", [P, 512]) for i in range(4)]
        pr = ps("pr", [P, 512])
        pl = ps("pl", [P, T, NG + NE])
        x_in = [sem("x_in0"), sem("x_in1")]
        g2_in = sem("g2_in")
        router_in = [sem(f"router_in{i}") for i in range(4)]
        raw_in = [sem("raw_in0"), sem("raw_in1")]
        w_high, w_low = sem("w_high_ready"), sem("w_low_ready")
        transposed, o_high, o_low = sem("transposed"), sem("o_high_ready"), sem("o_low_ready")
        xn_stored = sem("xn_stored")
        product, added = sem("product"), sem("added")
        squared, shifted, rstd_ready = sem("squared"), sem("shifted"), sem("rstd_ready")
        gain_ready, normed = sem("gain_ready"), sem("normed")
        xn_out = [sem("xn_out0"), sem("xn_out1")]
        logits_mm, lT_ready, logits_t = sem("logits_mm"), sem("lT_ready"), sem("logits_t")
        block = c.enter_context(nc.Block())
        x_rows = a["x"].rearrange("b (t p) d -> (b t) p d", p=P)
        xn_rows = s["xn2_dram"].rearrange("(t p) d -> t p d", p=P)
        h_rows = s["sum_dram"].rearrange("(t p) d -> t p d", p=P)
        h_out = [sem("h_out0"), sem("h_out1")]
        spare_out = sem("spare_out")
        order = [("o", 0)]
        for t in range(T):
            order += ([("o", t + 1)] if t + 1 < T else []) + ([("x", t - 1)] if t >= 1 else [])
        order += [("x", T - 1)]
        place = {what: i for i, what in enumerate(order)}

        @block.sync
        def _(sp):
            for i in range(4):
                if i >= 2:
                    sp.wait_ge(w_low, i - 1)
                sp.dma_start(raw[i % 2][:], a["w_out"][0, :, i * CW:(i + 1) * CW].rearrange(
                    "(k p) c -> p k c", p=P)).then_inc(raw_in[i % 2], 16)
            for t in range(2):
                sp.dma_start(x[:, t, :], x_rows[t]).then_inc(x_in[t], 16)
            sp.dma_start(g2[:], a["norm2_g"].to_broadcast([P, D])).then_inc(g2_in, 16)
            for i, (dst, src) in enumerate((
                    (wr[:, :, 0:NG], a["moe_wg"][0].rearrange("(p k) e -> p k e", p=P)),
                    (wr[:, :, NG:], a["moe_we"][0].rearrange("(p k) e -> p k e", p=P)),
                    (br[:, 0:NG], a["moe_bg"].to_broadcast([P, NG])),
                    (br[:, NG:], a["moe_be"].to_broadcast([P, NE])))):
                sp.dma_start(dst, src).then_inc(router_in[i], 16)
            sp.dma_start(h_rows[T], x_rows[0]).then_inc(spare_out, 16)
            for t in range(T):
                sp.wait_ge(added, 2 * t + 2)
                sp.dma_start(h_rows[t], h[:, t % 2, :]).then_inc(h_out[t % 2], 16)
                sp.wait_ge(normed, t + 1)
                sp.dma_start(xn_rows[t], xn[:, t % 2, :]).then_inc(xn_out[t % 2], 16)
                if t + 2 < T:
                    sp.dma_start(x[:, t % 2, :], x_rows[t + 2]).then_inc(x_in[t % 2], 16)
            for i in range(2):
                sp.wait_ge(xn_out[i], 16 * (T // 2))
                sp.wait_ge(h_out[i], 16 * (T // 2))
            sp.wait_ge(spare_out, 16)

        @block.tensor
        def _(pe):
            def transposes(kind, t):
                if (kind, t) not in place:
                    return
                i = place[kind, t]
                pe.wait_ge(normed, t + 1) if kind == "x" else None
                for g in range(2):
                    if i >= 1:
                        before = order[:i]
                        pe.wait_ge(o_low, 2 * sum(k == "o" for k, _ in before) - (1 - g)
                                   ) if before[-1][0] == "o" else pe.wait_ge(
                            xn_stored, 2 * sum(k == "x" for k, _ in before) - (1 - g))
                    for j in range(4):
                        if kind == "o":
                            src = (s["rg"] if g == 0 else s["od"])[:, t, j * P:(j + 1) * P]
                        else:
                            src = xn[:, t % 2, :].rearrange("p (c k) -> p k c", k=KD)[:, 4 * g + j, :]
                        last = nc.tensor.transpose(pt[g][:, j, :], src, ident[:])
                    last.then_inc(transposed, 1)

            def products(t):
                for half in range(2):
                    n = 2 * t + half
                    if t == 0:
                        pe.wait_ge(w_low, 2 * half + 2)
                    if n >= 4:
                        pe.wait_ge(added, n - 3)
                    if half == 0:
                        pe.wait_ge(o_low, 2 * t + 2)
                    for k in range(KD):
                        hi, lo = oh[:, t % 2, k, :], ol[:, t % 2, k, :]
                        w_hi, w_lo = wh[:, k, half * 512:half * 512 + 512], wl[:, k, half * 512:half * 512 + 512]
                        nc.tensor.matmul(po[n % 4][:], hi, w_hi, start=(k == 0), stop=False)
                        nc.tensor.matmul(po[n % 4][:], hi, w_lo, start=False, stop=False)
                        last = nc.tensor.matmul(po[n % 4][:], lo, w_hi, start=False, stop=(k == KD - 1))
                    last.then_inc(product, 1)

            def router(half):
                pe.wait_ge(xn_stored, 8 * (half + 1))
                if half == 0:
                    pe.wait_ge(router_in[0], 16)
                    pe.wait_ge(router_in[1], 16)
                else:
                    pe.wait_ge(lT_ready, 1)
                for k in range(KD):
                    last = nc.tensor.matmul(pr[0:NG + NE, :], wr[:, k, :], xnT[:, k, :], start=(k == 0),
                                            stop=(k == KD - 1))
                last.then_inc(logits_mm, 1)
                pe.wait_ge(lT_ready, half + 1)
                for j in range(4):
                    last = nc.tensor.transpose(pl[:, 4 * half + j, :], lT[:, j * P:(j + 1) * P],
                                               ident[0:NG + NE, 0:NG + NE])
                last.then_inc(logits_t, 1)

            transposes("o", 0)
            for t in range(T):
                transposes("o", t + 1)
                products(t)
                transposes("x", t - 1)
                if t == 4:
                    router(0)
            transposes("x", T - 1)
            router(1)

        @block.scalar
        def _(act):
            def w_split(i):
                act.wait_ge(raw_in[i % 2], 16 * (i // 2 + 1))
                nc.scalar.copy(wh[:, :, i * CW:(i + 1) * CW], raw[i % 2][:]).then_inc(w_high, 1)

            def take(kind, t):
                i = place[kind, t]
                for g in range(2):
                    act.wait_ge(transposed, 2 * i + g + 1)
                    if kind == "o":
                        if t >= 2 and g == 0:
                            act.wait_ge(product, 2 * (t - 1))
                        nc.scalar.copy(oh[:, t % 2, 4 * g:4 * g + 4, :], pt[g][:]).then_inc(o_high, 1)
                    else:
                        if t >= 4 and g == 0:
                            act.wait_ge(logits_mm, 1)
                        nc.scalar.copy(xnT[:, 4 * g:4 * g + 4, (t % 4) * P:(t % 4 + 1) * P],
                                       pt[g][:]).then_inc(xn_stored, 1)

            def square(t):
                act.wait_ge(added, 2 * t + 2)
                if t >= 1:
                    act.wait_ge(squared, t)
                nc.scalar.activation(sq[:], h[:, t % 2, :], ACT.Square,
                                     accum_out=ss[:, t:t + 1]).then_inc(squared, 1)

            take("o", 0)
            for i in range(4):
                w_split(i)
            for t in range(T):
                if t + 1 < T:
                    take("o", t + 1)
                if t >= 1:
                    take("x", t - 1)
                square(t)
            take("x", T - 1)

        @block.gpsimd
        def _(pool):
            for t in range(T):
                pool.wait_ge(squared, t + 1)
                nc.gpsimd.tensor_scalar(rs[:, t:t + 1], ss[:, t:t + 1], EPS * D, None,
                                        ALU.add).then_inc(shifted, 1)
                pool.wait_ge(shifted, t + 1)
                nc.gpsimd.tensor_tensor(rs[:, t:t + 1], rs[:, t:t + 1], s["minus_half"][:, 0:1],
                                        ALU.pow).then_inc(rstd_ready, 1)

        @block.vector
        def _(dve):
            def low(t):
                for g in range(2):
                    dve.wait_ge(o_high, 2 * t + g + 1)
                    nc.vector.tensor_tensor(ol[:, t % 2, 4 * g:4 * g + 4, :], pt[g][:],
                                            oh[:, t % 2, 4 * g:4 * g + 4, :].bitcast(F32),
                                            ALU.subtract).then_inc(o_low, 1)

            def add(t):
                dve.wait_ge(x_in[t % 2], 16 * (t // 2 + 1))
                for half in range(2):
                    n = 2 * t + half
                    dve.wait_ge(product, n + 1)
                    if t >= 2 and half == 0:
                        dve.wait_ge(h_out[t % 2], 16 * (t // 2))
                        dve.wait_ge(normed, t - 1)
                    nc.vector.tensor_tensor(h[:, t % 2, half * 512:half * 512 + 512], po[n % 4][:],
                                            x[:, t % 2, half * 512:half * 512 + 512], ALU.add).then_inc(added, 1)

            def norm(t):
                dve.wait_ge(rstd_ready, t + 1)
                if t >= 2:
                    dve.wait_ge(xn_out[t % 2], 16 * (t // 2))
                    dve.wait_ge(transposed, 2 * place["x", t - 2] + 2)
                nc.vector.scalar_tensor_tensor(out=xn[:, t % 2, :], in0=h[:, t % 2, :], scalar=rs[:, t:t + 1],
                                               in1=g2[:], op0=ALU.mult, op1=ALU.mult).then_inc(normed, 1)

            def logits(half):
                dve.wait_ge(logits_mm, half + 1)
                if half == 1:
                    dve.wait_ge(logits_t, 1)
                nc.vector.tensor_copy(lT[:], pr[0:NG + NE, :]).then_inc(lT_ready, 1)
                dve.wait_ge(logits_t, half + 1)
                nc.vector.tensor_tensor(s["logits"][:, 4 * half:4 * half + 4, :],
                                        pl[:, 4 * half:4 * half + 4, :],
                                        br[:].unsqueeze(1).to_broadcast([P, 4, NG + NE]), ALU.add)

            low(0)
            for i in range(4):
                dve.wait_ge(w_high, i + 1)
                nc.vector.tensor_tensor(wl[:, :, i * CW:(i + 1) * CW], raw[i % 2][:],
                                        wh[:, :, i * CW:(i + 1) * CW].bitcast(F32), ALU.subtract).then_inc(w_low, 1)
            dve.wait_ge(g2_in, 16)
            nc.vector.tensor_scalar(g2[:], g2[:], D ** 0.5, None, ALU.mult).then_inc(gain_ready, 1)
            dve.wait_ge(gain_ready, 1)
            dve.wait_ge(router_in[2], 16)
            dve.wait_ge(router_in[3], 16)
            for t in range(T):
                if t + 1 < T:
                    low(t + 1)
                add(t)
                norm(t)
                if t == 4:
                    logits(0)
            logits(1)


def stage_route(nc, a, s):
    with ExitStack() as c:
        sb, ps, sem = mem(nc, c, "route")
        gmax = sb("gmax", [P, T, 1])
        gexp = sb("gexp", [P, T, NG])
        gw = sb("gw", [P, T, 1])
        first = sb("first", [P, T, NG])
        taken = sb("taken", [P, T, 1])
        le = sb("le", [P, T, NG, EPG])
        top = sb("top", [P, T, 8])
        top_at = sb("top_at", [P, T, 8], U32)
        at = sb("at", [P, T, 2])
        e2 = sb("e2", [P, T, 1])
        w = sb("w", [P, T, 2])
        one = sb("one", [P, 2, T, NE])
        member = sb("member", [P, T, NE], BF16)
        weight = sb("weight", [P, T, NE])
        weight2 = sb("weight2", [P, T, NE])
        part = sb("part", [P, T, NE], BF16)
        iota_e = sb("iota_e", [P, NE])
        iota_t = sb("iota_t", [P, T])
        iota_p = sb("iota_p", [P, 1])
        before = sb("before", [P, P], BF16)
        ones = sb("ones", [P, P], BF16)
        plus1 = sb("plus1", [P, T, NE])
        pp = ps("pp", [P, T, NE])
        pc = ps("pc", [P, NE])
        logits, rows, place, counts = s["logits"], s["slot_rows"], s["place"], s["counts"]
        made, before_ready = sem("made"), sem("before_ready")
        step, gshift, gexp_ready = sem("step"), sem("gshift"), sem("gexp_ready")
        dshift, e2_ready = sem("dshift"), sem("e2_ready")
        member_ready, counted = sem("member_ready"), sem("counted")
        block = c.enter_context(nc.Block())

        @block.gpsimd
        def _(pool):
            nc.gpsimd.memset(ones[:], 1.0).then_inc(made, 1)
            nc.gpsimd.memset(before[:], 1.0).then_inc(made, 1)
            pool.wait_ge(made, 2)
            nc.gpsimd.affine_select(out=before[:], in_=before[:], compare_op=ALU.is_gt, fill=0.0, base=0,
                                    pattern=[[1, P]], channel_multiplier=-1).then_inc(before_ready, 1)
            for dst, pattern, mult in ((iota_e, [[1, NE]], 0), (iota_t, [[1, T]], 0), (iota_p, [[0, 1]], 1),
                                       (s["iota_slot"], [[1, CAP]], 0)):
                nc.gpsimd.iota(dst[:], pattern=pattern, base=0, channel_multiplier=mult,
                               allow_small_or_imprecise_dtypes=True).then_inc(made, 1)

        @block.tensor
        def _(pe):
            pe.wait_ge(before_ready, 1)
            pe.wait_ge(member_ready, 1)
            for t in range(T):
                nc.tensor.matmul(pp[:, t, :], before[:], member[:, t, :], start=True, stop=(t == 0))
                for earlier in range(t):
                    nc.tensor.matmul(pp[:, t, :], ones[:], member[:, earlier, :], start=False,
                                     stop=(earlier == t - 1))
            for t in range(T):
                last = nc.tensor.matmul(pc[:], ones[:], member[:, t, :], start=(t == 0), stop=(t == T - 1))
            last.then_inc(counted, 1)

        @block.scalar
        def _(act):
            act.wait_ge(gshift, 1)
            nc.scalar.activation(gexp[:], gexp[:], ACT.Exp).then_inc(gexp_ready, 1)
            act.wait_ge(dshift, 1)
            nc.scalar.activation(e2[:], e2[:], ACT.Exp).then_inc(e2_ready, 1)

        @block.vector
        def _(dve):
            n = [0]

            def then(ins):
                n[0] += 1
                ins.then_inc(step, 1)
                dve.wait_ge(step, n[0])

            V = nc.vector
            lg = logits[:, :, 0:NG]
            then(V.tensor_reduce(gmax[:], lg, AX.X, ALU.max))
            V.tensor_tensor(gexp[:], lg, gmax[:].to_broadcast([P, T, NG]), ALU.subtract).then_inc(gshift, 1)
            then(V.tensor_tensor(first[:], lg, gmax[:].to_broadcast([P, T, NG]), ALU.is_equal))
            then(V.tensor_copy(taken[:], first[:, :, 0:1]))
            for j in range(1, NG):
                then(V.tensor_tensor(first[:, :, j:j + 1], first[:, :, j:j + 1], taken[:], ALU.is_gt))
                then(V.tensor_tensor(taken[:], taken[:], first[:, :, j:j + 1], ALU.max))
            then(V.tensor_scalar(first[:], first[:], -1.0, -NEG, ALU.add, ALU.mult))
            then(V.tensor_tensor(le[:], logits[:, :, NG:].rearrange("p t (g e) -> p t g e", g=NG),
                                 first[:].unsqueeze(3).to_broadcast([P, T, NG, EPG]), ALU.add))
            for t in range(T):
                last = V.max(top[:, t, :], le[:, t].rearrange("p g e -> p (g e)"))
            then(last)
            for t in range(T):
                last = V.max_index(top_at[:, t, :], top[:, t, :], le[:, t].rearrange("p g e -> p (g e)"))
            V.tensor_tensor(e2[:], top[:, :, 1:2], top[:, :, 0:1], ALU.subtract).then_inc(dshift, 1)
            then(last)
            then(V.tensor_copy(at[:], top_at[:, :, 0:2]))
            dve.wait_ge(made, 6)
            for k in range(2):
                last = V.tensor_tensor(one[:, k], iota_e[:].unsqueeze(1).to_broadcast([P, T, NE]),
                                       at[:, :, k:k + 1].to_broadcast([P, T, NE]), ALU.is_equal)
            then(last)
            V.tensor_tensor(member[:], one[:, 0], one[:, 1], ALU.add).then_inc(member_ready, 1)
            dve.wait_ge(gexp_ready, 1)
            then(V.tensor_reduce(gw[:], gexp[:], AX.X, ALU.add))
            then(V.reciprocal(gw[:], gw[:]))
            dve.wait_ge(e2_ready, 1)
            then(V.tensor_scalar(w[:, :, 1:2], e2[:], 1.0, None, ALU.add))
            then(V.reciprocal(w[:, :, 0:1], w[:, :, 1:2]))
            then(V.tensor_tensor(w[:, :, 0:1], w[:, :, 0:1], gw[:], ALU.mult))
            then(V.tensor_tensor(w[:, :, 1:2], w[:, :, 0:1], e2[:], ALU.mult))
            then(V.tensor_tensor(weight[:], one[:, 0], w[:, :, 0:1].to_broadcast([P, T, NE]), ALU.mult))
            then(V.tensor_tensor(weight2[:], one[:, 1], w[:, :, 1:2].to_broadcast([P, T, NE]), ALU.mult))
            then(V.tensor_tensor(weight[:], weight[:], weight2[:], ALU.add))
            for k in range(3):
                then(V.tensor_copy(part[:], weight[:]))
                then(V.tensor_copy(rows[:, :, :, 3 + k], part[:]))
                if k < 2:
                    then(V.tensor_tensor(weight[:], weight[:], part[:], ALU.subtract))
            V.tensor_copy(rows[:, :, :, 0], iota_t[:].unsqueeze(2).to_broadcast([P, T, NE]))
            V.tensor_copy(rows[:, :, :, 1], iota_p[:].unsqueeze(2).to_broadcast([P, T, NE]))
            V.memset(rows[:, :, :, 2], 1.0)
            dve.wait_ge(counted, 1)
            dve.wait_ge(member_ready, 1)
            then(V.scalar_tensor_tensor(out=plus1[:].rearrange("p t e -> p (t e)"),
                                        in0=pp[:].rearrange("p t e -> p (t e)"), scalar=1.0,
                                        in1=member[:].rearrange("p t e -> p (t e)"), op0=ALU.add, op1=ALU.mult))
            V.tensor_scalar(place[:].rearrange("p e t -> p t e"), plus1[:], -1.0, None, ALU.add)
            V.tensor_copy(counts[:, 0:NE], pc[0:1, :])
            V.tensor_reduce(counts[:, NE:NE + 1], pc[0:1, :], AX.X, ALU.max)


def stage_experts(nc, a, s):
    with ExitStack() as c:
        sb, ps, sem = mem(nc, c, "experts")
        raw = sb("w_raw", [P, CHUNKS_E, WC])
        wh = [sb(f"w_high{i}", [P, WC], F32R) for i in range(3)]
        wl = [sb(f"w_low{i}", [P, WC], F32R) for i in range(3)]
        onehot = [sb(f"onehot{u}", [P, T, CAP], BF16) for u in range(2)]
        row = [sb(f"row{u}", [P, NROUTE]) for u in range(2)]
        tmp = [sb(f"tmp{u}", [P, 4]) for u in range(2)]
        token = [sb(f"token{u}", [P, 1], U32) for u in range(2)]
        dest = [sb(f"dest{u}", [P, 1], U32) for u in range(4)]
        wrow = [sb(f"wrow{u}", [P, 1]) for u in range(4)]
        xg = [sb(f"xg{u}", [P, D]) for u in range(2)]
        xTh = [sb(f"xT_high{u}", [P, KD, CAP], F32R) for u in range(2)]
        xTl = [sb(f"xT_low{u}", [P, KD, CAP], F32R) for u in range(2)]
        sl = sb("sl", [P, DE])
        hd = sb("hd", [P, DE])
        hTh = sb("hT_high", [P, KE, CAP], F32R)
        hTl = sb("hT_low", [P, KE, CAP], F32R)
        y = [sb(f"y{u}", [P, D]) for u in range(2)]
        o_xT_all, o_hT_all = sb("o_xT", [P, KD, CAP]), sb("o_hT", [P, KE, CAP])
        shifted_place = sb("shifted_place", [P, T])
        list_start = sb("list_start", [P, SEQ // CAP - 1])
        pid = ps("pid", [P, NROUTE])
        px = [ps(f"px{g}", [P, 4, CAP]) for g in range(2)]
        ph = [ps(f"ph{m}", [P, DE]) for m in range(2)]
        pt = ps("pt", [P, KE, CAP])
        py = [ps(f"py{g}", [P, 512]) for g in range(2)]
        ident, rows, place, counts, iota = s["ident"], s["slot_rows"], s["place"], s["counts"], s["iota_slot"]
        spare_row = sb("spare_row", [P, 1])

        class Sems:
            def __init__(self, k):
                self.onehot = sem(f"onehot_ready{k}")
                self.ids_mm = sem(f"ids_mm{k}")
                self.row_step = sem(f"row_step{k}")
                self.ids = sem(f"ids_ready{k}")
                self.passed = sem(f"pool_passed{k}")
                self.xg_in = [sem(f"xg_in{k}{u}") for u in range(2)]
                self.x_mm = sem(f"x_transposed{k}")
                self.silu = sem(f"silu_ready{k}")
                self.hd = sem(f"hidden_ready{k}")
                self.h_mm = sem(f"hidden_transposed{k}")
                self.y_ready = sem(f"y_ready{k}")
                self.y_out = [sem(f"y_out{k}{u}") for u in range(2)]

        def view_w(name, e):
            w = a[name][0]
            return w[bass.ds(e, 1)].rearrange("a (p k) f -> (a p) k f", k=KE if name == "moe_w2" else KD)

        def pick(q, e, n, u, src=None):
            places = place[:, bass.ds(e, 1), :].rearrange("p a t -> p (a t)") if src is None else src
            nc.vector.tensor_tensor(onehot[u][:], iota[:].unsqueeze(1).to_broadcast([P, T, CAP]),
                                    places.unsqueeze(2).to_broadcast([P, T, CAP]),
                                    ALU.is_equal).then_inc(q.onehot, 1)

        def ids_mm(pe, q, e, n, u):
            pe.wait_ge(q.onehot, n + 1)
            for t in range(T):
                last = nc.tensor.matmul(pid[:], onehot[u][:, t, :],
                                        rows[:, t, bass.ds(e, 1), :].rearrange("p a r -> p (a r)"),
                                        start=(t == 0), stop=(t == T - 1))
            last.then_inc(q.ids_mm, 1)

        def ids(dve, q, n, u, v):
            V = nc.vector
            dve.wait_ge(q.ids_mm, n + 1)
            V.tensor_copy(row[u][:], pid[:]).then_inc(q.row_step, 1)
            dve.wait_ge(q.row_step, 4 * n + 1)
            V.scalar_tensor_tensor(out=token[u][:], in0=row[u][:, 0:1], scalar=float(P), in1=row[u][:, 1:2],
                                   op0=ALU.mult, op1=ALU.add)
            V.scalar_tensor_tensor(out=tmp[u][:, 0:1], in0=row[u][:, 0:1], scalar=float(P),
                                   in1=row[u][:, 1:2], op0=ALU.mult, op1=ALU.add).then_inc(q.row_step, 1)
            V.tensor_tensor(tmp[u][:, 1:2], row[u][:, 3:4], row[u][:, 4:5], ALU.add).then_inc(q.row_step, 1)
            V.tensor_scalar(tmp[u][:, 2:3], row[u][:, 2:3], -1.0, 1.0, ALU.mult,
                            ALU.add).then_inc(q.row_step, 1)
            dve.wait_ge(q.row_step, 4 * n + 4)
            V.tensor_tensor(wrow[v][:], tmp[u][:, 1:2], row[u][:, 5:6], ALU.add)
            V.scalar_tensor_tensor(out=dest[v][:], in0=tmp[u][:, 2:3], scalar=spare_row[:], in1=tmp[u][:, 0:1],
                                   op0=ALU.mult, op1=ALU.add).then_inc(q.ids, 1)

        bound = {}

        def set_bounds(pool):
            bound["x"] = pool.to_reg(SEQ - 1)
            bound["y"] = pool.to_reg(SEQ + CAP - 1)

        def gather(pool, q, ids_ready, n, u):
            pool.wait_ge(ids_ready, n + 1)
            pool.sem_inc(q.passed, 1)
            nc.gpsimd.indirect_dma_start(xg[u][:], None, s["xn2_dram"],
                                         bass.IndirectOffsetOnAxis(token[u][:, 0:1], 0),
                                         bounds_check=bound["x"], oob_is_err=False).then_inc(q.xg_in[u], 16)

        def x_transposes(pe, q, n, u, arrived):
            pe.wait_ge(q.xg_in[u], arrived)
            for g in range(2):
                for j in range(4):
                    last = nc.tensor.transpose(px[g][:, j, :], xg[u][:].rearrange(
                        "p (c k) -> p k c", k=KD)[:, 4 * g + j, :], ident[:])
                last.then_inc(q.x_mm, 1)

        def h_transposes(pe, q, n):
            pe.wait_ge(q.hd, n + 1)
            for j in range(KE):
                last = nc.tensor.transpose(pt[:, j, :], hd[:].rearrange("p (c k) -> p k c", k=KE)[:, j, :],
                                           ident[:])
            last.then_inc(q.h_mm, 1)

        def scatter(pool, q, done, n, u, v):
            pool.wait_ge(done.y_ready, 2 * n + 2)
            pool.sem_inc(q.passed, 1)
            nc.gpsimd.indirect_dma_start(s["sum_dram"], bass.IndirectOffsetOnAxis(dest[v][:, 0:1], 0), y[u][:],
                                         None, bounds_check=bound["y"], oob_is_err=True,
                                         compute_op=ALU.add).then_inc(q.y_out[u], 16)

        def silu(act, q):
            nc.scalar.activation(sl[:], ph[0][:], ACT.Silu).then_inc(q.silu, 1)

        def hidden(dve, q, n):
            dve.wait_ge(q.silu, n + 1)
            nc.vector.tensor_tensor(hd[:], ph[1][:], sl[:], ALU.mult).then_inc(q.hd, 1)

        def weighted(act, q, g, u, v):
            nc.scalar.activation(y[u][:, g * 512:g * 512 + 512], py[g][:], ACT.Copy,
                                 scale=wrow[v][:, 0:1]).then_inc(q.y_ready, 1)

        def some(n, k):
            return n >= k if isinstance(n, int) else True

        q = Sems("")
        spare_made = sem("spare_made")
        raw_in = [sem(f"raw_in{c}") for c in range(CHUNKS_E)]
        w_high, w_low = sem("w_high_ready"), sem("w_low_ready")
        chunk_used = sem("chunk_used")
        xT_high, xT_low = sem("xT_high_ready"), sem("xT_low_ready")
        hT_high, hT_low = sem("hT_high_ready"), sem("hT_low_ready")

        def number(e, c):
            if isinstance(e, int) and e in (0, NE):
                return {0: 0, 1: 1, 4: 2, 5: 3}[c] if e == 0 else CHUNKS_E * NE + c - 4
            return CHUNKS_E * e + c - 2

        def chunks_of(e, tail):
            return (2, 3) if tail else (0, 1, 4, 5) if isinstance(e, int) and e == 0 else range(CHUNKS_E)

        def slot(c):
            return (c + 1) % 3

        def high(act, e, c):
            act.wait_ge(raw_in[c], 16 * e if c in (2, 3) else 16 * (e + 1))
            n = number(e, c)
            if isinstance(e, int) and e == 0:
                if c == 4:
                    act.wait_ge(chunk_used, 2)
            elif isinstance(e, int) and e == NE and c == 2:
                act.wait_ge(chunk_used, n)
            else:
                act.wait_ge(chunk_used, n - 2)
            nc.scalar.copy(wh[slot(c)][:], raw[:, c, :]).then_inc(w_high, 1)

        def low(dve, e, c):
            dve.wait_ge(w_high, number(e, c) + 1)
            nc.vector.tensor_tensor(wl[slot(c)][:], raw[:, c, :], wh[slot(c)][:].bitcast(F32),
                                    ALU.subtract).then_inc(w_low, 1)

        def sp_expert(sp, e, r, j, last, tail=False):
            for c in chunks_of(e, tail):
                if some(e, 1) and not (isinstance(e, int) and e == 1 and c in (2, 3)):
                    sp.wait_ge(w_low, number(e - 1, c) + 1)
                w = view_w(("moe_w1", "moe_w2", "moe_w3")[c // 2], e - 1 if c in (2, 3) else e)
                sp.dma_start(raw[:, c, :], w.rearrange("p (c k) f -> p c (k f)", c=2)[:, c % 2, :]) \
                    .then_inc(raw_in[c], 16)

        def product(out, x_hi, x_lo, w_hi, w_lo, start, stop):
            nc.tensor.matmul(out, x_hi, w_hi, start=start, stop=False)
            nc.tensor.matmul(out, x_hi, w_lo, start=False, stop=False)
            return nc.tensor.matmul(out, x_lo, w_hi, start=False, stop=stop)

        def gate(pe, e, c, u):
            pe.wait_ge(w_low, number(e, c) + 1)
            for k in range(KD // 2):
                w = slice(k * DE, (k + 1) * DE)
                kx = KD // 2 * (c % 2) + k
                last = product(ph[c // 4][:], xTh[u][:, kx, :], xTl[u][:, kx, :], wh[slot(c)][:, w],
                               wl[slot(c)][:, w], kx == 0, kx == KD - 1)
            last.then_inc(chunk_used, 1)

        def down(pe, e, c):
            pe.wait_ge(w_low, number(e, c) + 1)
            for k in range(KE // 2):
                kx = KE // 2 * (c % 2) + k
                for g in range(2):
                    w = slice(k * D + g * 512, k * D + g * 512 + 512)
                    last = product(py[g][:], hTh[:, kx, :], hTl[:, kx, :], wh[slot(c)][:, w], wl[slot(c)][:, w],
                                   kx == 0, kx == KE - 1)
            last.then_inc(chunk_used, 1)

        def pe_ids(pe, e, u):
            if some(e, 1):
                pe.wait_ge(q.row_step, 4 * (e - 1) + 1)
            ids_mm(pe, q, e, e, u)

        def pe_x(pe, e, r, u):
            if some(e, 1):
                pe.wait_ge(xT_low, 2 * e)
            x_transposes(pe, q, e, u, 16 * (r + 1))

        def pe_expert(pe, e, r, j, last, tail=False):
            u = j % 2
            if not tail:
                pe.wait_ge(xT_low, 2 * e + 2)
                if some(e, 1):
                    pe.wait_ge(q.silu, e)
                gate(pe, e, 0, u)
            if some(e, 1):
                h_transposes(pe, q, e - 1)
            if not tail:
                gate(pe, e, 1, u)
                if not (last and j >= 2):
                    pe_ids(pe, e + 2, u)
                if not (last and j == 3):
                    pe_x(pe, e + 1, pair(r, j, 1), 1 - u)
            if some(e, 1):
                pe.wait_ge(hT_low, e)
                if some(e, 2):
                    pe.wait_ge(q.y_ready, 2 * e - 2)
                down(pe, e, 2)
                down(pe, e, 3)
            if not tail:
                if some(e, 1):
                    pe.wait_ge(q.hd, e)
                gate(pe, e, 4, u)
                gate(pe, e, 5, u)

        def act_expert(act, e, r, j, last, tail=False):
            u = j % 2
            if some(e, 1):
                if not (tail or (isinstance(e, int) and e == 0)):
                    high(act, e, 2)
                act.wait_ge(q.h_mm, e)
                nc.scalar.copy(hTh[:], pt[:]).then_inc(hT_high, 1)
                if not tail:
                    high(act, e, 3)
            if not tail:
                act.wait_ge(chunk_used, number(e, 1) + 1)
                if some(e, 1):
                    act.wait_ge(q.hd, e)
                silu(act, q)
                high(act, e, 4)
                if not (last and j == 3):
                    act_x(act, e + 1, 1 - u)
                high(act, e, 5)
                more = (0, 1) if not (last and j == 3) else ()
            else:
                more = ()
            if more:
                high(act, e + 1, 0)
            if some(e, 1):
                act.wait_ge(chunk_used, number(e, 3) + 1)
                if some(e, 3):
                    act.wait_ge(q.y_out[1 - u], 16 * pair(r, j, -1))
                for g in range(2):
                    weighted(act, q, g, 1 - u, (j - 1) % 4)
            if more:
                high(act, e + 1, 1)
            if last and j == 3 and not tail:
                high(act, e + 1, 2)
                high(act, e + 1, 3)

        def act_x(act, e, u):
            for g in range(2):
                act.wait_ge(q.x_mm, 2 * e + g + 1)
                nc.scalar.copy(xTh[u][:, 4 * g:4 * g + 4, :], px[g][:]).then_inc(xT_high, 1)

        def dve_x(dve, e, u):
            for g in range(2):
                dve.wait_ge(xT_high, 2 * e + g + 1)
                nc.vector.tensor_tensor(xTl[u][:, 4 * g:4 * g + 4, :], px[g][:],
                                        xTh[u][:, 4 * g:4 * g + 4, :].bitcast(F32),
                                        ALU.subtract).then_inc(xT_low, 1)

        def dve_expert(dve, e, r, j, last, tail=False):
            u = j % 2
            if some(e, 1):
                dve.wait_ge(chunk_used, number(e - 1, 5) + 1)
                hidden(dve, q, e - 1)
                if not tail:
                    low(dve, e, 2)
                dve.wait_ge(hT_high, e)
                nc.vector.tensor_tensor(hTl[:], pt[:], hTh[:].bitcast(F32), ALU.subtract).then_inc(hT_low, 1)
                if not tail:
                    low(dve, e, 3)
            if tail:
                return
            low(dve, e, 4)
            if not (last and j >= 2):
                dve_ids(dve, e + 2, r + 1, (j + 2) % 4)
            if not (last and j == 3):
                dve_x(dve, e + 1, 1 - u)
            low(dve, e, 5)
            if not (last and j == 3):
                low(dve, e + 1, 0)
            if not (last and j >= 1):
                pick(q, e + 3, e + 3, 1 - u)
            if not (last and j == 3):
                low(dve, e + 1, 1)
            else:
                low(dve, e + 1, 2)
                low(dve, e + 1, 3)

        def dve_ids(dve, e, r, j):
            if some(e, 2):
                dve.wait_ge(q.xg_in[j % 2], 16 * r)
            if some(e, 4):
                dve.wait_ge(q.y_out[j % 2], 16 * (r - 1))
            ids(dve, q, e, j % 2, j)

        def pool_gather(pool, e, u):
            if some(e, 2):
                pool.wait_ge(q.x_mm, 2 * (e - 1))
            gather(pool, q, q.ids, e, u)

        def pool_expert(pool, e, r, j, last, tail=False):
            u = j % 2
            if not (tail or (last and j >= 2)):
                pool_gather(pool, e + 2, u)
            if some(e, 1):
                if some(e, 2):
                    pool.wait_ge(q.y_out[u], 16 * r)
                scatter(pool, q, q, e - 1, 1 - u, (j - 1) % 4)

        def pair(r, j, d):
            return r + (j + d) // 2 - j // 2

        def over_experts(eng, expert):
            for j in range(4):
                expert(eng, j, j // 2, j, False)
            with eng.Fori(1, NE // 4 - 1) as i:
                for j in range(4):
                    expert(eng, 4 * i + j, 2 * i + j // 2, j, False)
            for j in range(4):
                e = NE - 4 + j
                expert(eng, e, e // 2, j, True)
            expert(eng, NE, NE // 2, 0, True, tail=True)

        with ExitStack() as b:
            block = b.enter_context(nc.Block())

            @block.sync
            def _(sp):
                over_experts(sp, sp_expert)

            @block.tensor
            def _(pe):
                for e in range(2):
                    pe_ids(pe, e, e)
                pe_x(pe, 0, 0, 0)
                over_experts(pe, pe_expert)

            @block.scalar
            def _(act):
                for c in range(2):
                    high(act, 0, c)
                act_x(act, 0, 0)
                over_experts(act, act_expert)

            @block.gpsimd
            def _(pool):
                set_bounds(pool)
                nc.gpsimd.iota(spare_row[:], pattern=[[0, 1]], base=SEQ, channel_multiplier=1,
                               allow_small_or_imprecise_dtypes=True).then_inc(spare_made, 1)
                for e in range(2):
                    pool_gather(pool, e, e)
                over_experts(pool, pool_expert)
                for u in range(2):
                    pool.wait_ge(q.y_out[u], 16 * (NE // 2))

            @block.vector
            def _(dve):
                dve.wait_ge(spare_made, 1)
                for e in range(2):
                    pick(q, e, e, e)
                for e in range(2):
                    dve_ids(dve, e, 0, e)
                pick(q, 2, 2, 0)
                for c in range(2):
                    low(dve, 0, c)
                dve_x(dve, 0, 0)
                over_experts(dve, dve_expert)

        MORE = SEQ // CAP - 1
        o = Sems("o")
        turn, starts, shift = sem("turn"), sem("starts"), sem("shifted")
        o_w_in = [sem(f"ow_in{c}") for c in range(3)]
        o_xT, o_gated, o_hT, o_down = sem("oxT_ready"), sem("ogated"), sem("ohT_ready"), sem("oy_product")

        class moved:
            passed, xg_in, y_out = o.passed, [sem("oxg_moved")], [sem("oy_moved")]

        def items(eng, item, skip):
            most = eng.value_load(counts[0:1, NE:NE + 1], min_val=0, max_val=SEQ)
            with eng.If(most > CAP):
                with eng.Fori(0, NE) as e:
                    count = eng.value_load(counts[0:1, bass.ds(e, 1)], min_val=0, max_val=SEQ)
                    with eng.Fori(0, MORE) as k:
                        n = MORE * e + k
                        with eng.If(count > CAP * (k + 1)):
                            item(eng, e, k, n)
                        with eng.Else():
                            skip(eng, n)
                        eng.nop()
                    eng.nop()
                eng.nop()
            eng.nop()

        def back_to_zero(pool, which):
            pool.dma_reset(range(which.num, which.num + 1))
            pool.sem_clear(which)

        def own(eng, n, *counted):
            if n is not None:
                eng.wait_ge(turn, n + 1)
            for which, amount in counted:
                eng.sem_inc(which, amount)

        with ExitStack() as b:
            block = b.enter_context(nc.Block())

            @block.sync
            def _(sp):
                def item(sp, e, k, n):
                    sp.wait_ge(turn, n + 1)
                    for c, name in enumerate(("moe_w1", "moe_w2", "moe_w3")):
                        sp.dma_start(raw[:, 2 * c:2 * c + 2, :], view_w(name, e).rearrange(
                            "p (c k) f -> p c (k f)", c=2)).then_inc(o_w_in[c], 16)
                items(sp, item, lambda eng, n: own(eng, n, *((w_in, 16) for w_in in o_w_in)))

            @block.tensor
            def _(pe):
                def item(pe, e, k, n):
                    ids_mm(pe, o, e, n, 0)
                    x_transposes(pe, o, n, 0, n + 1)
                    pe.wait_ge(o_xT, 2 * n + 2)
                    for m in range(2):
                        pe.wait_ge(o_w_in[2 * m], 16 * (n + 1))
                        for kx in range(KD):
                            last = nc.tensor.matmul(ph[m][:], o_xT_all[:, kx, :], raw[:, 4 * m + kx // 4, :]
                                                    .rearrange("p (k f) -> p k f", f=DE)[:, kx % 4, :],
                                                    start=(kx == 0), stop=(kx == KD - 1))
                        last.then_inc(o_gated, 1)
                    h_transposes(pe, o, n)
                    pe.wait_ge(o_w_in[1], 16 * (n + 1))
                    pe.wait_ge(o_hT, n + 1)
                    for g in range(2):
                        for kx in range(KE):
                            last = nc.tensor.matmul(py[g][:], o_hT_all[:, kx, :], raw[:, 2 + kx // 2, :].rearrange(
                                "p (k f) -> p k f", f=D)[:, kx % 2, g * 512:g * 512 + 512],
                                start=(kx == 0), stop=(kx == KE - 1))
                    last.then_inc(o_down, 1)
                items(pe, item, lambda eng, n: own(eng, n, (o.ids_mm, 1), (o.x_mm, 2), (o_gated, 2), (o.h_mm, 1),
                                                   (o_down, 1)))

            @block.scalar
            def _(act):
                def item(act, e, k, n):
                    for g in range(2):
                        act.wait_ge(o.x_mm, 2 * n + g + 1)
                        nc.scalar.copy(o_xT_all[:, 4 * g:4 * g + 4, :], px[g][:]).then_inc(o_xT, 1)
                    act.wait_ge(o_gated, 2 * n + 1)
                    silu(act, o)
                    act.wait_ge(o_down, n + 1)
                    for g in range(2):
                        weighted(act, o, g, 0, 0)
                items(act, item, lambda eng, n: own(eng, n, (o_xT, 2), (o.silu, 1), (o.y_ready, 2)))

            @block.gpsimd
            def _(pool):
                def item(pool, e, k, n):
                    gather(pool, moved, o.ids, n, 0)
                    pool.wait_ge(moved.xg_in[0], 16)
                    back_to_zero(pool, moved.xg_in[0])
                    pool.sem_inc(o.xg_in[0], 1)
                    scatter(pool, moved, o, n, 0, 0)
                    pool.wait_ge(moved.y_out[0], 16)
                    back_to_zero(pool, moved.y_out[0])
                    pool.sem_inc(turn, 1)
                set_bounds(pool)
                pool.sem_inc(turn, 1)
                items(pool, item, lambda eng, n: own(eng, None, (o.xg_in[0], 1), (turn, 1)))

            @block.vector
            def _(dve):
                for k in range(MORE):
                    last = nc.vector.memset(list_start[:, k:k + 1], float(CAP * (k + 1)))
                last.then_inc(starts, 1)
                dve.wait_ge(starts, 1)

                def item(dve, e, k, n):
                    dve.wait_ge(turn, n + 1)
                    nc.vector.tensor_tensor(shifted_place[:], place[:, bass.ds(e, 1), :].rearrange(
                        "p a t -> p (a t)"), list_start[:, bass.ds(k, 1)].to_broadcast([P, T]),
                        ALU.subtract).then_inc(shift, 1)
                    dve.wait_ge(shift, n + 1)
                    pick(o, e, n, 0, shifted_place[:])
                    ids(dve, o, n, 0, 0)
                    dve.wait_ge(o_gated, 2 * n + 2)
                    hidden(dve, o, n)
                    dve.wait_ge(o.h_mm, n + 1)
                    nc.vector.tensor_copy(o_hT_all[:], pt[:]).then_inc(o_hT, 1)
                items(dve, item, lambda eng, n: own(eng, n, (shift, 1), (o.onehot, 1), (o.row_step, 4), (o.ids, 1),
                                                    (o.hd, 1), (o_hT, 1)))


def stage_store(nc, a, s):
    with ExitStack() as c:
        sb, ps, sem = mem(nc, c, "store")
        stored = [sem(f"stored{i}") for i in range(2)]
        block = c.enter_context(nc.Block())
        rows = s["sum_dram"].rearrange("(t p) d -> t p d", p=P)
        out_rows = a["out"].rearrange("b (t p) d -> (b t) p d", p=P)

        def store(eng, i):
            for t in range(i, T, 2):
                eng.dma_start(out_rows[t], rows[t]).then_inc(stored[i], 16)
            eng.wait_ge(stored[i], 16 * (T // 2))

        @block.sync
        def _(sp):
            store(sp, 0)

        @block.scalar
        def _(act):
            store(act, 1)


INPUTS = ["x", "rel_bias", "norm1_g", "w_in", "gla_wa2", "gla_ba", "gla_onorm_g", "diff_qnorm_g",
          "diff_knorm_g", "diff_lq1", "diff_lk1", "diff_lq2", "diff_lk2", "diff_subln_g", "w_out", "norm2_g",
          "moe_wg", "moe_bg", "moe_we", "moe_be", "moe_w1", "moe_w3", "moe_w2"]


def kernel(**inputs):
    import concourse.bacc as bacc
    from concourse.bass_utils import run_bass_kernel_spmd

    nc = bacc.Bacc("TRN2", target_bir_lowering=False, num_devices=1)
    arrays = {f"in_{n}": np.ascontiguousarray(inputs[n]) for n in INPUTS}
    arrays["in_bucket_onehot"] = buckets()
    a = {n[3:]: nc.dram_tensor(n, v.shape, mybir.dt.from_np(v.dtype), kind="ExternalInput").ap()
         for n, v in arrays.items()}
    a["out"] = nc.dram_tensor("out", (1, SEQ, D), F32, kind="ExternalOutput").ap()
    build(nc, a)
    r = run_bass_kernel_spmd(nc, [arrays], core_ids=[0])
    return r.results[0]["out"]
```

```python
import math
from contextlib import ExitStack

import numpy as np
import concourse.bass as bass
from concourse import mybir

F32 = mybir.dt.float32
F32R = mybir.dt.float32r
BF16 = mybir.dt.bfloat16
U32 = mybir.dt.uint32
I32 = mybir.dt.int32
ALU = mybir.AluOpType
ACT = mybir.ActivationFunctionType
AX = mybir.AxisListType

P = 128
SEQ = 1024
D = 1024
T = SEQ // P
KD = D // P
HG = 4
GDK, GDV = 64, 128
HD = 4
DDK, DDV = 64, 128
GR = 16
TAU = 16.0
EPS = 1e-6
LAMBDA_INIT = 0.8 - 0.6 * math.exp(-0.3 * 0)
NG, EPG = 4, 8
NE = NG * EPG
DE = 512
KE = DE // P
NEG = -1e30
BUCKETS, MAX_DIST = 32, 128
CAP = P
REL = 3 * P
CW = 256
CHUNKS_E, WC = 6, 2048
NROUTE = 6
NONE = 64 * P

GQ, GK, GV, GRC, GLR, DQ, DK, DV = 0, 256, 512, 1024, 1536, 1552, 2064, 2576


def buckets():
    rel = (REL - P) - np.arange(REL)
    n = np.maximum(rel, 0)
    exact = BUCKETS // 2
    large = exact + (np.log(np.maximum(n, exact).astype(np.float32) / np.float32(exact))
                     / np.float32(math.log(MAX_DIST / exact)) * np.float32(BUCKETS - exact)).astype(np.int32)
    b = np.where(n < exact, n, np.minimum(large, BUCKETS - 1))
    return (b[None, :] == np.arange(BUCKETS)[:, None]).astype(np.float32)


MAP = {"dqT": 20, "dkT": 36, "dv": 52, "gv": 68, "gqT": 84, "gkT": 92, "glr": 100, "xh": 101, "xl": 133,
       "rg": 101,
       "w_raw": 120, "w_in_raw": 206.5, "slot_rows": 216, "place": 219, "iota_slot": 220, "counts": 220.5}
LOCAL = {"norm1": 20, "project": 165, "mixers": 117, "outproj": 36}
END = 223.9


def mem(nc, c, stage):
    at = [LOCAL.get(stage, 20) * 1024]

    def sb(name, shape, dt=F32, kib=None):
        size = math.prod(shape[1:]) * mybir.dt.size(dt)
        size = -(-size // 32) * 32
        if kib is None:
            kib = at[0] / 1024
            at[0] += size
        assert kib * 1024 + size <= END * 1024, (name, kib, size)
        return nc.alloc_sbuf_tensor_at(f"{stage}_{name}", shape, dt, offset=int(kib * 1024))

    def ps(name, shape, dt=F32):
        return c.enter_context(nc.psum_tensor(f"{stage}_{name}", shape, dt))

    sems = []

    def sem(name):
        sems.append(nc.alloc_semaphore(f"{stage}_{name}"))
        return sems[-1]

    def clear():
        nc.clear_and_free_semaphores(sems)
        nc.all_engine_barrier()
    c.callback(clear)
    return sb, ps, sem


def build(nc, a):
    with ExitStack() as top:
        def keep(name, shape, dt=F32):
            return top.enter_context(nc.sbuf_tensor(name, shape, dt))

        def dram(name, shape, dt=F32):
            return nc.dram_tensor(name, shape, dt, kind="Internal").ap()

        def place(name, shape, dt=F32):
            return nc.alloc_sbuf_tensor_at(name, shape, dt, offset=int(MAP[name] * 1024))

        s = {
            "rel_dram": dram("rel_dram", [HD, REL]), "xn2_dram": dram("xn2_dram", [SEQ, D]),
            "r_dram": dram("r_dram", [P, T, HG * GDV]), "sum_dram": dram("sum_dram", [SEQ + CAP, D]),
            "ident": keep("ident", [P, P]), "causal": keep("causal", [P, HG, 64]),
            "gain_q": keep("gain_q", [P, 1]), "gain_k": keep("gain_k", [P, 1]), "lam": keep("lam", [P, 1]),
            "minus_half": keep("minus_half", [P, 8]),
            "logits": keep("logits", [P, T, NG + NE]),
            "dqT": place("dqT", [P, HD, SEQ]), "dkT": place("dkT", [P, HD, SEQ]),
            "dv": place("dv", [P, T, HD * DDV]), "gv": place("gv", [P, T, HG * GDV]),
            "gqT": place("gqT", [P, 2, SEQ]), "gkT": place("gkT", [P, 2, SEQ]),
            "glr": place("glr", [P, T, GR]), "xh": place("xh", [P, KD, SEQ], F32R),
            "xl": place("xl", [P, KD, SEQ], F32R), "rg": place("rg", [P, T, HG * GDV]),
            "slot_rows": place("slot_rows", [P, T, NE, NROUTE], BF16),
            "place": place("place", [P, NE, T]), "iota_slot": place("iota_slot", [P, CAP]),
            "counts": place("counts", [1, NE + 1], I32),
            "w_in_raw": [nc.alloc_sbuf_tensor_at(f"w_in_raw{i}", [P, KD, CW + GR], F32,
                                                 offset=int((MAP["w_in_raw"] + 8.5 * i) * 1024)) for i in range(2)],
            "w_in_ready": [nc.alloc_semaphore(f"w_in_ready{i}") for i in range(2)],
            "w_out_raw": [nc.alloc_sbuf_tensor_at(f"w_out_raw{i}", [P, KD, CW], F32,
                                                  offset=int((MAP["gqT"] + 8 * i) * 1024)) for i in range(2)],
            "w_out_ready": [nc.alloc_semaphore(f"w_out_ready{i}") for i in range(2)],
            "w_raw": place("w_raw", [P, 2, CHUNKS_E, WC]),
            "raw_in": [[nc.alloc_semaphore(f"raw_in{u}{c}") for c in range(CHUNKS_E)] for u in range(2)],
        }
        stages = [stage_norm1, stage_project, stage_mixers, stage_outproj,
                  stage_route, stage_experts, stage_store]
        for stage in stages:
            stage(nc, a, s)


CHUNKS = [(DQ, CW), (DQ + CW, CW), (DK, CW), (DK + CW, CW), (GV, CW), (GV + CW, CW), (DV, CW),
          (DV + CW, CW), (GRC, CW), (GRC + CW, CW + GR), (GQ, CW), (GK, CW)]
NORMED = 4
SILU = 8
CHANNEL = 10


def load_w_in(sp, a, s, i):
    col, w = CHUNKS[i]
    sp.dma_start(s["w_in_raw"][i % 2][:, :, 0:w], a["w_in"][0, :, col:col + w].rearrange(
        "(k p) c -> p k c", p=P)).then_inc(s["w_in_ready"][i % 2], 16)


def stage_norm1(nc, a, s):
    with ExitStack() as c:
        sb, ps, sem = mem(nc, c, "norm1")
        g1 = sb("g1", [P, D])
        x = sb("x", [P, T, D])
        sq = sb("sq", [P, D])
        xs = sb("xs", [P, 2, D])
        ss = sb("ss", [P, T])
        rs = sb("rs", [P, T])
        pt = [ps(f"pt{i}", [P, 4, P]) for i in range(4)]
        xh, xl, ident = s["xh"], s["xl"], s["ident"]
        g1_in = sem("g1_in")
        x_in = [sem(f"x_in{t}") for t in range(T)]
        squared = sem("squared")
        gain_ready = sem("gain_ready")
        shifted = sem("shifted")
        rstd_ready = sem("rstd_ready")
        scaled = sem("scaled")
        transposed = sem("transposed")
        high_ready = sem("high_ready")
        low_ready = sem("low_ready")
        onehot = sb("c_onehot", [BUCKETS, REL])
        relb = sb("c_relb", [BUCKETS, HD])
        relf = sb("c_relf", [HD, REL])
        lvec = sb("c_lvec", [P, 4, DDK])
        lprod = sb("c_lprod", [P, 2, DDK])
        lsum = sb("c_lsum", [P, 2])
        lexp = sb("c_lexp", [P, 2])
        graw = sb("c_graw", [P, 2])
        pf = ps("pf", [HD, 512])
        causal = s["causal"]
        relb_in = sem("c_relb_in")
        onehot_in = sem("c_onehot_in")
        lvec_in = [sem(f"c_lvec_in{i}") for i in range(4)]
        gain_in = [sem(f"c_gain_in{i}") for i in range(4)]
        rel_out = sem("c_rel_out")
        filled = sem("c_filled")
        relf_mm = sem("c_relf_mm")
        step = sem("c_step")
        lam_step = sem("c_lam_step")
        lam_exp = sem("c_lam_exp")
        masked = sem("c_masked")
        block = c.enter_context(nc.Block())
        x_rows = a["x"].rearrange("b (t p) d -> (b t) p d", p=P)

        @block.sync
        def _(sp):
            for t in range(T):
                sp.dma_start(x[:, t, :], x_rows[t]).then_inc(x_in[t], 16)
                if t == 0:
                    sp.dma_start(g1[:], a["norm1_g"].to_broadcast([P, D])).then_inc(g1_in, 16)
                if t in (5, 6):
                    load_w_in(sp, a, s, t - 5)
            sp.dma_start(relb[:], a["rel_bias"]).then_inc(relb_in, 16)
            sp.dma_start(onehot[:], a["bucket_onehot"]).then_inc(onehot_in, 16)
            for i, n in enumerate(("diff_lq1", "diff_lk1", "diff_lq2", "diff_lk2")):
                sp.dma_start(lvec[:, i, :], a[n].to_broadcast([P, DDK])).then_inc(lvec_in[i], 16)
            for i, n in enumerate(("diff_qnorm_g", "diff_knorm_g")):
                for half in range(2):
                    sp.dma_start(graw[half * 64:half * 64 + 64, i:i + 1],
                                 a[n].rearrange("a k -> k a")).then_inc(gain_in[2 * i + half], 16)
            sp.wait_ge(masked, 1)
            sp.dma_start(s["rel_dram"], relf[:]).then_inc(rel_out, 16)
            sp.wait_ge(rel_out, 16)

        @block.scalar
        def _(act):
            def high(t):
                for j in range(2):
                    act.wait_ge(transposed, 2 * t + j + 1)
                    nc.scalar.copy(xh[:, 4 * j:4 * j + 4, t * P:(t + 1) * P],
                                   pt[(2 * t + j) % 4][:]).then_inc(high_ready, 1)
            for t in range(T):
                act.wait_ge(x_in[t], 16)
                if t >= 1:
                    act.wait_ge(squared, t)
                nc.scalar.activation(sq[:], x[:, t, :], ACT.Square,
                                     accum_out=ss[:, t:t + 1]).then_inc(squared, 1)
                if t >= 1:
                    high(t - 1)
            high(T - 1)
            act.wait_ge(lam_step, 3)
            nc.scalar.activation(lexp[:], lsum[:], ACT.Exp).then_inc(lam_exp, 1)

        @block.vector
        def _(dve):
            def low(t):
                for j in range(2):
                    n = 2 * t + j
                    dve.wait_ge(high_ready, n + 1)
                    hi = xh[:, 4 * j:4 * j + 4, t * P:(t + 1) * P]
                    nc.vector.tensor_tensor(xl[:, 4 * j:4 * j + 4, t * P:(t + 1) * P], pt[n % 4][:],
                                            hi.bitcast(F32), ALU.subtract).then_inc(low_ready, 1)
            dve.wait_ge(g1_in, 16)
            nc.vector.tensor_scalar(g1[:], g1[:], D ** 0.5, None, ALU.mult).then_inc(gain_ready, 1)
            dve.wait_ge(gain_ready, 1)
            for t in range(T):
                dve.wait_ge(rstd_ready, t + 1)
                if t >= 2:
                    dve.wait_ge(transposed, 2 * (t - 1))
                nc.vector.scalar_tensor_tensor(out=xs[:, t % 2, :], in0=x[:, t, :], scalar=rs[:, t:t + 1],
                                               in1=g1[:], op0=ALU.mult, op1=ALU.mult).then_inc(scaled, 1)
                if t >= 1:
                    low(t - 1)
            low(T - 1)
            dve.wait_ge(relf_mm, 1)
            nc.vector.tensor_copy(relf[:], pf[:, 0:REL]).then_inc(step, 1)
            dve.wait_ge(step, 1)
            nc.vector.tensor_scalar(relf[:, 1:REL], relf[:, 1:REL], relf[:, 0:1], None,
                                    ALU.subtract).then_inc(step, 1)
            dve.wait_ge(step, 2)
            nc.vector.memset(relf[:, 0:1], 0.0)
            nc.vector.memset(relf[:, REL - P + 1:REL], NEG).then_inc(masked, 1)
            for i in range(4):
                dve.wait_ge(lvec_in[i], 16)
            for i in range(2):
                nc.vector.tensor_tensor(lprod[:, i, :], lvec[:, 2 * i, :], lvec[:, 2 * i + 1, :],
                                        ALU.mult).then_inc(lam_step, 1)
            dve.wait_ge(lam_step, 2)
            nc.vector.tensor_reduce(lsum[:], lprod[:], AX.X, ALU.add).then_inc(lam_step, 1)
            dve.wait_ge(lam_exp, 1)
            nc.vector.tensor_tensor(lexp[:, 0:1], lexp[:, 0:1], lexp[:, 1:2], ALU.subtract).then_inc(lam_step, 1)
            dve.wait_ge(lam_step, 4)
            nc.vector.tensor_scalar(s["lam"][:], lexp[:, 0:1], LAMBDA_INIT, None, ALU.add)
            for i in range(4):
                dve.wait_ge(gain_in[i], 16)
            nc.vector.tensor_scalar(s["gain_q"][:], graw[:, 0:1], DDK ** -0.5 * DDK ** 0.5, None, ALU.mult)
            nc.vector.tensor_scalar(s["gain_k"][:], graw[:, 1:2], DDK ** 0.5, None, ALU.mult)

        @block.gpsimd
        def _(pool):
            nc.gpsimd.memset(ident[:], 0.0).then_inc(filled, 1)
            nc.gpsimd.memset(causal[:], 1.0).then_inc(filled, 1)
            nc.gpsimd.memset(s["minus_half"][:], -0.5).then_inc(filled, 1)
            pool.wait_ge(filled, 3)
            nc.gpsimd.affine_select(out=ident[:], in_=ident[:], compare_op=ALU.not_equal, fill=1.0, base=0,
                                    pattern=[[-1, P]], channel_multiplier=1).then_inc(filled, 1)
            for t in range(T):
                pool.wait_ge(squared, t + 1)
                nc.gpsimd.tensor_scalar(rs[:, t:t + 1], ss[:, t:t + 1], EPS * D, None,
                                        ALU.add).then_inc(shifted, 1)
                pool.wait_ge(shifted, t + 1)
                nc.gpsimd.tensor_tensor(rs[:, t:t + 1], rs[:, t:t + 1], s["minus_half"][:, 0:1],
                                        ALU.pow).then_inc(rstd_ready, 1)
            for half in range(2):
                v = causal[64 * half:64 * half + 64]
                pool.wait_ge(filled, 4 + half)
                nc.gpsimd.affine_select(out=v, in_=v, compare_op=ALU.is_ge, fill=0.0, base=0,
                                        pattern=[[0, HG], [1, 64]],
                                        channel_multiplier=-1).then_inc(filled, 1)

        @block.tensor
        def _(pe):
            pe.wait_ge(filled, 4)
            for t in range(T):
                pe.wait_ge(scaled, t + 1)
                for j in range(2):
                    n = 2 * t + j
                    if n >= 4:
                        pe.wait_ge(low_ready, n - 3)
                    for k in range(4):
                        last = nc.tensor.transpose(pt[n % 4][:, k, :],
                                                   xs[:, t % 2, (4 * j + k) * P:(4 * j + k + 1) * P], ident[:])
                    last.then_inc(transposed, 1)
            pe.wait_ge(relb_in, 16)
            pe.wait_ge(onehot_in, 16)
            nc.tensor.matmul(pf[:, 0:REL], relb[:], onehot[:], start=True, stop=True).then_inc(relf_mm, 1)

def stage_project(nc, a, s):
    with ExitStack() as c:
        sb, ps, sem = mem(nc, c, "project")
        W = CW + GR
        raw, raw_in = s["w_in_raw"], s["w_in_ready"]
        c.callback(lambda: nc.clear_and_free_semaphores(raw_in))
        wh = [sb(f"w_high{i}", [P, KD, W], F32R) for i in range(2)]
        wl = [sb(f"w_low{i}", [P, KD, W], F32R) for i in range(2)]
        sq = sb("sq", [P, 2, 4, DDK])
        ss = sb("ss", [P, 2, 4])
        rs = sb("rs", [P, 2, 4])
        qn = sb("qn", [P, 2, 4 * DDK])
        rst = sb("rst", [P, 2, CW])
        pm = [ps(f"pm{i}", [P, 512]) for i in range(4)]
        pt = [ps(f"pt{i}", [P, 2, P]) for i in range(2)]
        xh, xl, ident = s["xh"], s["xl"], s["ident"]
        high_ready = sem("high_ready")
        low_ready = sem("low_ready")
        tile_ready = sem("tile_ready")
        bank_free_dve = sem("bank_free_dve")
        bank_free_act = sem("bank_free_act")
        squared = sem("squared")
        summed = sem("summed")
        shifted = sem("shifted")
        rstd_ready = sem("rstd_ready")
        normed = sem("normed")
        transposed = sem("transposed")
        stored = sem("stored")
        gated = sem("gated")
        r_out = [sem("r_out0"), sem("r_out1")]
        block = c.enter_context(nc.Block())
        BANKS = 4

        @block.sync
        def _(sp):
            for i in range(2, len(CHUNKS)):
                sp.wait_ge(low_ready, i - 1)
                load_w_in(sp, a, s, i)

        @block.tensor
        def _(pe):
            def products(t, slot, out, w):
                for k in range(KD):
                    hi, lo = xh[:, k, t * P:(t + 1) * P], xl[:, k, t * P:(t + 1) * P]
                    w_hi, w_lo = wh[slot][:, k, 0:w], wl[slot][:, k, 0:w]
                    nc.tensor.matmul(out, hi, w_hi, start=(k == 0), stop=False)
                    nc.tensor.matmul(out, hi, w_lo, start=False, stop=False)
                    last = nc.tensor.matmul(out, lo, w_hi, start=False, stop=(k == KD - 1))
                last.then_inc(tile_ready, 1)

            def transposes(n, t):
                pe.wait_ge(normed, n + 1)
                pe.wait_ge(stored, n + 1)
                for j in range(2):
                    last = nc.tensor.transpose(pt[t % 2][:, j, :], qn[:, t % 2, j * P:(j + 1) * P], ident[:])
                last.then_inc(transposed, 1)

            with pe.Fori(0, NORMED // 2) as i:
                for slot in range(2):
                    pe.wait_ge(low_ready, 2 * i + slot + 1)
                    for t in range(T):
                        n = (2 * i + slot) * T + t
                        pe.wait_ge(bank_free_dve, n + 1)
                        products(t, slot, pm[t % BANKS][:, 0:CW], CW)
                        if t >= 2:
                            transposes(n - 2, t - 2)
                    for t in range(T - 2, T):
                        transposes((2 * i + slot) * T + t, t)
            with pe.Fori(NORMED // 2, SILU // 2) as i:
                for slot in range(2):
                    pe.wait_ge(low_ready, 2 * i + slot + 1)
                    for t in range(T):
                        pe.wait_ge(bank_free_dve, (2 * i + slot) * T + t + 1)
                        products(t, slot, pm[t % BANKS][:, 0:CW], CW)
            for ch in range(SILU, CHANNEL):
                w = CHUNKS[ch][1]
                pe.wait_ge(low_ready, ch + 1)
                for t in range(T):
                    m = (ch - SILU) * T + t - BANKS
                    if m < 0:
                        pe.wait_ge(bank_free_dve, SILU * T + t + 1)
                    else:
                        pe.wait_ge(bank_free_act, m + 1)
                    products(t, ch % 2, pm[t % BANKS][:, 0:w], w)
            for ch in range(CHANNEL, len(CHUNKS)):
                pe.wait_ge(low_ready, ch + 1)
                w_hi, w_lo = wh[ch % 2], wl[ch % 2]
                for g in range(4):
                    j, half = g // 2, g % 2
                    if ch == CHANNEL:
                        pe.wait_ge(bank_free_act, (CHANNEL - SILU) * T - BANKS + g + 1)
                    else:
                        pe.wait_ge(bank_free_dve, SILU * T + BANKS + g + 1)
                    for k in range(KD):
                        m_hi, m_lo = w_hi[:, k, j * P:(j + 1) * P], w_lo[:, k, j * P:(j + 1) * P]
                        n_hi, n_lo = xh[:, k, half * 512:half * 512 + 512], xl[:, k, half * 512:half * 512 + 512]
                        nc.tensor.matmul(pm[g][:], m_hi, n_hi, start=(k == 0), stop=False)
                        nc.tensor.matmul(pm[g][:], m_hi, n_lo, start=False, stop=False)
                        last = nc.tensor.matmul(pm[g][:], m_lo, n_hi, start=False, stop=(k == KD - 1))
                    last.then_inc(tile_ready, 1)

        @block.scalar
        def _(act):
            def high(ch):
                w = CHUNKS[ch][1]
                act.wait_ge(raw_in[ch % 2], 16 * (ch // 2 + 1))
                if ch >= 2:
                    act.wait_ge(tile_ready, T * (ch - 1))
                nc.scalar.copy(wh[ch % 2][:, :, 0:w], raw[ch % 2][:, :, 0:w]).then_inc(high_ready, 1)

            def store_transposed(n):
                ch, t = n // T, n % T
                dst, gain = (s["dqT"], s["gain_q"]) if ch < 2 else (s["dkT"], s["gain_k"])
                pair = 2 * (ch % 2)
                act.wait_ge(transposed, n + 1)
                nc.scalar.activation(dst[:, pair:pair + 2, t * P:(t + 1) * P], pt[n % 2][:], ACT.Copy,
                                     scale=gain[:, 0:1]).then_inc(stored, 1)

            act.sem_inc(stored, 2)
            high(0)
            for ch in range(len(CHUNKS)):
                if ch + 1 < len(CHUNKS):
                    high(ch + 1)
                for t in range(T):
                    n = ch * T + t
                    if ch < NORMED:
                        act.wait_ge(tile_ready, n + 1)
                        if n >= 2:
                            act.wait_ge(summed, n - 1)
                        nc.scalar.activation(sq[:, n % 2], pm[t % BANKS][:, 0:CW].rearrange(
                            "p (g d) -> p g d", g=4), ACT.Square).then_inc(squared, 1)
                        if t >= 3:
                            store_transposed(n - 3)
                        if t == T - 1:
                            for m in range(n - 2, n + 1):
                                store_transposed(m)
                    elif SILU <= ch < CHANNEL:
                        m = (ch - SILU) * T + t
                        act.wait_ge(tile_ready, n + 1)
                        if m >= 2:
                            act.wait_ge(r_out[m % 2], 16 * (m // 2))
                        if ch == SILU + 1:
                            nc.scalar.copy(s["glr"][:, t, :], pm[t % BANKS][:, CW:CW + GR])
                        nc.scalar.activation(rst[:, m % 2, :], pm[t % BANKS][:, 0:CW], ACT.Silu) \
                            .then_inc(bank_free_act, 1)
                        act.wait_ge(bank_free_act, m + 1)
                        act.dma_start(s["r_dram"][:, t, (ch - SILU) * CW:(ch - SILU + 1) * CW],
                                      rst[:, m % 2, :]).then_inc(r_out[m % 2], 16)
            for i in range(2):
                act.wait_ge(r_out[i], 16 * T)

        @block.gpsimd
        def _(pool):
            for n in range(NORMED * T):
                pool.wait_ge(summed, n + 1)
                if n >= 2:
                    pool.wait_ge(normed, n - 1)
                nc.gpsimd.tensor_scalar(rs[:, n % 2, :], ss[:, n % 2, :], EPS * DDK, None,
                                        ALU.add).then_inc(shifted, 1)
                pool.wait_ge(shifted, n + 1)
                nc.gpsimd.tensor_tensor(rs[:, n % 2, :], rs[:, n % 2, :], s["minus_half"][:, 0:4],
                                        ALU.pow).then_inc(rstd_ready, 1)

        @block.vector
        def _(dve):
            def low(ch):
                w = CHUNKS[ch][1]
                dve.wait_ge(high_ready, ch + 1)
                nc.vector.tensor_tensor(wl[ch % 2][:, :, 0:w], raw[ch % 2][:, :, 0:w],
                                        wh[ch % 2][:, :, 0:w].bitcast(F32), ALU.subtract).then_inc(low_ready, 1)

            dve.sem_inc(bank_free_dve, BANKS)
            low(0)
            for ch in range(len(CHUNKS)):
                if ch + 1 < len(CHUNKS):
                    low(ch + 1)
                for t in range(T):
                    n = ch * T + t
                    if ch < NORMED:
                        i = n % 2
                        dve.wait_ge(squared, n + 1)
                        if n >= 2:
                            dve.wait_ge(rstd_ready, n - 1)
                        nc.vector.tensor_reduce(ss[:, i, :], sq[:, i], AX.X, ALU.add).then_inc(summed, 1)
                        dve.wait_ge(rstd_ready, n + 1)
                        if n >= 2:
                            dve.wait_ge(transposed, n - 1)
                        nc.vector.tensor_tensor(qn[:, i].rearrange("p (g d) -> p g d", g=4),
                                                pm[t % BANKS][:, 0:CW].rearrange("p (g d) -> p g d", g=4),
                                                rs[:, i, :].unsqueeze(2).to_broadcast([P, 4, DDK]),
                                                ALU.mult).then_inc(normed, 1)
                        dve.wait_ge(normed, n + 1)
                        dve.sem_inc(bank_free_dve, 1)
                    elif ch < SILU:
                        dst = s["gv"] if ch < 6 else s["dv"]
                        dve.wait_ge(tile_ready, n + 1)
                        nc.vector.tensor_copy(dst[:, t, (ch % 2) * CW:(ch % 2 + 1) * CW],
                                              pm[t % BANKS][:, 0:CW]).then_inc(bank_free_dve, 1)
                    elif ch >= CHANNEL and t < 4:
                        dst = s["gqT"] if ch == CHANNEL else s["gkT"]
                        dve.wait_ge(tile_ready, CHANNEL * T + (ch - CHANNEL) * 4 + t + 1)
                        nc.vector.tensor_copy(dst[:, t // 2, (t % 2) * 512:(t % 2) * 512 + 512],
                                              pm[t][:]).then_inc(bank_free_dve, 1)


def stage_mixers(nc, a, s):
    with ExitStack() as c_:
        sb, ps, sem = mem(nc, c_, "mixers")
        ident, causal, gqT, gkT, gv = s["ident"], s["causal"], s["gqT"], s["gkT"], s["gv"]
        dqT, dkT, dv, rgn = s["dqT"], s["dkT"], s["dv"], s["rg"]
        bias = sb("bias", [P, HD, 2 * P])
        mirror = sb("mirror", [P, HD, 2 * P])
        anti = sb("anti", [P, P])
        gain = sb("gain", [P, DDV])
        neg_lam = sb("neg_lam", [P, 1])
        nmax = sb("nmax", [P, 2, 2])
        sums = sb("sums", [P, 3, 2])
        coef = sb("coef", [P, 2, 2])
        prob = sb("prob", [P, 2, 2, SEQ])
        wt = sb("wt", [P, 2, SEQ])
        wT = sb("wT", [P, 2, T, P])
        sq = sb("sq", [P, DDV])
        ss = sb("ss", [P, 2])
        rs = sb("rs", [P, 2])
        inv = sb("inv", [P, 4])
        glrT = sb("glrT", [GR, SEQ])
        wa2 = sb("wa2", [GR, 2 * P])
        ba = sb("ba", [P, 2])
        absz = sb("absz", [P, 2, SEQ])
        minz = sb("minz", [P, 2, SEQ])
        keepsum = sb("keepsum", [P, SEQ])
        b = absz
        arg = sb("arg", [P, 3, 2, P])
        ex = sb("ex", [P, 2, 5, 2, P])
        E_B, E_MQ, E_MK, E_OFF, E_LAST = range(5)
        g_gain = sb("g_gain", [P, GDV])
        st = sb("st", [P, 2, 5, 2, P])
        QD, KD_, QO, QI, KL = range(5)
        kdT = sb("kdT", [P, 2, P])
        sc = sb("sc", [P, 2, 2, P])
        state = sb("state", [P, 2, GDV])
        g_o = sb("g_o", [P, HG, GDV])
        g_sq = sb("g_sq", [P, HG, GDV])
        g_ss = sb("g_ss", [P, HG])
        g_rs = sb("g_rs", [P, HG])
        score = [ps(f"score{i}", [P, SEQ]) for i in range(2)]
        pt = [ps(f"pt{i}", [P, 4, P]) for i in range(2)]
        po = [ps(f"po{i}", [P, 512]) for i in range(2)]
        bias_in, gain_in = sem("bias_in"), sem("gain_in")
        prepared, zeroed, anti_ready, turned = sem("prepared"), sem("zeroed"), sem("anti_ready"), sem("turned")
        scored = [sem("scored0"), sem("scored1")]
        biased = [sem("biased0"), sem("biased1")]
        max_ready = [sem("max_ready0"), sem("max_ready1")]
        exp_done = [sem("exp_done0"), sem("exp_done1")]
        coef_step, weighted = sem("coef_step"), sem("weighted")
        transposed, wT_ready = sem("transposed"), sem("wT_ready")
        o_ready, squared = sem("o_ready"), sem("squared")
        shifted, rooted, rstd_ready, normed = sem("shifted"), sem("rooted"), sem("rstd_ready"), sem("normed")
        wa2_in, g_gain_in, r_in = sem("wa2_in"), sem("g_gain_in"), sem("r_in")
        ba_in = [sem("ba_in0"), sem("ba_in1")]
        filled, cleared = sem("filled"), sem("cleared")
        glrT_mm, glrT_ready, z_ready = sem("glrT_mm"), sem("glrT_ready"), sem("z_ready")
        abs_ready, min_ready, log_step = sem("abs_ready"), sem("min_ready"), sem("log_step")
        sum_step, b_ready = sem("sum_step"), sem("b_ready")
        arg_step, arg_ready, factors = sem("arg_step"), sem("arg_ready"), sem("factors_ready")
        g_gain_ready, rgn_ready = sem("g_gain_ready"), sem("rgn_ready")
        staged, g_scored, kdT_ready = sem("staged"), sem("g_scored"), sem("kdT_ready")
        masked, g_o_mm, g_taken = sem("masked"), sem("g_o_mm"), sem("g_taken")
        state_ready, g_squared, g_summed = sem("state_ready"), sem("g_squared"), sem("g_summed")
        g_shifted, g_rstd, g_normed = sem("g_shifted"), sem("g_rstd"), sem("g_normed")
        gated = sem("gated")
        block = c_.enter_context(nc.Block())
        N = HD * T
        TILE_ORDER = (7, 0, 6, 1, 5, 2, 4, 3)

        def item(n):
            return n // T, TILE_ORDER[n % T]
        groups = [-(-(item(n)[1] + 1) // 4) for n in range(N)]
        first = [sum(groups[:n]) for n in range(N + 1)]

        steps, when = [], {}
        for n in range(N):
            steps.append(("attend", n))
            if n >= 5 and (n - 5) % 3 == 0 and (n - 5) // 3 < T:
                steps.append(("inner", (n - 5) // 3))
            if n >= 7 and (n - 7) % 3 == 0 and (n - 7) // 3 < T:
                steps.append(("outer", (n - 7) // 3))
        M = len(steps)
        for n in range(T):
            when["factors", steps.index(("attend", 3 + 3 * n))] = n
            when["scale", steps.index(("attend", 4 + 3 * n))] = n

        def at(m, kind):
            return steps[m][1] if 0 <= m < M and steps[m][0] == kind else None

        def tok(x, n):
            return x[:, :, n * P:(n + 1) * P]

        @block.sync
        def _(sp):
            sp.dma_start(wa2[:], a["gla_wa2"][0]).then_inc(wa2_in, 16)
            for j in range(2):
                sp.dma_start(ba[:, j:j + 1], a["gla_ba"][:, j * P:(j + 1) * P].rearrange(
                    "a p -> p a")).then_inc(ba_in[j], 16)
            sp.dma_start(gain[:], a["diff_subln_g"].to_broadcast([P, DDV])).then_inc(gain_in, 16)
            for h in range(HD):
                sp.dma_start(mirror[:, h, :], bass.AP(s["rel_dram"].tensor, h * REL + 1,
                                                      [[1, P], [1, 2 * P]])).then_inc(bias_in, 16)
            sp.dma_start(g_gain[:], a["gla_onorm_g"].to_broadcast([P, GDV])).then_inc(g_gain_in, 16)
            sp.dma_start(rgn[:], s["r_dram"]).then_inc(r_in, 16)
            sp.wait_ge(staged, T)
            for i in range(2):
                load_w_out(sp, a, i, s["w_out_raw"][i], s["w_out_ready"][i])

        @block.tensor
        def _(pe):
            def free_scores(m, comp):
                kind, n = steps[m - 1] if m else (None, 0)
                if kind is None:
                    pe.wait_ge(min_ready, 2 * comp + 2)
                elif kind == "attend":
                    pe.wait_ge(exp_done[comp], n + 1)
                elif kind == "inner":
                    pe.wait_ge(masked, n + 1)
                    if comp == 0:
                        pe.wait_ge(kdT_ready, n + 1)
                elif comp == 0:
                    pe.wait_ge(g_taken, n + 1)
                else:
                    pe.wait_ge(state_ready, n + 2)

            def scores(m, n):
                h, t = item(n)
                for comp in range(2):
                    r = 64 * comp
                    free_scores(m, comp)
                    for k0 in range(0, (t + 1) * P, 512):
                        k1 = min(k0 + 512, (t + 1) * P)
                        last = nc.tensor.matmul(score[comp][:, k0:k1], dqT[r:r + 64, h, t * P:(t + 1) * P],
                                                dkT[r:r + 64, h, k0:k1], start=True, stop=True)
                    last.then_inc(scored[comp], 1)

            def transposes(n):
                pe.wait_ge(weighted, n + 1)
                for g in range(groups[n]):
                    i = first[n] + g
                    if i >= 2:
                        pe.wait_ge(wT_ready, i - 1)
                    for j in range(4 * g, min(4 * g + 4, item(n)[1] + 1)):
                        last = nc.tensor.transpose(pt[i % 2][:, j % 4, :], wt[:, n % 2, j * P:(j + 1) * P],
                                                   ident[:])
                    last.then_inc(transposed, 1)

            def values(n):
                h, t = item(n)
                pe.wait_ge(wT_ready, first[n + 1])
                if n == 0:
                    pe.wait_ge(prepared, 4)
                if n >= 2:
                    pe.wait_ge(normed, n - 1)
                for j in range(t + 1):
                    last = nc.tensor.matmul(po[n % 2][:, 0:DDV], wT[:, n % 2, j, :],
                                            dv[:, j, h * DDV:(h + 1) * DDV], start=(j == 0), stop=(j == t))
                last.then_inc(o_ready, 1)

            def inner(m, n):
                u = n % 2
                pe.wait_ge(staged, n + 1)
                free_scores(m, 0)
                free_scores(m, 1)
                for p in range(2):
                    nc.tensor.transpose(score[0][:, p * P:(p + 1) * P], st[:, u, KL, p, :], ident[:])
                for i, (key, query) in enumerate(((KD_, QD), (QO, QO))):
                    for p in range(2):
                        for odd in range(2):
                            r = 64 * odd
                            out = (score[0][:, 512:1024], score[1][:, 0:512])[odd]
                            last = nc.tensor.matmul(out[:, (2 * i + p) * P:(2 * i + p + 1) * P],
                                                    st[r:r + 64, u, key, p, :], st[r:r + 64, u, query, p, :],
                                                    start=True, stop=True)
                last.then_inc(g_scored, 1)

            def outer(m, n):
                u = n % 2
                free_scores(m, 0)
                pe.wait_ge(masked, n + 1)
                pe.wait_ge(state_ready, n + 1)
                for h in range(HG):
                    r, p = 64 * (h % 2), h // 2
                    o = score[0][:, 512 * (h % 2) + p * P:512 * (h % 2) + (p + 1) * P]
                    nc.tensor.matmul(o, sc[:, h % 2, p, :], gv[:, n, h * P:(h + 1) * P], start=True,
                                     stop=False)
                    nc.tensor.matmul(o, st[r:r + 64, u, QI, p, :], state[r:r + 64, p, :], start=False, stop=True)
                free_scores(m, 1)
                pe.wait_ge(kdT_ready, n + 1)
                for p in range(2):
                    last = nc.tensor.matmul(score[1][:, p * 256:(p + 1) * 256], kdT[:, p, :],
                                            gv[:, n, p * 256:(p + 1) * 256], start=True, stop=True)
                last.then_inc(g_o_mm, 1)

            for t in range(T):
                last = nc.tensor.transpose(pt[t // 4][0:GR, t % 4, :], s["glr"][:, t, :], ident[:])
            last.then_inc(glrT_mm, 1)
            pe.wait_ge(wa2_in, 16)
            pe.wait_ge(glrT_ready, 1)
            for g in range(4):
                nc.tensor.matmul(score[g // 2][:, (g % 2) * 512:(g % 2 + 1) * 512],
                                 wa2[:, (g // 2) * P:(g // 2 + 1) * P],
                                 glrT[:, (g % 2) * 512:(g % 2 + 1) * 512], start=True,
                                 stop=True).then_inc(z_ready, 1)
            pe.wait_ge(bias_in, 16 * HD)
            pe.wait_ge(anti_ready, 1)
            for h in range(HD):
                last = nc.tensor.matmul(po[h // 2][:, (h % 2) * 256:(h % 2) * 256 + 256], anti[:],
                                        mirror[:, h, :], start=True, stop=True)
            last.then_inc(turned, 1)

            for m in range(M + 3):
                if m < M:
                    kind, n = steps[m]
                    {"attend": scores, "inner": inner, "outer": outer}[kind](m, n)
                if at(m - 2, "attend") is not None:
                    transposes(at(m - 2, "attend"))
                if at(m - 3, "attend") is not None:
                    values(at(m - 3, "attend"))

        @block.scalar
        def _(act):
            def exps(n):
                nk = (item(n)[1] + 1) * P
                for comp in range(2):
                    act.wait_ge(max_ready[comp], n + 1)
                    if n >= 2:
                        act.wait_ge(weighted, n - 1)
                    nc.scalar.activation(prob[:, n % 2, comp, 0:nk], score[comp][:, 0:nk], ACT.Exp,
                                         bias=nmax[:, n % 2, comp:comp + 1],
                                         accum_out=sums[:, n % 3, comp:comp + 1]).then_inc(exp_done[comp], 1)

            def copies(n):
                for g in range(groups[n]):
                    w = min(4, item(n)[1] + 1 - 4 * g)
                    act.wait_ge(transposed, first[n] + g + 1)
                    if n >= 2 and g == 0:
                        act.wait_ge(o_ready, n - 1)
                    nc.scalar.copy(wT[:, n % 2, 4 * g:4 * g + w, :],
                                   pt[(first[n] + g) % 2][:, 0:w, :]).then_inc(wT_ready, 1)

            def square(n):
                act.wait_ge(o_ready, n + 1)
                if n >= 1:
                    act.wait_ge(squared, n)
                if n >= 2:
                    act.wait_ge(shifted, n - 1)
                nc.scalar.activation(sq[:], po[n % 2][:, 0:DDV], ACT.Square, scale=inv[:, n % 4:n % 4 + 1],
                                     accum_out=ss[:, n % 2:n % 2 + 1]).then_inc(squared, 1)

            def make_factors(n):
                u = n % 2
                act.wait_ge(arg_ready, n + 1)
                if n >= 2:
                    act.wait_ge(state_ready, n)
                E = nc.scalar.activation
                E(ex[:, u, E_B], tok(b, n), ACT.Exp, scale=1.0 / TAU)
                E(ex[:, u, E_MQ], arg[:, 0], ACT.Exp, scale=1.0 / TAU)
                E(ex[:, u, E_MK], arg[:, 0], ACT.Exp, scale=-1.0 / TAU)
                E(ex[:, u, E_OFF, :, 0:64], arg[:, 1, :, 0:64], ACT.Exp, scale=-1.0 / TAU)
                E(ex[:, u, E_OFF, :, 64:P], arg[:, 1, :, 64:P], ACT.Exp, scale=1.0 / TAU)
                E(ex[:, u, E_LAST], arg[:, 2], ACT.Exp, scale=-1.0 / TAU).then_inc(factors, 1)

            def inner(n):
                act.wait_ge(g_scored, n + 1)
                if n >= 1:
                    act.wait_ge(g_o_mm, n)
                nc.scalar.copy(kdT[:], score[0][:, 0:2 * P].rearrange("p (j x) -> p j x", j=2)) \
                    .then_inc(kdT_ready, 1)

            def outer(n):
                act.wait_ge(g_o_mm, n + 1)
                if n >= 1:
                    act.wait_ge(g_normed, n)
                for odd in range(2):
                    last = nc.scalar.copy(g_o[:, 2 * odd:2 * odd + 2, :], score[0][:, 512 * odd:512 * odd + 2 * P]
                                          .rearrange("p (h d) -> p h d", h=2))
                last.then_inc(g_taken, 1)
                act.wait_ge(g_taken, n + 1)
                nc.scalar.activation(g_sq[:], g_o[:], ACT.Square).then_inc(g_squared, 1)

            act.wait_ge(ba_in[0], 16)
            act.wait_ge(ba_in[1], 16)
            for g in range(4):
                act.wait_ge(z_ready, g + 1)
                nc.scalar.activation(absz[:, g // 2, (g % 2) * 512:(g % 2 + 1) * 512],
                                     score[g // 2][:, (g % 2) * 512:(g % 2 + 1) * 512], ACT.Abs,
                                     bias=ba[:, g // 2:g // 2 + 1]).then_inc(abs_ready, 1)
            for m in range(M + 3):
                if m < M:
                    kind, n = steps[m]
                    {"attend": exps, "inner": inner, "outer": outer}[kind](n)
                if m == 0:
                    act.wait_ge(abs_ready, 4)
                    nc.scalar.activation(absz[:], absz[:], ACT.Exp, scale=-1.0).then_inc(log_step, 1)
                    act.wait_ge(log_step, 1)
                    nc.scalar.activation(absz[:], absz[:], ACT.Ln, bias=1.0).then_inc(log_step, 1)
                if at(m - 2, "attend") is not None:
                    copies(at(m - 2, "attend"))
                if at(m - 3, "attend") is not None:
                    square(at(m - 3, "attend"))
                if ("factors", m) in when:
                    make_factors(when["factors", m])

        @block.gpsimd
        def _(pool):
            nc.gpsimd.memset(anti[:], 0.0).then_inc(zeroed, 1)
            pool.wait_ge(zeroed, 1)
            nc.gpsimd.affine_select(out=anti[:], in_=anti[:], compare_op=ALU.not_equal, fill=1.0,
                                    base=-(P - 1), pattern=[[1, P]], channel_multiplier=1).then_inc(anti_ready, 1)
            nc.gpsimd.memset(keepsum[:], 1.0).then_inc(filled, 1)
            pool.wait_ge(filled, 1)
            nc.gpsimd.memset(keepsum[:].rearrange("p (n x) -> p n x", x=P)[:, :, 0:1], 0.0).then_inc(filled, 1)
            pool.wait_ge(g_gain_ready, 1)
            pool.wait_ge(r_in, 16)
            for m in range(M + 4):
                if at(m - 1, "outer") is not None:
                    n = at(m - 1, "outer")
                    pool.wait_ge(g_summed, n + 1)
                    if n >= 1:
                        pool.wait_ge(g_normed, n)
                    nc.gpsimd.tensor_scalar(g_rs[:], g_ss[:], EPS * GDV, None, ALU.add).then_inc(g_shifted, 1)
                    pool.wait_ge(g_shifted, n + 1)
                    nc.gpsimd.tensor_tensor(g_rs[:], g_rs[:], s["minus_half"][:, 0:HG],
                                            ALU.pow).then_inc(g_rstd, 1)
                if at(m, "inner") is not None:
                    n = at(m, "inner")
                    v = rgn[:, n, :].rearrange("p (h d) -> p h d", h=HG)
                    nc.gpsimd.tensor_tensor(v, v, g_gain[:].unsqueeze(1).to_broadcast([P, HG, GDV]),
                                            ALU.mult).then_inc(rgn_ready, 1)
                if at(m - 3, "attend") is not None:
                    n = at(m - 3, "attend")
                    i = n % 2
                    pool.wait_ge(squared, n + 1)
                    if n >= 2:
                        pool.wait_ge(normed, n - 1)
                    nc.gpsimd.tensor_scalar(rs[:, i:i + 1], ss[:, i:i + 1], EPS * DDV, None,
                                            ALU.add).then_inc(shifted, 1)
                    pool.wait_ge(shifted, n + 1)
                    nc.gpsimd.tensor_tensor(rs[:, i:i + 1], rs[:, i:i + 1], s["minus_half"][:, 0:1],
                                            ALU.pow).then_inc(rooted, 1)
                    pool.wait_ge(rooted, n + 1)
                    nc.gpsimd.tensor_tensor(rs[:, i:i + 1], rs[:, i:i + 1], inv[:, n % 4:n % 4 + 1],
                                            ALU.mult).then_inc(rstd_ready, 1)

        @block.vector
        def _(dve):
            dve.wait_ge(glrT_mm, 1)
            for i in range(2):
                last = nc.vector.tensor_copy(glrT[:, i * 512:(i + 1) * 512].rearrange("p (j x) -> p j x", j=4),
                                             pt[i][0:GR])
            last.then_inc(glrT_ready, 1)
            dve.wait_ge(gain_in, 16)
            nc.vector.tensor_scalar(gain[:], gain[:], (1.0 - LAMBDA_INIT) * DDV ** 0.5, None,
                                    ALU.mult).then_inc(prepared, 1)
            nc.vector.tensor_scalar(neg_lam[:], s["lam"][:], -1.0, None, ALU.mult).then_inc(prepared, 1)
            dve.wait_ge(ba_in[0], 16)
            dve.wait_ge(ba_in[1], 16)
            for g in range(4):
                dve.wait_ge(abs_ready, g + 1)
                nc.vector.tensor_scalar(minz[:, g // 2, (g % 2) * 512:(g % 2 + 1) * 512],
                                        score[g // 2][:, (g % 2) * 512:(g % 2 + 1) * 512],
                                        ba[:, g // 2:g // 2 + 1], 0.0, ALU.add, ALU.min).then_inc(min_ready, 1)
            dve.wait_ge(turned, 1)
            for i in range(2):
                nc.vector.tensor_copy(bias[:, 2 * i:2 * i + 2, :], po[i][:].rearrange(
                    "p (h x) -> p h x", h=2)).then_inc(prepared, 1)
            dve.wait_ge(prepared, 4)
            dve.wait_ge(g_gain_in, 16)
            nc.vector.tensor_scalar(g_gain[:], g_gain[:], GDV ** 0.5, None, ALU.mult).then_inc(g_gain_ready, 1)
            nc.vector.memset(sc[:], 0.0).then_inc(cleared, 1)
            nc.vector.memset(state[:], 0.0).then_inc(state_ready, 1)

            def running_sums():
                dve.wait_ge(filled, 2)
                dve.wait_ge(log_step, 2)
                dve.wait_ge(min_ready, 4)
                nc.vector.tensor_tensor(minz[:], minz[:], absz[:], ALU.subtract).then_inc(sum_step, 1)
                dve.wait_ge(sum_step, 1)
                for p in range(2):
                    nc.vector.tensor_tensor_scan(b[:, p, :], keepsum[:], minz[:, p, :], 0.0, ALU.mult,
                                                 ALU.add).then_inc(b_ready, 1)

            def maxima(n):
                h, nk = n // T, (item(n)[1] + 1) * P
                w = min(nk, 2 * P)
                for comp in range(2):
                    dve.wait_ge(scored[comp], n + 1)
                    near = score[comp][:, nk - w:nk]
                    nc.vector.tensor_tensor(near, near, bias[:, h, 2 * P - w:2 * P],
                                            ALU.add).then_inc(biased[comp], 1)
                    dve.wait_ge(biased[comp], n + 1)
                    nc.vector.tensor_reduce(nmax[:, n % 2, comp:comp + 1], score[comp][:, 0:nk], AX.X, ALU.max,
                                            negate=True).then_inc(max_ready[comp], 1)

            def weights(n):
                nk, i = (item(n)[1] + 1) * P, n % 2
                dve.wait_ge(exp_done[0], n + 1)
                dve.wait_ge(exp_done[1], n + 1)
                if n >= 4:
                    dve.wait_ge(rstd_ready, n - 3)
                nc.vector.reciprocal(inv[:, n % 4:n % 4 + 1], sums[:, n % 3, 0:1])
                nc.vector.reciprocal(coef[:, i, 0:1], sums[:, n % 3, 1:2]).then_inc(coef_step, 1)
                dve.wait_ge(coef_step, 2 * n + 1)
                nc.vector.tensor_scalar(coef[:, i, 1:2], coef[:, i, 0:1], sums[:, n % 3, 0:1], neg_lam[:],
                                        ALU.mult, ALU.mult).then_inc(coef_step, 1)
                dve.wait_ge(coef_step, 2 * n + 2)
                if n >= 2:
                    dve.wait_ge(transposed, first[n - 1])
                nc.vector.scalar_tensor_tensor(out=wt[:, i, 0:nk], in0=prob[:, i, 1, 0:nk],
                                               scalar=coef[:, i, 1:2], in1=prob[:, i, 0, 0:nk],
                                               op0=ALU.mult, op1=ALU.add).then_inc(weighted, 1)

            def norm(n):
                h, t = item(n)
                dve.wait_ge(rstd_ready, n + 1)
                nc.vector.scalar_tensor_tensor(out=dqT[:, h, t * P:(t + 1) * P], in0=po[n % 2][:, 0:DDV],
                                               scalar=rs[:, n % 2:n % 2 + 1], in1=gain[:], op0=ALU.mult,
                                               op1=ALU.mult).then_inc(normed, 1)

            def exponents(n):
                if n == 0:
                    dve.wait_ge(b_ready, 2)
                if n >= 1:
                    dve.wait_ge(factors, n)
                v = tok(b, n)
                for half in range(2):
                    w = slice(64 * half, 64 * half + 64)
                    mid = 64 * half + 31
                    last = nc.vector.tensor_tensor(arg[:, 0, :, w], v[:, :, w],
                                                   v[:, :, mid:mid + 1].to_broadcast([P, 2, 64]), ALU.subtract)
                last.then_inc(arg_step, 1)
                for i, last_of in ((1, 63), (2, 127)):
                    nc.vector.tensor_tensor(arg[:, i], v, v[:, :, last_of:last_of + 1].to_broadcast([P, 2, P]),
                                            ALU.subtract)
                dve.wait_ge(arg_step, n + 1)
                nc.vector.tensor_scalar(arg[:, 0], arg[:, 0], 40.0 * TAU, -40.0 * TAU, ALU.min,
                                        ALU.max).then_inc(arg_ready, 1)

            def scale(n):
                u = n % 2
                dve.wait_ge(factors, n + 1)
                if n >= 2:
                    dve.wait_ge(g_o_mm, n - 1)
                q, k = tok(gqT, n), tok(gkT, n)

                def scaled_q(dst, src, e):
                    return nc.vector.scalar_tensor_tensor(out=dst, in0=src, scalar=GDK ** -0.5, in1=e,
                                                          op0=ALU.mult, op1=ALU.mult)
                scaled_q(st[:, u, QD], q, ex[:, u, E_MQ])
                nc.vector.tensor_tensor(st[:, u, KD_], k, ex[:, u, E_MK], ALU.mult)
                nc.vector.tensor_tensor(st[:, u, QO, :, 0:64], k[:, :, 0:64], ex[:, u, E_OFF, :, 0:64], ALU.mult)
                scaled_q(st[:, u, QO, :, 64:P], q[:, :, 64:P], ex[:, u, E_OFF, :, 64:P])
                nc.vector.tensor_tensor(st[:, u, KL], k, ex[:, u, E_LAST], ALU.mult)
                scaled_q(st[:, u, QI], q, ex[:, u, E_B]).then_inc(staged, 1)

            def mask(n):
                dve.wait_ge(g_scored, n + 1)
                if n == 0:
                    dve.wait_ge(cleared, 1)
                if n >= 1:
                    dve.wait_ge(g_o_mm, n)
                for odd in range(2):
                    v = (score[0][:, 512:1024], score[1][:, 0:512])[odd].rearrange(
                        "p (i h x) -> p i h x", i=2, h=2)
                    nc.vector.tensor_copy(sc[0:64, odd, :, 64:P], v[0:64, 1, :, 64:P])
                    for g in (0, 64):
                        last = nc.vector.tensor_tensor(sc[g:g + 64, odd, :, g:g + 64],
                                                       v[g:g + 64, 0, :, g:g + 64], causal[g:g + 64, 0:2],
                                                       ALU.mult)
                last.then_inc(masked, 1)

            def carry(n):
                dve.wait_ge(g_o_mm, n + 1)
                for r in (0, 64):
                    for p in range(2):
                        last = nc.vector.scalar_tensor_tensor(
                            out=state[r:r + 64, p, :], in0=state[r:r + 64, p, :],
                            scalar=ex[r:r + 64, n % 2, E_B, p, P - 1:P],
                            in1=score[1][r:r + 64, p * 256 + 2 * r:p * 256 + 2 * r + P],
                            op0=ALU.mult, op1=ALU.add)
                last.then_inc(state_ready, 1)

            def g_sum(n):
                dve.wait_ge(g_squared, n + 1)
                nc.vector.tensor_reduce(g_ss[:], g_sq[:], AX.X, ALU.add).then_inc(g_summed, 1)

            def g_norm(n):
                dve.wait_ge(g_rstd, n + 1)
                nc.vector.tensor_tensor(g_o[:], g_o[:], g_rs[:].unsqueeze(2).to_broadcast([P, HG, GDV]),
                                        ALU.mult).then_inc(gated, 1)
                dve.wait_ge(gated, n + 1)
                dve.wait_ge(rgn_ready, n + 1)
                v = rgn[:, n, :].rearrange("p (h o d) -> p o h d", h=2, o=2)
                nc.vector.tensor_tensor(v, g_o[:].rearrange("p (o h) d -> p o h d", o=2), v,
                                        ALU.mult).then_inc(g_normed, 1)

            for m in range(M + 4):
                if at(m - 1, "attend") is not None:
                    weights(at(m - 1, "attend"))
                if m < M:
                    kind, n = steps[m]
                    {"attend": maxima, "inner": mask, "outer": carry}[kind](n)
                if m == 2:
                    running_sums()
                if at(m - 1, "outer") is not None:
                    g_sum(at(m - 1, "outer"))
                if at(m - 2, "outer") is not None:
                    g_norm(at(m - 2, "outer"))
                if at(m - 4, "attend") is not None:
                    norm(at(m - 4, "attend"))
                if ("factors", m) in when:
                    exponents(when["factors", m])
                if ("scale", m) in when:
                    scale(when["scale", m])


def load_w_out(sp, a, i, dst, done):
    sp.dma_start(dst[:], a["w_out"][0, :, i * CW:(i + 1) * CW].rearrange(
        "(k p) c -> p k c", p=P)).then_inc(done, 16)


def stage_outproj(nc, a, s):
    with ExitStack() as c:
        sb, ps, sem = mem(nc, c, "outproj")
        x = sb("x", [P, 2, D])
        g2 = sb("g2", [P, D])
        xn = sb("xn", [P, 2, D])
        h = sb("h", [P, 2, D], kib=192)
        oh = sb("o_high", [P, 2, KD, P], F32R)
        ol = sb("o_low", [P, 2, KD, P], F32R)
        sq = sb("sq", [P, D])
        raw = s["w_out_raw"] + [sb("w_raw2", [P, KD, CW]), sb("w_raw3", [P, KD, CW], kib=181)]
        xnT = sb("xnT", [P, KD, 512], kib=84)
        wh = sb("w_high", [P, KD, D], F32R, kib=117)
        wl = sb("w_low", [P, KD, D], F32R, kib=149)
        wr = sb("w_router", [P, KD, NG + NE], kib=189)
        br = sb("b_router", [P, NG + NE], kib=190.5)
        ss = sb("ss", [P, T], kib=190.75)
        rs = sb("rs", [P, T], kib=190.8125)
        lT = sb("lT", [NG + NE, 512], kib=100)
        ident = s["ident"]
        pt = [ps(f"pt{i}", [P, 4, P]) for i in range(2)]
        po = [ps(f"po{i}", [P, 512]) for i in range(4)]
        pr = ps("pr", [P, 512])
        pl = ps("pl", [P, T, NG + NE])
        x_in = [sem("x_in0"), sem("x_in1")]
        g2_in = sem("g2_in")
        router_in = [sem(f"router_in{i}") for i in range(4)]
        raw_in = s["w_out_ready"] + [sem("raw_in2"), sem("raw_in3")]
        c.callback(lambda: nc.clear_and_free_semaphores(s["w_out_ready"]))
        w_high, w_low = sem("w_high_ready"), sem("w_low_ready")
        transposed, o_high, o_low = sem("transposed"), sem("o_high_ready"), sem("o_low_ready")
        xn_stored = sem("xn_stored")
        product, added = sem("product"), sem("added")
        squared, shifted, rstd_ready = sem("squared"), sem("shifted"), sem("rstd_ready")
        gain_ready, normed = sem("gain_ready"), sem("normed")
        xn_out = [sem("xn_out0"), sem("xn_out1")]
        logits_mm, lT_ready, logits_t = sem("logits_mm"), sem("lT_ready"), sem("logits_t")
        block = c.enter_context(nc.Block())
        x_rows = a["x"].rearrange("b (t p) d -> (b t) p d", p=P)
        xn_rows = s["xn2_dram"].rearrange("(t p) d -> t p d", p=P)
        h_rows = s["sum_dram"].rearrange("(t p) d -> t p d", p=P)
        h_out = [sem("h_out0"), sem("h_out1")]
        spare_out = sem("spare_out")
        order = [("o", 0)]
        for t in range(T):
            order += ([("o", t + 1)] if t + 1 < T else []) + ([("x", t - 1)] if t >= 1 else [])
        order += [("x", T - 1)]
        place = {what: i for i, what in enumerate(order)}

        @block.sync
        def _(sp):
            for i in (2, 3):
                load_w_out(sp, a, i, raw[i], raw_in[i])
            for t in range(2):
                sp.dma_start(x[:, t, :], x_rows[t]).then_inc(x_in[t], 16)
            sp.dma_start(g2[:], a["norm2_g"].to_broadcast([P, D])).then_inc(g2_in, 16)
            for i, (dst, src) in enumerate((
                    (wr[:, :, 0:NG], a["moe_wg"][0].rearrange("(p k) e -> p k e", p=P)),
                    (wr[:, :, NG:], a["moe_we"][0].rearrange("(p k) e -> p k e", p=P)),
                    (br[:, 0:NG], a["moe_bg"].to_broadcast([P, NG])),
                    (br[:, NG:], a["moe_be"].to_broadcast([P, NE])))):
                sp.dma_start(dst, src).then_inc(router_in[i], 16)
            sp.dma_start(h_rows[T], x_rows[0]).then_inc(spare_out, 16)
            for t in range(T):
                sp.wait_ge(added, 2 * t + 2)
                sp.dma_start(h_rows[t], h[:, t % 2, :]).then_inc(h_out[t % 2], 16)
                sp.wait_ge(normed, t + 1)
                sp.dma_start(xn_rows[t], xn[:, t % 2, :]).then_inc(xn_out[t % 2], 16)
                if t + 2 < T:
                    sp.dma_start(x[:, t % 2, :], x_rows[t + 2]).then_inc(x_in[t % 2], 16)
            for chunk in (4, 5):
                load_chunk(sp, a, s, 1, 1, chunk)
            for i in range(2):
                sp.wait_ge(xn_out[i], 16 * (T // 2))
                sp.wait_ge(h_out[i], 16 * (T // 2))
            sp.wait_ge(spare_out, 16)

        @block.tensor
        def _(pe):
            def transposes(kind, t):
                if (kind, t) not in place:
                    return
                i = place[kind, t]
                pe.wait_ge(normed, t + 1) if kind == "x" else None
                for g in range(2):
                    if i >= 1:
                        before = order[:i]
                        pe.wait_ge(o_low, 2 * sum(k == "o" for k, _ in before) - (1 - g)
                                   ) if before[-1][0] == "o" else pe.wait_ge(
                            xn_stored, 2 * sum(k == "x" for k, _ in before) - (1 - g))
                    for j in range(4):
                        if kind == "o":
                            src = s["rg"][:, t, j * P:(j + 1) * P] if g == 0 else s["dqT"][:, j, t * P:(t + 1) * P]
                        else:
                            src = xn[:, t % 2, :].rearrange("p (c k) -> p k c", k=KD)[:, 4 * g + j, :]
                        last = nc.tensor.transpose(pt[g][:, j, :], src, ident[:])
                    last.then_inc(transposed, 1)

            def products(t):
                for half in range(2):
                    n = 2 * t + half
                    if t == 0:
                        pe.wait_ge(w_low, 2 * half + 2)
                    if n >= 4:
                        pe.wait_ge(added, n - 3)
                    if half == 0:
                        pe.wait_ge(o_low, 2 * t + 2)
                    for k in range(KD):
                        hi, lo = oh[:, t % 2, k, :], ol[:, t % 2, k, :]
                        w_hi, w_lo = wh[:, k, half * 512:half * 512 + 512], wl[:, k, half * 512:half * 512 + 512]
                        nc.tensor.matmul(po[n % 4][:], hi, w_hi, start=(k == 0), stop=False)
                        nc.tensor.matmul(po[n % 4][:], hi, w_lo, start=False, stop=False)
                        last = nc.tensor.matmul(po[n % 4][:], lo, w_hi, start=False, stop=(k == KD - 1))
                    last.then_inc(product, 1)

            def router(half):
                pe.wait_ge(xn_stored, 8 * (half + 1))
                if half == 0:
                    pe.wait_ge(router_in[0], 16)
                    pe.wait_ge(router_in[1], 16)
                else:
                    pe.wait_ge(lT_ready, 1)
                for k in range(KD):
                    last = nc.tensor.matmul(pr[0:NG + NE, :], wr[:, k, :], xnT[:, k, :], start=(k == 0),
                                            stop=(k == KD - 1))
                last.then_inc(logits_mm, 1)
                pe.wait_ge(lT_ready, half + 1)
                for j in range(4):
                    last = nc.tensor.transpose(pl[:, 4 * half + j, :], lT[:, j * P:(j + 1) * P],
                                               ident[0:NG + NE, 0:NG + NE])
                last.then_inc(logits_t, 1)

            transposes("o", 0)
            for t in range(T):
                transposes("o", t + 1)
                products(t)
                transposes("x", t - 1)
                if t == 4:
                    router(0)
            transposes("x", T - 1)
            router(1)

        @block.scalar
        def _(act):
            def w_split(i):
                act.wait_ge(raw_in[i], 16)
                nc.scalar.copy(wh[:, :, i * CW:(i + 1) * CW], raw[i][:]).then_inc(w_high, 1)

            def take(kind, t):
                i = place[kind, t]
                for g in range(2):
                    act.wait_ge(transposed, 2 * i + g + 1)
                    if kind == "o":
                        if t >= 2 and g == 0:
                            act.wait_ge(product, 2 * (t - 1))
                        nc.scalar.copy(oh[:, t % 2, 4 * g:4 * g + 4, :], pt[g][:]).then_inc(o_high, 1)
                    else:
                        if t >= 4 and g == 0:
                            act.wait_ge(logits_mm, 1)
                        nc.scalar.copy(xnT[:, 4 * g:4 * g + 4, (t % 4) * P:(t % 4 + 1) * P],
                                       pt[g][:]).then_inc(xn_stored, 1)

            def square(t):
                act.wait_ge(added, 2 * t + 2)
                if t >= 1:
                    act.wait_ge(squared, t)
                nc.scalar.activation(sq[:], h[:, t % 2, :], ACT.Square,
                                     accum_out=ss[:, t:t + 1]).then_inc(squared, 1)

            take("o", 0)
            for i in range(4):
                w_split(i)
            for t in range(T):
                if t + 1 < T:
                    take("o", t + 1)
                if t >= 1:
                    take("x", t - 1)
                square(t)
            take("x", T - 1)

        @block.gpsimd
        def _(pool):
            for t in range(T):
                pool.wait_ge(squared, t + 1)
                nc.gpsimd.tensor_scalar(rs[:, t:t + 1], ss[:, t:t + 1], EPS * D, None,
                                        ALU.add).then_inc(shifted, 1)
                pool.wait_ge(shifted, t + 1)
                nc.gpsimd.tensor_tensor(rs[:, t:t + 1], rs[:, t:t + 1], s["minus_half"][:, 0:1],
                                        ALU.pow).then_inc(rstd_ready, 1)

        @block.vector
        def _(dve):
            def low(t):
                for g in range(2):
                    dve.wait_ge(o_high, 2 * t + g + 1)
                    nc.vector.tensor_tensor(ol[:, t % 2, 4 * g:4 * g + 4, :], pt[g][:],
                                            oh[:, t % 2, 4 * g:4 * g + 4, :].bitcast(F32),
                                            ALU.subtract).then_inc(o_low, 1)

            def add(t):
                dve.wait_ge(x_in[t % 2], 16 * (t // 2 + 1))
                for half in range(2):
                    n = 2 * t + half
                    dve.wait_ge(product, n + 1)
                    if t >= 2 and half == 0:
                        dve.wait_ge(h_out[t % 2], 16 * (t // 2))
                        dve.wait_ge(normed, t - 1)
                    nc.vector.tensor_tensor(h[:, t % 2, half * 512:half * 512 + 512], po[n % 4][:],
                                            x[:, t % 2, half * 512:half * 512 + 512], ALU.add).then_inc(added, 1)

            def norm(t):
                dve.wait_ge(rstd_ready, t + 1)
                if t >= 2:
                    dve.wait_ge(xn_out[t % 2], 16 * (t // 2))
                    dve.wait_ge(transposed, 2 * place["x", t - 2] + 2)
                nc.vector.scalar_tensor_tensor(out=xn[:, t % 2, :], in0=h[:, t % 2, :], scalar=rs[:, t:t + 1],
                                               in1=g2[:], op0=ALU.mult, op1=ALU.mult).then_inc(normed, 1)

            def logits(half):
                dve.wait_ge(logits_mm, half + 1)
                if half == 1:
                    dve.wait_ge(logits_t, 1)
                nc.vector.tensor_copy(lT[:], pr[0:NG + NE, :]).then_inc(lT_ready, 1)
                dve.wait_ge(logits_t, half + 1)
                nc.vector.tensor_tensor(s["logits"][:, 4 * half:4 * half + 4, :],
                                        pl[:, 4 * half:4 * half + 4, :],
                                        br[:].unsqueeze(1).to_broadcast([P, 4, NG + NE]), ALU.add)

            low(0)
            for i in range(4):
                dve.wait_ge(w_high, i + 1)
                nc.vector.tensor_tensor(wl[:, :, i * CW:(i + 1) * CW], raw[i][:],
                                        wh[:, :, i * CW:(i + 1) * CW].bitcast(F32), ALU.subtract).then_inc(w_low, 1)
            dve.wait_ge(g2_in, 16)
            nc.vector.tensor_scalar(g2[:], g2[:], D ** 0.5, None, ALU.mult).then_inc(gain_ready, 1)
            dve.wait_ge(gain_ready, 1)
            dve.wait_ge(router_in[2], 16)
            dve.wait_ge(router_in[3], 16)
            for t in range(T):
                if t + 1 < T:
                    low(t + 1)
                add(t)
                norm(t)
                if t == 4:
                    logits(0)
            logits(1)


def expert_weights(a, name, e):
    k = KE if name == "moe_w2" else KD
    return a[name][0][bass.ds(e, 1)].rearrange("a (p k) f -> (a p) k f", k=k)


def load_chunk(sp, a, s, e, u, c):
    w = expert_weights(a, ("moe_w1", "moe_w2", "moe_w3")[c // 2], e - 1 if c in (2, 3) else e)
    sp.dma_start(s["w_raw"][:, u, c, :], w.rearrange("p (c k) f -> p c (k f)", c=2)[:, c % 2, :]) \
        .then_inc(s["raw_in"][u][c], 16)


def chunks_of(e):
    return (2, 3) if isinstance(e, int) and e == NE else (0, 1, 4, 5) if isinstance(e, int) and e == 0 \
        else range(CHUNKS_E)


def stage_route(nc, a, s):
    with ExitStack() as c:
        sb, ps, sem = mem(nc, c, "route")
        gmax = sb("gmax", [P, T, 1])
        gexp = sb("gexp", [P, T, NG])
        gw = sb("gw", [P, T, 1])
        first = sb("first", [P, T, NG])
        taken = sb("taken", [P, T, 1])
        le = sb("le", [P, T, NG, EPG])
        top = sb("top", [P, T, 8])
        top_at = sb("top_at", [P, T, 8], U32)
        at = sb("at", [P, T, 2])
        e2 = sb("e2", [P, T, 1])
        w = sb("w", [P, T, 2])
        one = sb("one", [P, 2, T, NE])
        member = sb("member", [P, T, NE], BF16)
        weight = sb("weight", [P, T, NE])
        weight2 = sb("weight2", [P, T, NE])
        part = sb("part", [P, T, NE], BF16)
        iota_e = sb("iota_e", [P, NE])
        iota_t = sb("iota_t", [P, T])
        iota_p = sb("iota_p", [P, 1])
        before = sb("before", [P, P], BF16)
        ones = sb("ones", [P, P], BF16)
        plus1 = sb("plus1", [P, T, NE])
        pp = ps("pp", [P, T, NE])
        pc = ps("pc", [P, NE])
        logits, rows, place, counts = s["logits"], s["slot_rows"], s["place"], s["counts"]
        made, before_ready = sem("made"), sem("before_ready")
        step, gshift, gexp_ready = sem("step"), sem("gshift"), sem("gexp_ready")
        dshift, e2_ready = sem("dshift"), sem("e2_ready")
        member_ready, counted = sem("member_ready"), sem("counted")
        block = c.enter_context(nc.Block())

        @block.sync
        def _(sp):
            for e in range(2):
                for chunk in chunks_of(e) if e == 0 else range(2):
                    load_chunk(sp, a, s, e, e, chunk)

        @block.gpsimd
        def _(pool):
            nc.gpsimd.memset(ones[:], 1.0).then_inc(made, 1)
            nc.gpsimd.memset(before[:], 1.0).then_inc(made, 1)
            pool.wait_ge(made, 2)
            nc.gpsimd.affine_select(out=before[:], in_=before[:], compare_op=ALU.is_gt, fill=0.0, base=0,
                                    pattern=[[1, P]], channel_multiplier=-1).then_inc(before_ready, 1)
            for dst, pattern, base, mult in ((iota_e, [[1, NE]], 0, 0), (iota_t, [[P, T]], -NONE, 0),
                                             (iota_p, [[0, 1]], 0, 1), (s["iota_slot"], [[1, CAP]], 0, 0)):
                nc.gpsimd.iota(dst[:], pattern=pattern, base=base, channel_multiplier=mult,
                               allow_small_or_imprecise_dtypes=True).then_inc(made, 1)

        @block.tensor
        def _(pe):
            pe.wait_ge(before_ready, 1)
            pe.wait_ge(member_ready, 1)
            for t in range(T):
                nc.tensor.matmul(pp[:, t, :], before[:], member[:, t, :], start=True, stop=(t == 0))
                for earlier in range(t):
                    nc.tensor.matmul(pp[:, t, :], ones[:], member[:, earlier, :], start=False,
                                     stop=(earlier == t - 1))
            for t in range(T):
                last = nc.tensor.matmul(pc[:], ones[:], member[:, t, :], start=(t == 0), stop=(t == T - 1))
            last.then_inc(counted, 1)

        @block.scalar
        def _(act):
            act.wait_ge(gshift, 1)
            nc.scalar.activation(gexp[:], gexp[:], ACT.Exp).then_inc(gexp_ready, 1)
            act.wait_ge(dshift, 1)
            nc.scalar.activation(e2[:], e2[:], ACT.Exp).then_inc(e2_ready, 1)

        @block.vector
        def _(dve):
            n = [0]

            def then(ins):
                n[0] += 1
                ins.then_inc(step, 1)
                dve.wait_ge(step, n[0])

            V = nc.vector
            lg = logits[:, :, 0:NG]
            then(V.tensor_reduce(gmax[:], lg, AX.X, ALU.max))
            V.tensor_tensor(gexp[:], lg, gmax[:].to_broadcast([P, T, NG]), ALU.subtract).then_inc(gshift, 1)
            then(V.tensor_tensor(first[:], lg, gmax[:].to_broadcast([P, T, NG]), ALU.is_equal))
            then(V.tensor_copy(taken[:], first[:, :, 0:1]))
            for j in range(1, NG):
                then(V.tensor_tensor(first[:, :, j:j + 1], first[:, :, j:j + 1], taken[:], ALU.is_gt))
                then(V.tensor_tensor(taken[:], taken[:], first[:, :, j:j + 1], ALU.max))
            then(V.tensor_scalar(first[:], first[:], -1.0, -NEG, ALU.add, ALU.mult))
            then(V.tensor_tensor(le[:], logits[:, :, NG:].rearrange("p t (g e) -> p t g e", g=NG),
                                 first[:].unsqueeze(3).to_broadcast([P, T, NG, EPG]), ALU.add))
            for t in range(T):
                last = V.max(top[:, t, :], le[:, t].rearrange("p g e -> p (g e)"))
            then(last)
            for t in range(T):
                last = V.max_index(top_at[:, t, :], top[:, t, :], le[:, t].rearrange("p g e -> p (g e)"))
            V.tensor_tensor(e2[:], top[:, :, 1:2], top[:, :, 0:1], ALU.subtract).then_inc(dshift, 1)
            then(last)
            then(V.tensor_copy(at[:], top_at[:, :, 0:2]))
            dve.wait_ge(made, 6)
            for k in range(2):
                last = V.tensor_tensor(one[:, k], iota_e[:].unsqueeze(1).to_broadcast([P, T, NE]),
                                       at[:, :, k:k + 1].to_broadcast([P, T, NE]), ALU.is_equal)
            then(last)
            V.tensor_tensor(member[:], one[:, 0], one[:, 1], ALU.add).then_inc(member_ready, 1)
            dve.wait_ge(gexp_ready, 1)
            then(V.tensor_reduce(gw[:], gexp[:], AX.X, ALU.add))
            then(V.reciprocal(gw[:], gw[:]))
            dve.wait_ge(e2_ready, 1)
            then(V.tensor_scalar(w[:, :, 1:2], e2[:], 1.0, None, ALU.add))
            then(V.reciprocal(w[:, :, 0:1], w[:, :, 1:2]))
            then(V.tensor_tensor(w[:, :, 0:1], w[:, :, 0:1], gw[:], ALU.mult))
            then(V.tensor_tensor(w[:, :, 1:2], w[:, :, 0:1], e2[:], ALU.mult))
            then(V.tensor_tensor(weight[:], one[:, 0], w[:, :, 0:1].to_broadcast([P, T, NE]), ALU.mult))
            then(V.tensor_tensor(weight2[:], one[:, 1], w[:, :, 1:2].to_broadcast([P, T, NE]), ALU.mult))
            then(V.tensor_tensor(weight[:], weight[:], weight2[:], ALU.add))
            for k in range(3):
                then(V.tensor_copy(part[:], weight[:]))
                then(V.tensor_copy(rows[:, :, :, 3 + k], part[:]))
                if k < 2:
                    then(V.tensor_tensor(weight[:], weight[:], part[:], ALU.subtract))
            V.tensor_copy(rows[:, :, :, 0], iota_t[:].unsqueeze(2).to_broadcast([P, T, NE]))
            V.tensor_copy(rows[:, :, :, 1], iota_p[:].unsqueeze(2).to_broadcast([P, T, NE]))
            V.memset(rows[:, :, :, 2], 1.0)
            dve.wait_ge(counted, 1)
            dve.wait_ge(member_ready, 1)
            then(V.scalar_tensor_tensor(out=plus1[:].rearrange("p t e -> p (t e)"),
                                        in0=pp[:].rearrange("p t e -> p (t e)"), scalar=1.0,
                                        in1=member[:].rearrange("p t e -> p (t e)"), op0=ALU.add, op1=ALU.mult))
            V.tensor_scalar(place[:].rearrange("p e t -> p t e"), plus1[:], -1.0, None, ALU.add)
            V.tensor_copy(counts[:, 0:NE], pc[0:1, :])
            V.tensor_reduce(counts[:, NE:NE + 1], pc[0:1, :], AX.X, ALU.max)


def stage_experts(nc, a, s):
    with ExitStack() as c:
        sb, ps, sem = mem(nc, c, "experts")
        raw, raw_in = s["w_raw"], s["raw_in"]
        c.callback(lambda: nc.clear_and_free_semaphores([done for each in raw_in for done in each]))
        wh = [sb(f"w_high{i}", [P, WC], F32R) for i in range(3)]
        wl = [sb(f"w_low{i}", [P, WC], F32R) for i in range(3)]
        onehot = [sb(f"onehot{u}", [P, T, CAP], BF16) for u in range(2)]
        row = [sb(f"row{u}", [P, NROUTE]) for u in range(4)]
        tmp = [sb(f"tmp{u}", [P, 4]) for u in range(2)]
        token = [sb(f"token{u}", [P, 1], U32) for u in range(2)]
        dest = [sb(f"dest{u}", [P, 1], U32) for u in range(4)]
        wrow = [sb(f"wrow{u}", [P, 1]) for u in range(4)]
        xg = [sb(f"xg{u}", [P, D]) for u in range(2)]
        xTh = [sb(f"xT_high{u}", [P, KD, CAP], F32R) for u in range(2)]
        xTl = [sb(f"xT_low{u}", [P, KD, CAP], F32R) for u in range(2)]
        sl = sb("sl", [P, DE])
        hd = sb("hd", [P, DE])
        hTh = sb("hT_high", [P, KE, CAP], F32R)
        hTl = sb("hT_low", [P, KE, CAP], F32R)
        y = [sb(f"y{u}", [P, D]) for u in range(2)]
        o_xT_all, o_hT_all = sb("o_xT", [P, KD, CAP]), sb("o_hT", [P, KE, CAP])
        shifted_place = sb("shifted_place", [P, T])
        list_start = sb("list_start", [P, SEQ // CAP - 1])
        pid = ps("pid", [P, NROUTE])
        px = [ps(f"px{g}", [P, 4, CAP]) for g in range(2)]
        ph = [ps(f"ph{m}", [P, DE]) for m in range(2)]
        pt = ps("pt", [P, KE, CAP])
        py = [ps(f"py{g}", [P, 512]) for g in range(2)]
        ident, rows, place, counts, iota = s["ident"], s["slot_rows"], s["place"], s["counts"], s["iota_slot"]
        spare_row = sb("spare_row", [P, 1])

        class Sems:
            def __init__(self, k):
                self.onehot = sem(f"onehot_ready{k}")
                self.ids_mm = sem(f"ids_mm{k}")
                self.row_ready = sem(f"row_ready{k}")
                self.target_step = sem(f"target_step{k}")
                self.targets = sem(f"targets{k}")
                self.ids = sem(f"ids_ready{k}")
                self.passed = sem(f"pool_passed{k}")
                self.xg_in = [sem(f"xg_in{k}{u}") for u in range(2)]
                self.x_mm = sem(f"x_transposed{k}")
                self.silu = sem(f"silu_ready{k}")
                self.hd = sem(f"hidden_ready{k}")
                self.h_mm = sem(f"hidden_transposed{k}")
                self.y_ready = sem(f"y_ready{k}")
                self.y_out = [sem(f"y_out{k}{u}") for u in range(2)]

        def pick(q, e, n, u, src=None):
            places = place[:, bass.ds(e, 1), :].rearrange("p a t -> p (a t)") if src is None else src
            nc.vector.tensor_tensor(onehot[u][:], iota[:].unsqueeze(1).to_broadcast([P, T, CAP]),
                                    places.unsqueeze(2).to_broadcast([P, T, CAP]),
                                    ALU.is_equal).then_inc(q.onehot, 1)

        def ids_mm(pe, q, e, n, u):
            pe.wait_ge(q.onehot, n + 1)
            for t in range(T):
                last = nc.tensor.matmul(pid[:], onehot[u][:, t, :],
                                        rows[:, t, bass.ds(e, 1), :].rearrange("p a r -> p (a r)"),
                                        start=(t == 0), stop=(t == T - 1))
            last.then_inc(q.ids_mm, 1)

        def ids(dve, q, n, u, v):
            dve.wait_ge(q.ids_mm, n + 1)
            nc.vector.tensor_copy(row[v][:], pid[:]).then_inc(q.row_ready, 1)
            dve.wait_ge(q.row_ready, n + 1)
            nc.vector.scalar_tensor_tensor(out=token[u][:], in0=row[v][:, 0:1], scalar=float(NONE),
                                           in1=row[v][:, 1:2], op0=ALU.add, op1=ALU.add).then_inc(q.ids, 1)

        def targets(dve, q, n, u, v):
            V = nc.vector
            V.scalar_tensor_tensor(out=tmp[u][:, 0:1], in0=row[v][:, 0:1], scalar=float(NONE),
                                   in1=row[v][:, 1:2], op0=ALU.add, op1=ALU.add).then_inc(q.target_step, 1)
            V.tensor_tensor(tmp[u][:, 1:2], row[v][:, 3:4], row[v][:, 4:5], ALU.add).then_inc(q.target_step, 1)
            V.tensor_scalar(tmp[u][:, 2:3], row[v][:, 2:3], -1.0, 1.0, ALU.mult,
                            ALU.add).then_inc(q.target_step, 1)
            dve.wait_ge(q.target_step, 3 * n + 3)
            V.tensor_tensor(wrow[v][:], tmp[u][:, 1:2], row[v][:, 5:6], ALU.add).then_inc(q.targets, 1)
            V.scalar_tensor_tensor(out=dest[v][:], in0=tmp[u][:, 2:3], scalar=spare_row[:], in1=tmp[u][:, 0:1],
                                   op0=ALU.mult, op1=ALU.add).then_inc(q.targets, 1)

        bound = {}

        def set_bounds(pool):
            bound["x"] = pool.to_reg(SEQ - 1)
            bound["y"] = pool.to_reg(SEQ + CAP - 1)

        def gather(pool, q, ids_ready, n, u):
            pool.wait_ge(ids_ready, n + 1)
            pool.sem_inc(q.passed, 1)
            nc.gpsimd.indirect_dma_start(xg[u][:], None, s["xn2_dram"],
                                         bass.IndirectOffsetOnAxis(token[u][:, 0:1], 0),
                                         bounds_check=bound["x"], oob_is_err=False).then_inc(q.xg_in[u], 16)

        def x_transposes(pe, q, n, u, arrived):
            pe.wait_ge(q.xg_in[u], arrived)
            for g in range(2):
                for j in range(4):
                    last = nc.tensor.transpose(px[g][:, j, :], xg[u][:].rearrange(
                        "p (c k) -> p k c", k=KD)[:, 4 * g + j, :], ident[:])
                last.then_inc(q.x_mm, 1)

        def h_transposes(pe, q, n):
            pe.wait_ge(q.hd, n + 1)
            for j in range(KE):
                last = nc.tensor.transpose(pt[:, j, :], hd[:].rearrange("p (c k) -> p k c", k=KE)[:, j, :],
                                           ident[:])
            last.then_inc(q.h_mm, 1)

        def scatter(pool, q, done, n, u, v):
            pool.wait_ge(done.targets, 2 * n + 2)
            pool.wait_ge(done.y_ready, 2 * n + 2)
            pool.sem_inc(q.passed, 1)
            nc.gpsimd.indirect_dma_start(s["sum_dram"], bass.IndirectOffsetOnAxis(dest[v][:, 0:1], 0), y[u][:],
                                         None, bounds_check=bound["y"], oob_is_err=True,
                                         compute_op=ALU.add).then_inc(q.y_out[u], 16)

        def silu(act, q):
            nc.scalar.activation(sl[:], ph[0][:], ACT.Silu).then_inc(q.silu, 1)

        def hidden(dve, q, n):
            dve.wait_ge(q.silu, n + 1)
            nc.vector.tensor_tensor(hd[:], ph[1][:], sl[:], ALU.mult).then_inc(q.hd, 1)

        def weighted(act, q, g, u, v):
            nc.scalar.activation(y[u][:, g * 512:g * 512 + 512], py[g][:], ACT.Copy,
                                 scale=wrow[v][:, 0:1]).then_inc(q.y_ready, 1)

        def some(n, k):
            return n >= k if isinstance(n, int) else True

        q = Sems("")
        spare_made, xg_cleared = sem("spare_made"), sem("xg_cleared")
        w_high, w_low = sem("w_high_ready"), sem("w_low_ready")
        chunk_used = sem("chunk_used")
        xT_high, xT_low = sem("xT_high_ready"), sem("xT_low_ready")
        hT_high, hT_low = sem("hT_high_ready"), sem("hT_low_ready")

        def number(e, c):
            if isinstance(e, int) and e in (0, NE):
                return {0: 0, 1: 1, 4: 2, 5: 3}[c] if e == 0 else CHUNKS_E * NE + c - 4
            return CHUNKS_E * e + c - 2

        def slot(c):
            return (c + 1) % 3

        def high(act, e, r, u, c):
            act.wait_ge(raw_in[u][c], 16 * (r + u) if c in (2, 3) else 16 * (r + 1))
            n = number(e, c)
            if isinstance(e, int) and e == 0:
                if c == 4:
                    act.wait_ge(chunk_used, 2)
            elif isinstance(e, int) and e == NE and c == 2:
                act.wait_ge(chunk_used, n)
            else:
                act.wait_ge(chunk_used, n - 2)
            nc.scalar.copy(wh[slot(c)][:], raw[:, u, c, :]).then_inc(w_high, 1)

        def low(dve, e, u, c):
            dve.wait_ge(w_high, number(e, c) + 1)
            nc.vector.tensor_tensor(wl[slot(c)][:], raw[:, u, c, :], wh[slot(c)][:].bitcast(F32),
                                    ALU.subtract).then_inc(w_low, 1)

        def sp_expert(sp, e, r, j, last, tail=False):
            if not some(e, 2):
                return
            for c in chunks_of(e):
                if not (isinstance(e, int) and e == 2 and c in (2, 3)):
                    sp.wait_ge(w_low, number(e - 2, c) + 1)
                load_chunk(sp, a, s, e, j % 2, c)

        def product(out, x_hi, x_lo, w_hi, w_lo, start, stop):
            nc.tensor.matmul(out, x_hi, w_hi, start=start, stop=False)
            nc.tensor.matmul(out, x_hi, w_lo, start=False, stop=False)
            return nc.tensor.matmul(out, x_lo, w_hi, start=False, stop=stop)

        def gate(pe, e, c, u):
            pe.wait_ge(w_low, number(e, c) + 1)
            for k in range(KD // 2):
                w = slice(k * DE, (k + 1) * DE)
                kx = KD // 2 * (c % 2) + k
                last = product(ph[c // 4][:], xTh[u][:, kx, :], xTl[u][:, kx, :], wh[slot(c)][:, w],
                               wl[slot(c)][:, w], kx == 0, kx == KD - 1)
            last.then_inc(chunk_used, 1)

        def down(pe, e, c):
            pe.wait_ge(w_low, number(e, c) + 1)
            for k in range(KE // 2):
                kx = KE // 2 * (c % 2) + k
                for g in range(2):
                    w = slice(k * D + g * 512, k * D + g * 512 + 512)
                    last = product(py[g][:], hTh[:, kx, :], hTl[:, kx, :], wh[slot(c)][:, w], wl[slot(c)][:, w],
                                   kx == 0, kx == KE - 1)
            last.then_inc(chunk_used, 1)

        def pe_ids(pe, e, u):
            if some(e, 1):
                pe.wait_ge(q.row_ready, e)
            ids_mm(pe, q, e, e, u)

        def pe_x(pe, e, r, u):
            if some(e, 1):
                pe.wait_ge(xT_low, 2 * e)
            x_transposes(pe, q, e, u, 16 * (r + 1))

        def pe_expert(pe, e, r, j, last, tail=False):
            u = j % 2
            if not tail:
                pe.wait_ge(xT_low, 2 * e + 2)
                if some(e, 1):
                    pe.wait_ge(q.silu, e)
                gate(pe, e, 0, u)
            if some(e, 1):
                h_transposes(pe, q, e - 1)
            if not tail:
                gate(pe, e, 1, u)
                if not (last and j == 3):
                    pe_x(pe, e + 1, pair(r, j, 1), 1 - u)
                if not (last and j >= 1):
                    pe_ids(pe, e + 3, 1 - u)
            if some(e, 1):
                pe.wait_ge(hT_low, e)
                if some(e, 2):
                    pe.wait_ge(q.y_ready, 2 * e - 2)
                down(pe, e, 2)
                down(pe, e, 3)
            if not tail:
                if some(e, 1):
                    pe.wait_ge(q.hd, e)
                gate(pe, e, 4, u)
                gate(pe, e, 5, u)

        def act_expert(act, e, r, j, last, tail=False):
            u = j % 2
            if some(e, 1):
                if not (tail or (isinstance(e, int) and e == 0)):
                    high(act, e, r, u, 2)
                act.wait_ge(q.h_mm, e)
                nc.scalar.copy(hTh[:], pt[:]).then_inc(hT_high, 1)
                if not tail:
                    high(act, e, r, u, 3)
            if not tail:
                act.wait_ge(chunk_used, number(e, 1) + 1)
                if some(e, 1):
                    act.wait_ge(q.hd, e)
                silu(act, q)
                high(act, e, r, u, 4)
                if not (last and j == 3):
                    act_x(act, e + 1, 1 - u)
                high(act, e, r, u, 5)
                more = (0, 1) if not (last and j == 3) else ()
            else:
                more = ()
            if more:
                high(act, e + 1, pair(r, j, 1), 1 - u, 0)
            if some(e, 1):
                act.wait_ge(chunk_used, number(e, 3) + 1)
                act.wait_ge(q.targets, 2 * e)
                if some(e, 3):
                    act.wait_ge(q.y_out[1 - u], 16 * pair(r, j, -1))
                for g in range(2):
                    weighted(act, q, g, 1 - u, (j - 1) % 4)
            if more:
                high(act, e + 1, pair(r, j, 1), 1 - u, 1)
            if last and j == 3 and not tail:
                high(act, e + 1, pair(r, j, 1), 1 - u, 2)
                high(act, e + 1, pair(r, j, 1), 1 - u, 3)

        def act_x(act, e, u):
            for g in range(2):
                act.wait_ge(q.x_mm, 2 * e + g + 1)
                nc.scalar.copy(xTh[u][:, 4 * g:4 * g + 4, :], px[g][:]).then_inc(xT_high, 1)

        def dve_x(dve, e, u):
            for g in range(2):
                dve.wait_ge(xT_high, 2 * e + g + 1)
                nc.vector.tensor_tensor(xTl[u][:, 4 * g:4 * g + 4, :], px[g][:],
                                        xTh[u][:, 4 * g:4 * g + 4, :].bitcast(F32),
                                        ALU.subtract).then_inc(xT_low, 1)

        def dve_expert(dve, e, r, j, last, tail=False):
            u = j % 2
            if some(e, 1):
                dve.wait_ge(chunk_used, number(e - 1, 5) + 1)
                hidden(dve, q, e - 1)
                if not tail:
                    low(dve, e, u, 2)
                dve.wait_ge(hT_high, e)
                nc.vector.tensor_tensor(hTl[:], pt[:], hTh[:].bitcast(F32), ALU.subtract).then_inc(hT_low, 1)
                if not tail:
                    low(dve, e, u, 3)
            if tail:
                return
            low(dve, e, u, 4)
            if not (last and j >= 2):
                dve_targets(dve, e + 2, r + 1, (j + 2) % 4)
            if not (last and j == 3):
                dve_x(dve, e + 1, 1 - u)
            if not (last and j >= 1):
                dve_ids(dve, e + 3, pair(r, j, 3), (j + 3) % 4)
            low(dve, e, u, 5)
            if not (last and j == 3):
                low(dve, e + 1, 1 - u, 0)
            if not last:
                pick(q, e + 4, e + 4, u)
            if not (last and j == 3):
                low(dve, e + 1, 1 - u, 1)
            else:
                low(dve, e + 1, 1 - u, 2)
                low(dve, e + 1, 1 - u, 3)

        def dve_ids(dve, e, r, j):
            if some(e, 2):
                dve.wait_ge(q.xg_in[j % 2], 16 * r)
            ids(dve, q, e, j % 2, j)

        def dve_targets(dve, e, r, j):
            if some(e, 4):
                dve.wait_ge(q.y_out[j % 2], 16 * (r - 1))
            targets(dve, q, e, j % 2, j)

        def pool_gather(pool, e, u):
            if some(e, 2):
                pool.wait_ge(q.x_mm, 2 * (e - 1))
            gather(pool, q, q.ids, e, u)

        def pool_expert(pool, e, r, j, last, tail=False):
            u = j % 2
            if not (tail or (last and j >= 1)):
                pool_gather(pool, e + 3, 1 - u)
            if some(e, 1):
                if some(e, 2):
                    pool.wait_ge(q.y_out[u], 16 * r)
                scatter(pool, q, q, e - 1, 1 - u, (j - 1) % 4)

        def pair(r, j, d):
            return r + (j + d) // 2 - j // 2

        def over_experts(eng, expert):
            for j in range(4):
                expert(eng, j, j // 2, j, False)
            with eng.Fori(1, NE // 4 - 1) as i:
                for j in range(4):
                    expert(eng, 4 * i + j, 2 * i + j // 2, j, False)
            for j in range(4):
                e = NE - 4 + j
                expert(eng, e, e // 2, j, True)
            expert(eng, NE, NE // 2, 0, True, tail=True)

        with ExitStack() as b:
            block = b.enter_context(nc.Block())

            @block.sync
            def _(sp):
                sp.wait_ge(q.passed, 2)
                for chunk in (2, 3):
                    load_chunk(sp, a, s, 1, 1, chunk)
                over_experts(sp, sp_expert)

            @block.tensor
            def _(pe):
                for e in range(3):
                    pe_ids(pe, e, e % 2)
                pe_x(pe, 0, 0, 0)
                over_experts(pe, pe_expert)

            @block.scalar
            def _(act):
                for c in range(2):
                    high(act, 0, 0, 0, c)
                act_x(act, 0, 0)
                over_experts(act, act_expert)

            @block.gpsimd
            def _(pool):
                set_bounds(pool)
                nc.gpsimd.iota(spare_row[:], pattern=[[0, 1]], base=SEQ - NONE, channel_multiplier=1,
                               allow_small_or_imprecise_dtypes=True).then_inc(spare_made, 1)
                for u in range(2):
                    nc.gpsimd.memset(xg[u][:], 0.0).then_inc(xg_cleared, 1)
                pool.wait_ge(xg_cleared, 2)
                for e in range(3):
                    pool_gather(pool, e, e % 2)
                over_experts(pool, pool_expert)
                for u in range(2):
                    pool.wait_ge(q.y_out[u], 16 * (NE // 2))

            @block.vector
            def _(dve):
                dve.wait_ge(spare_made, 1)
                for e in range(2):
                    pick(q, e, e, e)
                for e in range(2):
                    dve_ids(dve, e, 0, e)
                    pick(q, e + 2, e + 2, e)
                for c in range(2):
                    low(dve, 0, 0, c)
                dve_x(dve, 0, 0)
                for e in range(2):
                    dve_targets(dve, e, 0, e)
                dve_ids(dve, 2, 1, 2)
                over_experts(dve, dve_expert)

        MORE = SEQ // CAP - 1
        o = Sems("o")
        turn, starts, shift = sem("turn"), sem("starts"), sem("shifted")
        o_w_in = [sem(f"ow_in{c}") for c in range(3)]
        o_xT, o_gated, o_hT, o_down = sem("oxT_ready"), sem("ogated"), sem("ohT_ready"), sem("oy_product")

        class moved:
            passed, xg_in, y_out = o.passed, [sem("oxg_moved")], [sem("oy_moved")]

        def items(eng, item, skip):
            most = eng.value_load(counts[0:1, NE:NE + 1], min_val=0, max_val=SEQ)
            with eng.If(most > CAP):
                with eng.Fori(0, NE) as e:
                    count = eng.value_load(counts[0:1, bass.ds(e, 1)], min_val=0, max_val=SEQ)
                    with eng.Fori(0, MORE) as k:
                        n = MORE * e + k
                        with eng.If(count > CAP * (k + 1)):
                            item(eng, e, k, n)
                        with eng.Else():
                            skip(eng, n)
                        eng.nop()
                    eng.nop()
                eng.nop()
            eng.nop()

        def back_to_zero(pool, which):
            pool.dma_reset(range(which.num, which.num + 1))
            pool.sem_clear(which)

        def own(eng, n, *counted):
            if n is not None:
                eng.wait_ge(turn, n + 1)
            for which, amount in counted:
                eng.sem_inc(which, amount)

        with ExitStack() as b:
            block = b.enter_context(nc.Block())

            @block.sync
            def _(sp):
                def item(sp, e, k, n):
                    sp.wait_ge(turn, n + 1)
                    for c, name in enumerate(("moe_w1", "moe_w2", "moe_w3")):
                        sp.dma_start(raw[:, 0, 2 * c:2 * c + 2, :], expert_weights(a, name, e).rearrange(
                            "p (c k) f -> p c (k f)", c=2)).then_inc(o_w_in[c], 16)
                items(sp, item, lambda eng, n: own(eng, n, *((w_in, 16) for w_in in o_w_in)))

            @block.tensor
            def _(pe):
                def item(pe, e, k, n):
                    ids_mm(pe, o, e, n, 0)
                    x_transposes(pe, o, n, 0, n + 1)
                    pe.wait_ge(o_xT, 2 * n + 2)
                    for m in range(2):
                        pe.wait_ge(o_w_in[2 * m], 16 * (n + 1))
                        for kx in range(KD):
                            last = nc.tensor.matmul(ph[m][:], o_xT_all[:, kx, :], raw[:, 0, 4 * m + kx // 4, :]
                                                    .rearrange("p (k f) -> p k f", f=DE)[:, kx % 4, :],
                                                    start=(kx == 0), stop=(kx == KD - 1))
                        last.then_inc(o_gated, 1)
                    h_transposes(pe, o, n)
                    pe.wait_ge(o_w_in[1], 16 * (n + 1))
                    pe.wait_ge(o_hT, n + 1)
                    for g in range(2):
                        for kx in range(KE):
                            last = nc.tensor.matmul(py[g][:], o_hT_all[:, kx, :], raw[:, 0, 2 + kx // 2, :].rearrange(
                                "p (k f) -> p k f", f=D)[:, kx % 2, g * 512:g * 512 + 512],
                                start=(kx == 0), stop=(kx == KE - 1))
                    last.then_inc(o_down, 1)
                items(pe, item, lambda eng, n: own(eng, n, (o.ids_mm, 1), (o.x_mm, 2), (o_gated, 2), (o.h_mm, 1),
                                                   (o_down, 1)))

            @block.scalar
            def _(act):
                def item(act, e, k, n):
                    for g in range(2):
                        act.wait_ge(o.x_mm, 2 * n + g + 1)
                        nc.scalar.copy(o_xT_all[:, 4 * g:4 * g + 4, :], px[g][:]).then_inc(o_xT, 1)
                    act.wait_ge(o_gated, 2 * n + 1)
                    silu(act, o)
                    act.wait_ge(o_down, n + 1)
                    for g in range(2):
                        weighted(act, o, g, 0, 0)
                items(act, item, lambda eng, n: own(eng, n, (o_xT, 2), (o.silu, 1), (o.y_ready, 2)))

            @block.gpsimd
            def _(pool):
                def item(pool, e, k, n):
                    gather(pool, moved, o.ids, n, 0)
                    pool.wait_ge(moved.xg_in[0], 16)
                    back_to_zero(pool, moved.xg_in[0])
                    pool.sem_inc(o.xg_in[0], 1)
                    scatter(pool, moved, o, n, 0, 0)
                    pool.wait_ge(moved.y_out[0], 16)
                    back_to_zero(pool, moved.y_out[0])
                    pool.sem_inc(turn, 1)
                set_bounds(pool)
                pool.sem_inc(turn, 1)
                items(pool, item, lambda eng, n: own(eng, None, (o.xg_in[0], 1), (turn, 1)))

            @block.vector
            def _(dve):
                for k in range(MORE):
                    last = nc.vector.memset(list_start[:, k:k + 1], float(CAP * (k + 1)))
                last.then_inc(starts, 1)
                dve.wait_ge(starts, 1)

                def item(dve, e, k, n):
                    dve.wait_ge(turn, n + 1)
                    nc.vector.tensor_tensor(shifted_place[:], place[:, bass.ds(e, 1), :].rearrange(
                        "p a t -> p (a t)"), list_start[:, bass.ds(k, 1)].to_broadcast([P, T]),
                        ALU.subtract).then_inc(shift, 1)
                    dve.wait_ge(shift, n + 1)
                    pick(o, e, n, 0, shifted_place[:])
                    ids(dve, o, n, 0, 0)
                    targets(dve, o, n, 0, 0)
                    dve.wait_ge(o_gated, 2 * n + 2)
                    hidden(dve, o, n)
                    dve.wait_ge(o.h_mm, n + 1)
                    nc.vector.tensor_copy(o_hT_all[:], pt[:]).then_inc(o_hT, 1)
                items(dve, item, lambda eng, n: own(eng, n, (shift, 1), (o.onehot, 1), (o.row_ready, 1), (o.ids, 1), (o.target_step, 3), (o.targets, 2),
                                                    (o.hd, 1), (o_hT, 1)))


def stage_store(nc, a, s):
    with ExitStack() as c:
        sb, ps, sem = mem(nc, c, "store")
        stored = [sem(f"stored{i}") for i in range(2)]
        block = c.enter_context(nc.Block())
        rows = s["sum_dram"].rearrange("(t p) d -> t p d", p=P)
        out_rows = a["out"].rearrange("b (t p) d -> (b t) p d", p=P)

        def store(eng, i):
            for t in range(i, T, 2):
                eng.dma_start(out_rows[t], rows[t]).then_inc(stored[i], 16)
            eng.wait_ge(stored[i], 16 * (T // 2))

        @block.sync
        def _(sp):
            store(sp, 0)

        @block.scalar
        def _(act):
            store(act, 1)


INPUTS = ["x", "rel_bias", "norm1_g", "w_in", "gla_wa2", "gla_ba", "gla_onorm_g", "diff_qnorm_g",
          "diff_knorm_g", "diff_lq1", "diff_lk1", "diff_lq2", "diff_lk2", "diff_subln_g", "w_out", "norm2_g",
          "moe_wg", "moe_bg", "moe_we", "moe_be", "moe_w1", "moe_w3", "moe_w2"]


def kernel(**inputs):
    import concourse.bacc as bacc
    from concourse.bass_utils import run_bass_kernel_spmd

    nc = bacc.Bacc("TRN2", target_bir_lowering=False, num_devices=1)
    arrays = {f"in_{n}": np.ascontiguousarray(inputs[n]) for n in INPUTS}
    arrays["in_bucket_onehot"] = buckets()
    a = {n[3:]: nc.dram_tensor(n, v.shape, mybir.dt.from_np(v.dtype), kind="ExternalInput").ap()
         for n, v in arrays.items()}
    a["out"] = nc.dram_tensor("out", (1, SEQ, D), F32, kind="ExternalOutput").ap()
    build(nc, a)
    r = run_bass_kernel_spmd(nc, [arrays], core_ids=[0])
    return r.results[0]["out"]
```
